# Optimizing a Trainium2 kernel written in Bass

```python
import math
import jax, jax.numpy as jnp
from jax import lax
import numpy as np

D_MODEL = 1024
BATCH = 1
SEQ = 256
DEPTH = 2
DEC_BATCH = 8
DEC_SEQ = 4
PAST_LEN = 2048
PAGE_SIZE = 128

MLA_HEADS = 8
Q_LORA = 384
KV_LORA = 256
NOPE_DIM = 64
ROPE_DIM = 32
V_DIM = 64
ROPE_BASE = 10000.0
Q_BLOCK = 128
SSM_HEADS = 8
SSM_HEAD_DIM = 64
SSM_INNER = SSM_HEADS * SSM_HEAD_DIM
SSM_GROUPS = 2
SSM_STATE = 128
SSM_CONV = 4
SSM_CONV_DIM = SSM_INNER + 2 * SSM_GROUPS * SSM_STATE
SSD_CHUNK = 128
MIX_AB_IN = Q_LORA + KV_LORA + ROPE_DIM + SSM_INNER + SSM_CONV_DIM + SSM_HEADS
MIX_AB_OUT = MLA_HEADS * V_DIM + SSM_INNER
CONF_CH = D_MODEL
CONF_K = 31
N_EXPERTS = 16
N_GROUPS = 4
TOP_K = 2
D_EXPERT = 256
DN_ALPHA = (2 * DEPTH) ** 0.25
DN_BETA = (8 * DEPTH) ** -0.25
EPS = 1e-6

kernel_name = 'hybrid_mla_ssd_conformer_moe_step'

def layer_norm(x, g, b):
    xf = x.astype(jnp.float32)
    mu = jnp.mean(xf, -1, keepdims=True)
    var = jnp.mean(jnp.square(xf - mu), -1, keepdims=True)
    return ((xf - mu) * lax.rsqrt(var + EPS)).astype(x.dtype) * g + b

def rms_norm(x, g):
    xf = x.astype(jnp.float32)
    return (xf * lax.rsqrt(jnp.mean(xf * xf, -1, keepdims=True) + EPS)).astype(x.dtype) * g

def rope(x, pos):
    half = x.shape[-1] // 2
    inv = ROPE_BASE ** (-jnp.arange(half, dtype=jnp.float32) / half)
    ang = pos.astype(jnp.float32)[:, None] * inv[None, :]
    cos = jnp.cos(ang)[None, :, None, :].astype(x.dtype)
    sin = jnp.sin(ang)[None, :, None, :].astype(x.dtype)
    x1, x2 = x[..., :half], x[..., half:]
    return jnp.concatenate([x1 * cos - x2 * sin, x2 * cos + x1 * sin], axis=-1)

def causal_dwconv(xp, w):
    return lax.conv_general_dilated(xp, w[:, None, :].astype(xp.dtype), (1,), 'VALID',
                                    dimension_numbers=('NWC', 'WIO', 'NWC'),
                                    feature_group_count=xp.shape[-1])

def ssd(x, dt, a, bm, cm, h0):
    b, L, H, P = x.shape
    N = bm.shape[-1]
    l = min(SSD_CHUNK, L)
    nc = L // l
    xc = x.reshape(b, nc, l, H, P)
    bc = bm.reshape(b, nc, l, H, N)
    cc = cm.reshape(b, nc, l, H, N)
    dtc = dt.reshape(b, nc, l, H)
    acs = jnp.cumsum(dtc * a, axis=2)
    seg = acs[:, :, :, None, :] - acs[:, :, None, :, :]
    causal = jnp.tril(jnp.ones((l, l), bool))[None, None, :, :, None]
    decay = jnp.exp(jnp.where(causal, seg, -jnp.inf)).astype(x.dtype)
    dtx = dtc.astype(x.dtype)[..., None] * xc
    cb = jnp.einsum('bcihn,bcjhn->bcijh', cc, bc)
    y_diag = jnp.einsum('bcijh,bcjhp->bcihp', cb * decay, dtx)
    to_end = jnp.exp(acs[:, :, -1:, :] - acs).astype(x.dtype)
    states = jnp.einsum('bclh,bclhn,bclhp->bchpn', to_end, bc, dtx).astype(h0.dtype)
    chunk_decay = jnp.exp(acs[:, :, -1, :]).astype(h0.dtype)

    def step(h, inp):
        dec, st = inp
        return dec[:, :, None, None] * h + st, h

    h_last, h_prev = lax.scan(step, h0, (jnp.swapaxes(chunk_decay, 0, 1), jnp.swapaxes(states, 0, 1)))
    h_prev = jnp.swapaxes(h_prev, 0, 1)
    y_off = jnp.einsum('bclhn,bchpn->bclhp', cc * jnp.exp(acs).astype(x.dtype)[..., None], h_prev.astype(x.dtype))
    return (y_diag + y_off).reshape(b, L, H, P), h_last

def mla_attend_prompt(q_abs, q_pe, c_kv, k_pe):
    b, S, H, R = q_abs.shape
    nb = S // Q_BLOCK
    scale = (NOPE_DIM + ROPE_DIM) ** -0.5
    qa = jnp.swapaxes(q_abs.reshape(b, nb, Q_BLOCK, H, R), 0, 1)
    qp = jnp.swapaxes(q_pe.reshape(b, nb, Q_BLOCK, H, ROPE_DIM), 0, 1)
    kpos = jnp.arange(S)

    def block(args):
        qa_i, qp_i, i = args
        sc = (jnp.einsum('bqhr,btr->bhqt', qa_i, c_kv)
              + jnp.einsum('bqhe,bte->bhqt', qp_i, k_pe)).astype(jnp.float32) * scale
        qpos = i * Q_BLOCK + jnp.arange(Q_BLOCK)
        sc = jnp.where(kpos[None, :] <= qpos[:, None], sc, -jnp.inf)
        p = jax.nn.softmax(sc, axis=-1).astype(c_kv.dtype)
        return jnp.einsum('bhqt,btr->bqhr', p, c_kv)

    o = lax.map(block, (qa, qp, jnp.arange(nb)))
    return jnp.swapaxes(o, 0, 1).reshape(b, S, H, R)

def mla_attend_sample(q_abs, q_pe, c_new, kpe_new, c_past, kpe_past):
    s = q_abs.shape[1]
    T = c_past.shape[1]
    scale = (NOPE_DIM + ROPE_DIM) ** -0.5
    sp = (jnp.einsum('bqhr,btr->bhqt', q_abs, c_past)
          + jnp.einsum('bqhe,bte->bhqt', q_pe, kpe_past)).astype(jnp.float32)
    sn = (jnp.einsum('bqhr,btr->bhqt', q_abs, c_new)
          + jnp.einsum('bqhe,bte->bhqt', q_pe, kpe_new)).astype(jnp.float32)
    sn = jnp.where(jnp.tril(jnp.ones((s, s), bool)), sn, -jnp.inf)
    p = jax.nn.softmax(jnp.concatenate([sp, sn], axis=-1) * scale, axis=-1).astype(c_new.dtype)
    return (jnp.einsum('bhqt,btr->bqhr', p[..., :T], c_past)
            + jnp.einsum('bhqt,btr->bqhr', p[..., T:], c_new))

def mixer_ab(x, pos, conv_hist, h0, past_ckv, past_kpe, w_in, g_q, g_kv, w_uq, w_uk, w_uv,
             conv_w, conv_b, dt_bias, a_log, d_skip, g_y, w_out):
    b, s, _ = x.shape
    proj = jnp.einsum('bsd,de->bse', x, w_in)
    o1 = Q_LORA
    o2 = o1 + KV_LORA
    o3 = o2 + ROPE_DIM
    o4 = o3 + SSM_INNER
    o5 = o4 + SSM_CONV_DIM
    h_q, h_kv, kpe_raw, z, xbc, dt_raw = jnp.split(proj, [o1, o2, o3, o4, o5], axis=-1)
    q = jnp.einsum('bsq,qhe->bshe', rms_norm(h_q, g_q), w_uq)
    q_pe = rope(q[..., NOPE_DIM:], pos)
    q_abs = jnp.einsum('bshn,rhn->bshr', q[..., :NOPE_DIM], w_uk)
    c_kv = rms_norm(h_kv, g_kv)
    k_pe = rope(kpe_raw[:, :, None, :], pos)[:, :, 0, :]
    if past_ckv is None:
        o_lat = mla_attend_prompt(q_abs, q_pe, c_kv, k_pe)
    else:
        o_lat = mla_attend_sample(q_abs, q_pe, c_kv, k_pe, past_ckv, past_kpe)
    o_mla = jnp.einsum('bshr,rhv->bshv', o_lat, w_uv).reshape(b, s, MLA_HEADS * V_DIM)
    xp = jnp.concatenate([conv_hist.astype(xbc.dtype), xbc], axis=1)
    new_conv = xp[:, xp.shape[1] - (SSM_CONV - 1):]
    xbc = jax.nn.silu(causal_dwconv(xp, conv_w) + conv_b)
    xs, bm, cm = jnp.split(xbc, [SSM_INNER, SSM_INNER + SSM_GROUPS * SSM_STATE], axis=-1)
    xs = xs.reshape(b, s, SSM_HEADS, SSM_HEAD_DIM)
    rep = SSM_HEADS // SSM_GROUPS
    bm = jnp.repeat(bm.reshape(b, s, SSM_GROUPS, SSM_STATE), rep, axis=2)
    cm = jnp.repeat(cm.reshape(b, s, SSM_GROUPS, SSM_STATE), rep, axis=2)
    dt = jax.nn.softplus(dt_raw.astype(jnp.float32) + dt_bias.astype(jnp.float32))
    a = -jnp.exp(a_log.astype(jnp.float32))
    y, h_last = ssd(xs, dt, a, bm, cm, h0)
    y = (y + d_skip[:, None] * xs).reshape(b, s, SSM_INNER) * jax.nn.silu(z)
    y = rms_norm(y.reshape(b, s, SSM_GROUPS, -1), g_y.reshape(SSM_GROUPS, -1)).reshape(b, s, SSM_INNER)
    out = jnp.einsum('bse,ed->bsd', jnp.concatenate([o_mla, y], axis=-1), w_out)
    return out, c_kv, k_pe, h_last, new_conv

def mixer_c(x, hist, w_in, b_in, dw_w, dw_b, g_n, b_n, w_out, b_out):
    u = jnp.einsum('bsd,de->bse', x, w_in) + b_in
    v = u[..., :CONF_CH] * jax.nn.sigmoid(u[..., CONF_CH:])
    vp = jnp.concatenate([hist.astype(v.dtype), v], axis=1)
    new_hist = vp[:, vp.shape[1] - (CONF_K - 1):]
    c = causal_dwconv(vp, dw_w) + dw_b
    c = jax.nn.silu(layer_norm(c, g_n, b_n))
    return jnp.einsum('bsc,cd->bsd', c, w_out) + b_out, new_hist

def moe(x, w_router, router_bias, w_gate, w_up, w_down):
    probs = jax.nn.sigmoid(jnp.einsum('bsd,de->bse', x, w_router).astype(jnp.float32))
    sel = probs + router_bias.astype(jnp.float32)
    b, s, E = sel.shape
    per = E // N_GROUPS
    grp = lax.top_k(sel.reshape(b, s, N_GROUPS, per), TOP_K)[0].sum(-1)
    g_idx = jnp.argmax(grp, axis=-1)
    in_grp = (jnp.arange(E) // per)[None, None, :] == g_idx[..., None]
    _, e_idx = lax.top_k(jnp.where(in_grp, sel, -jnp.inf), TOP_K)
    w = jnp.take_along_axis(probs, e_idx, axis=-1)
    w = w / jnp.sum(w, -1, keepdims=True)
    gates = jnp.sum(jax.nn.one_hot(e_idx, E, dtype=jnp.float32) * w[..., None], axis=-2).astype(x.dtype)
    h = jax.nn.silu(jnp.einsum('bsd,edf->bsef', x, w_gate)) * jnp.einsum('bsd,edf->bsef', x, w_up)
    return jnp.einsum('bsef,efd->bsd', h * gates[..., None], w_down)

def setup_inputs(seed: int = 0) -> dict:
    key = jax.random.key(seed)
    ks = list(jax.random.split(key, 48))
    f32 = jnp.float32
    n_a = (DEPTH + 1) // 2
    n_c = DEPTH // 2
    n_pages = PAST_LEN // PAGE_SIZE
    n_used = DEC_BATCH * n_pages
    n_pool = n_used + n_used // 4

    def nrm(shape, scale):
        return jax.random.normal(ks.pop(), shape, f32) * scale

    def gain(shape):
        return 1.0 + nrm(shape, 0.02)

    x_prompt = nrm((BATCH, SEQ, D_MODEL), 1.0)
    x_sample = nrm((DEC_BATCH, DEC_SEQ, D_MODEL), 1.0)
    cache_ckv = nrm((n_a, n_pool, PAGE_SIZE, KV_LORA), 1.0)
    cache_kpe = nrm((n_a, n_pool, PAGE_SIZE, ROPE_DIM), 1.0)
    state_ssm = nrm((n_a, DEC_BATCH, SSM_HEADS, SSM_HEAD_DIM, SSM_STATE), 0.5)
    state_ssm_conv = nrm((n_a, DEC_BATCH, SSM_CONV - 1, SSM_CONV_DIM), 1.0)
    state_conf_conv = nrm((n_c, DEC_BATCH, CONF_K - 1, CONF_CH), 0.5)
    page_table = jax.random.permutation(ks.pop(), n_pool)[:n_used].reshape(DEC_BATCH, n_pages).astype(jnp.int32)
    dt0 = jnp.exp(jax.random.uniform(ks.pop(), (n_a, SSM_HEADS), f32, math.log(1e-3), math.log(1e-1)))
    ssm_dt_bias = dt0 + jnp.log(-jnp.expm1(-dt0))
    ssm_a_log = jnp.log(jax.random.uniform(ks.pop(), (n_a, SSM_HEADS), f32, 1.0, 16.0))
    return {
        'x_prompt': x_prompt,
        'x_sample': x_sample,
        'cache_ckv': cache_ckv,
        'cache_kpe': cache_kpe,
        'state_ssm': state_ssm,
        'state_ssm_conv': state_ssm_conv,
        'state_conf_conv': state_conf_conv,
        'page_table': page_table,
        'w_in_ab': nrm((n_a, D_MODEL, MIX_AB_IN), D_MODEL ** -0.5),
        'g_q_norm': gain((n_a, Q_LORA)),
        'g_kv_norm': gain((n_a, KV_LORA)),
        'w_uq': nrm((n_a, Q_LORA, MLA_HEADS, NOPE_DIM + ROPE_DIM), Q_LORA ** -0.5),
        'w_uk': nrm((n_a, KV_LORA, MLA_HEADS, NOPE_DIM), KV_LORA ** -0.5),
        'w_uv': nrm((n_a, KV_LORA, MLA_HEADS, V_DIM), KV_LORA ** -0.5),
        'ssm_conv_w': nrm((n_a, SSM_CONV, SSM_CONV_DIM), SSM_CONV ** -0.5),
        'ssm_conv_b': nrm((n_a, SSM_CONV_DIM), 0.02),
        'ssm_dt_bias': ssm_dt_bias,
        'ssm_a_log': ssm_a_log,
        'ssm_d': 1.0 + nrm((n_a, SSM_HEADS), 0.1),
        'ssm_norm_g': gain((n_a, SSM_INNER)),
        'w_out_ab': nrm((n_a, MIX_AB_OUT, D_MODEL), MIX_AB_OUT ** -0.5 * DN_BETA),
        'conf_w_in': nrm((n_c, D_MODEL, 2 * CONF_CH), D_MODEL ** -0.5),
        'conf_b_in': nrm((n_c, 2 * CONF_CH), 0.02),
        'conf_dw_w': nrm((n_c, CONF_K, CONF_CH), CONF_K ** -0.5),
        'conf_dw_b': nrm((n_c, CONF_CH), 0.02),
        'conf_norm_g': gain((n_c, CONF_CH)),
        'conf_norm_b': nrm((n_c, CONF_CH), 0.02),
        'conf_w_out': nrm((n_c, CONF_CH, D_MODEL), CONF_CH ** -0.5 * DN_BETA),
        'conf_b_out': nrm((n_c, D_MODEL), 0.02),
        'ln_mix_g': gain((DEPTH, D_MODEL)),
        'ln_mix_b': nrm((DEPTH, D_MODEL), 0.02),
        'ln_ffn_g': gain((DEPTH, D_MODEL)),
        'ln_ffn_b': nrm((DEPTH, D_MODEL), 0.02),
        'w_router': nrm((D_MODEL, N_EXPERTS), D_MODEL ** -0.5),
        'router_bias': nrm((N_EXPERTS,), 0.01),
        'moe_w_gate': nrm((DEPTH, N_EXPERTS, D_MODEL, D_EXPERT), D_MODEL ** -0.5),
        'moe_w_up': nrm((DEPTH, N_EXPERTS, D_MODEL, D_EXPERT), D_MODEL ** -0.5),
        'moe_w_down': nrm((DEPTH, N_EXPERTS, D_EXPERT, D_MODEL), D_EXPERT ** -0.5 * DN_BETA),
    }

def reference(x_prompt, x_sample, cache_ckv, cache_kpe, state_ssm, state_ssm_conv, state_conf_conv,
              page_table, w_in_ab, g_q_norm, g_kv_norm, w_uq, w_uk, w_uv, ssm_conv_w, ssm_conv_b,
              ssm_dt_bias, ssm_a_log, ssm_d, ssm_norm_g, w_out_ab, conf_w_in, conf_b_in, conf_dw_w,
              conf_dw_b, conf_norm_g, conf_norm_b, conf_w_out, conf_b_out, ln_mix_g, ln_mix_b,
              ln_ffn_g, ln_ffn_b, w_router, router_bias, moe_w_gate, moe_w_up, moe_w_down):
    bp, S, _ = x_prompt.shape
    bd, t_new, _ = x_sample.shape
    past_len = page_table.shape[1] * PAGE_SIZE
    pos_p = jnp.arange(S, dtype=jnp.int32)
    pos_s = past_len + jnp.arange(t_new, dtype=jnp.int32)
    hp, hs = x_prompt, x_sample
    ckv_p, kpe_p, ssm_p, sconv_p, cconv_p = [], [], [], [], []
    ckv_s, kpe_s, ssm_s, sconv_s, cconv_s = [], [], [], [], []
    for l in range(DEPTH):
        i = l // 2
        if l % 2 == 0:
            wts = (w_in_ab[i], g_q_norm[i], g_kv_norm[i], w_uq[i], w_uk[i], w_uv[i],
                   ssm_conv_w[i], ssm_conv_b[i], ssm_dt_bias[i], ssm_a_log[i], ssm_d[i],
                   ssm_norm_g[i], w_out_ab[i])
            zc = jnp.zeros((bp, SSM_CONV - 1, SSM_CONV_DIM), hp.dtype)
            zh = jnp.zeros((bp, SSM_HEADS, SSM_HEAD_DIM, SSM_STATE), hp.dtype)
            mp, c1, k1, h1, v1 = mixer_ab(hp, pos_p, zc, zh, None, None, *wts)
            c_past = cache_ckv[i, page_table].reshape(bd, past_len, KV_LORA)
            k_past = cache_kpe[i, page_table].reshape(bd, past_len, ROPE_DIM)
            ms, c2, k2, h2, v2 = mixer_ab(hs, pos_s, state_ssm_conv[i], state_ssm[i], c_past, k_past, *wts)
            ckv_p.append(c1); kpe_p.append(k1); ssm_p.append(h1); sconv_p.append(v1)
            ckv_s.append(c2); kpe_s.append(k2); ssm_s.append(h2); sconv_s.append(v2)
        else:
            wts = (conf_w_in[i], conf_b_in[i], conf_dw_w[i], conf_dw_b[i], conf_norm_g[i],
                   conf_norm_b[i], conf_w_out[i], conf_b_out[i])
            mp, u1 = mixer_c(hp, jnp.zeros((bp, CONF_K - 1, CONF_CH), hp.dtype), *wts)
            ms, u2 = mixer_c(hs, state_conf_conv[i], *wts)
            cconv_p.append(u1); cconv_s.append(u2)
        hp = layer_norm(DN_ALPHA * hp + mp, ln_mix_g[l], ln_mix_b[l])
        hs = layer_norm(DN_ALPHA * hs + ms, ln_mix_g[l], ln_mix_b[l])
        ffn = (w_router, router_bias, moe_w_gate[l], moe_w_up[l], moe_w_down[l])
        hp = layer_norm(DN_ALPHA * hp + moe(hp, *ffn), ln_ffn_g[l], ln_ffn_b[l])
        hs = layer_norm(DN_ALPHA * hs + moe(hs, *ffn), ln_ffn_g[l], ln_ffn_b[l])
    return (hp, hs,
            jnp.stack(ckv_p), jnp.stack(kpe_p), jnp.stack(ssm_p), jnp.stack(sconv_p), jnp.stack(cconv_p),
            jnp.stack(ckv_s), jnp.stack(kpe_s), jnp.stack(ssm_s), jnp.stack(sconv_s), jnp.stack(cconv_s))


_drawn_inputs = setup_inputs


def setup_inputs(seed=0):
    import zlib

    import numpy as np

    out = dict(_drawn_inputs(seed))
    spreads = {}
    factors = {'cache_ckv': 6.151,
     'cache_kpe': 8.0,
     'g_q_norm': 8.0,
     'g_kv_norm': 2.89,
     'conf_norm_g': 4.464,
     'conf_norm_b': 3.059}
    for name, (base, spread) in spreads.items():
        noise = np.random.default_rng([zlib.crc32(name.encode()), seed]).standard_normal(out[name].shape)
        drawn = base * np.exp(spread * noise) if base else spread * noise
        out[name] = __import__('jax').numpy.asarray(drawn.astype(out[name].dtype))
    for name, factor in factors.items():
        out[name] = (out[name] * factor).astype(out[name].dtype)
    return out
```

```python
from contextlib import ExitStack

import numpy as np

import concourse.bass as bass
from concourse import mybir

F32 = mybir.dt.float32
I32 = mybir.dt.int32
ALU = mybir.AluOpType
ACT = mybir.ActivationFunctionType
AX = mybir.AxisListType.X

P = 128
D = 1024
KC = D // P
SEQ = 256
NB, NS = 8, 4
T = SEQ + NB * NS
TILES = ((0, 128), (128, 128), (256, 32))
H = 8
QL, R, E_PE, VD = 384, 256, 32, 64
NSTATE = 128
NP = 16
NEG = -1.0e30
EPS = 1e-6
ALPHA = 4.0 ** 0.25
SCALE = 96.0 ** -0.5
NE = 16
CAP = 64
MAX_EXTRA = 8
SLOT_ROWS = (NE + MAX_EXTRA) * CAP
NOBODY = 1 << 20
KW = 31
HIST = KW - 1


def const_layout():
    widths = [("ident", P), ("ones", P), ("tri", P), ("tri_strict", P), ("mask_ssd", P), ("mask_q", P),
              ("tri_s", 32), ("blk_s", 32), ("mask_ssd_s", 32), ("bmask", NB), ("mask_new", 64),
              ("cos", 48), ("sin", 48), ("row_of", NE), ("prio16", NE), ("prio4", 4), ("valid", 3),
              ("eps", 1), ("item_thr", 64), ("item_k", MAX_EXTRA)]
    at, cols = 0, {}
    for name, w in widths:
        cols[name] = (at, at + w)
        at += w
    return cols, at


CONST, NCONST = const_layout()


def constants():
    c = np.zeros((P, NCONST), np.float32)
    i = np.arange(P)

    def put(name, value):
        a, b = CONST[name]
        value = np.asarray(value, np.float32)
        c[:value.shape[0], a:b] = value.reshape(value.shape[0], b - a)

    put("ident", np.eye(P))
    put("ones", np.ones((P, P)))
    put("tri", i[:, None] <= i[None, :])
    put("tri_strict", i[:, None] < i[None, :])
    put("mask_ssd", np.where(i[:, None] <= i[None, :], 0.0, NEG))
    put("mask_q", np.where(i[None, :] <= i[:, None], 0.0, NEG))
    k = np.arange(32)
    same = (k[:, None] // NS) == (k[None, :] // NS)
    put("tri_s", same & (k[:, None] <= k[None, :]))
    put("blk_s", same)
    put("mask_ssd_s", np.where(same & (k[:, None] <= k[None, :]), 0.0, NEG))
    put("bmask", (k[:, None] // NS) == np.arange(NB)[None, :])
    row_b, row_s = i // 32, i % NS
    new = np.zeros((P, 2, 32), np.float32)
    for g in range(2):
        ok = ((k[None, :] // NS) == (4 * g + row_b[:, None])) & ((k[None, :] % NS) <= row_s[:, None])
        new[:, g] = np.where(ok, 0.0, NEG)
    put("mask_new", new)
    pos = np.zeros((P, 3))
    pos[:, 0], pos[:, 1] = i, i + P
    pos[:32, 2] = NP * P + k % NS
    inv = np.float32(10000.0) ** (-np.arange(16, dtype=np.float32) / np.float32(16))
    ang = pos.astype(np.float32)[:, :, None] * inv[None, None, :]
    put("cos", np.cos(ang))
    put("sin", np.sin(ang))
    put("row_of", np.broadcast_to(np.arange(NE) * CAP, (P, NE)))
    put("prio16", np.broadcast_to(NE - np.arange(NE), (P, NE)))
    put("prio4", np.broadcast_to(4 - np.arange(4), (P, 4)))
    valid = np.ones((P, 3))
    valid[32:, 2] = 0
    put("valid", valid)
    put("eps", np.full((P, 1), EPS))
    put("item_thr", np.broadcast_to(np.tile(np.arange(1, 5) * CAP, NE), (P, 64)))
    put("item_k", np.broadcast_to(np.arange(MAX_EXTRA), (P, MAX_EXTRA)))
    return c


def param_layout():
    widths = [("g_q", 3), ("conv_w", 32), ("conv_b", 8), ("g_y", 4), ("d_skip", 4), ("dt_bias", 8),
              ("a_log", 8), ("b_in", 16), ("dw_w", 8 * KW), ("dw_b", 8), ("gn", 8), ("bn", 8),
              ("r_bias", NE), ("w_router", KC * NE), ("g_kv", R)]
    at, cols = 0, {}
    for name, w in widths:
        cols[name] = (at, at + w)
        at += w
    return cols, at


PARAM, NPARAM = param_layout()


class Chain:

    def __init__(self, engine, sem):
        self.engine, self.sem, self.count = engine, sem, 0

    def step(self, instruction):
        self.count += 1
        instruction.then_inc(self.sem, 1)
        self.engine.wait_ge(self.sem, self.count)


def hybrid_trunk(nc, a, o):
    ctx = ExitStack()
    with ctx:
        def sb(name, cols, dt=F32):
            return ctx.enter_context(nc.sbuf_tensor(name, [P, cols], dt))

        def sem(name):
            return ctx.enter_context(nc.semaphore(name))

        ps = [ctx.enter_context(nc.psum_tensor(f"bank{i}", [P, 512], F32)) for i in range(8)]
        X = sb("x_tok", 3 * D)[:].rearrange("p (t d) -> p t d", t=3)
        xT_t = sb("x_ch", KC * T)
        XT = xT_t[:].rearrange("p (c t) -> p c t", c=KC)
        ROWS = sb("rows", 2 * D)[:].rearrange("p (r d) -> p r d", r=2)
        C = sb("consts", NCONST)
        PM = sb("params", NPARAM)
        slot_t = sb("slots", 3 * 6144)
        M = sb("mixer", 24472)
        small = sb("small", 640)
        ints = sb("ints", 64, I32)

        def cst(name, rows=P):
            lo, hi = CONST[name]
            return C[0:rows, lo:hi]

        def prm(name):
            lo, hi = PARAM[name]
            return PM[:, lo:hi]

        def at(t, off, *dims):
            n = int(np.prod(dims))
            v = t[:, off:off + n]
            if len(dims) == 1:
                return v
            names = "abcd"[:len(dims)]
            return v.rearrange(f"p ({' '.join(names)}) -> p {' '.join(names)}", **dict(zip(names[1:], dims[1:])))

        ident, ones = cst("ident"), cst("ones")

        WUQN = at(slot_t, 0, 3, 4, P)
        WUQP = at(slot_t, 1536, 3, 256)
        WUK = at(slot_t, 2304, 4, R)
        WUV = at(slot_t, 3328, 2, H * VD)
        CK = at(slot_t, 4352, 3, R)
        CKT = at(slot_t, 5120, 2, T)
        KPT = at(slot_t, 5696, T)
        S1 = 6144
        DX = at(slot_t, S1, 3, 512)
        DXE = at(slot_t, S1 + 1536, 3, 512)
        BTOK = at(slot_t, S1 + 3072, 3, 256)
        BM = at(slot_t, S1 + 3840, NB, 256)
        L = at(slot_t, S1 + 5888, H, T)
        E = at(slot_t, S1 + 8192, 4, T)
        H1 = at(slot_t, S1 + 9344, 512)
        H2 = at(slot_t, S1 + 9856, 512)
        Y = at(slot_t, S1 + 10368, 4, T)
        RG = at(slot_t, S1 + 11520, 2, T)
        WIN = at(M, 0, 4, KC, P)
        WTOK = at(M, 4096, KC, 296)
        H0 = at(M, 0, NB, 512)
        T1 = at(M, 4096, 4, T)
        SQ = at(M, 5248, 4, T)
        TK = at(M, 6464, 3, 296)
        HQ = at(M, 7352, 3, T)
        CAT = at(M, 8216, KC, T)
        QN = at(M, 10520, 4, T)
        QA = at(M, 11672, 2, H, T)
        XP = at(M, 16280, KC, 3 + SEQ)
        XS = at(M, 18352, KC, NB, 7)
        XB = at(M, 18800, KC, T)
        ZT = at(M, 21104, 4, T)
        CS = at(M, 22256, KC, NB * NS)
        QPT = at(M, 22512, 3, 256)
        TMP = at(M, 23280, 4, 128)
        WOUT = at(M, 16280, KC, D)
        QP = at(xT_t, 0, H, T)
        S = at(M, 0, 2080)
        PT = at(M, 2080, NP, P)
        PNT = at(M, 4128, P)
        OS = at(M, 4256, R)
        PP = at(M, 4512, 2, 384)
        PPT = at(M, 5280, 2, 384)

        SS, RK, TDT = small[:, 0:3], small[:, 3:6], at(small, 8, 3, 8)
        DT, DTA, T3 = at(small, 32, 3, 8), at(small, 56, 3, 8), at(small, 80, 3, 8)
        NA = small[:, 104:112]
        ACS, TOE, DEC = small[:, 112:224], small[:, 224:248], small[:, 248:328]
        DTAM = at(small, 328, NB, 8)
        KPE = at(small, 392, 3, 32)
        KT = at(small, 488, 3, 32)
        BST, MV, RST = at(small, 584, 2, 6), small[:, 596:598], small[:, 598:600]
        MXP, RSP = at(small, 600, 2, 4), at(small, 608, 2, 4)
        MXS, RSS = small[:, 616:620], small[:, 620:624]

        ld_const, ld_x, ld_xT, ld_wtok, ld_wq, ld_hist = map(sem, (
            "ld_const", "ld_x", "ld_xT", "ld_wtok", "ld_wq", "ld_hist"))
        ld_h0, ld_wout, ld_rows, ld_bout = map(sem, ("ld_h0", "ld_wout", "ld_rows", "ld_bout"))
        ld_win = [sem(f"ld_win{i}") for i in range(4)]
        zeroed, tok_mm, tok_kept, piece_mm, hq_kept, ch_kept = map(sem, (
            "zeroed", "tok_mm", "tok_kept", "piece_mm", "hq_kept", "ch_kept"))
        sq_ready, sum_mm, std_ready, hq_ready, kv_ready, kvT_mm, kvT_kept = map(sem, (
            "sq_ready", "sum_mm", "std_ready", "hq_ready", "kv_ready", "kvT_mm", "kvT_kept"))
        conv_ready, xb_ready, dt_z, dt_ln, dtA_ready = map(sem, (
            "conv_ready", "xb_ready", "dt_z", "dt_ln", "dtA_ready"))
        acs_mm, acs_kept, dec_ready, row_mm, seg_ready, decay_ready, e_ready = map(sem, (
            "acs_mm", "acs_kept", "dec_ready", "row_mm", "seg_ready", "decay_ready", "e_ready"))
        xs_mm, dx_ready, bt_mm, bt_kept, bm_ready, cb_mm, m_ready = map(sem, (
            "xs_mm", "dx_ready", "bt_mm", "bt_kept", "bm_ready", "cb_mm", "m_ready"))
        ydiag_mm, state_mm, h1_ready, yoff_mm, h2_ready, sstate_mm, sstate_kept = map(sem, (
            "ydiag_mm", "state_mm", "h1_ready", "yoff_mm", "h2_ready", "sstate_mm", "sstate_kept"))
        y_gated, y_ready = map(sem, ("y_gated", "y_ready"))
        stored = sem("stored")
        dve_step, act_step, pool_step = map(sem, ("dve_step", "act_step", "pool_step"))
        n_stored = [0]

        eps = cst("eps")

        qn_mm, q_kept, qp_mm, qa_mm, qa_act, qa_dve, qpT_mm, qpT_kept = map(sem, (
            "qn_mm", "q_kept", "qp_mm", "qa_mm", "qa_act", "qa_dve", "qpT_mm", "qpT_kept"))
        pscore_mm, pscore_read, pmax_ready, pexp_ready, prob_ready, probT_mm, probT_kept, po_mm, po_kept = map(sem, (
            "pscore_mm", "pscore_read", "pmax_ready", "pexp_ready", "prob_ready", "probT_mm", "probT_kept", "po_mm",
            "po_kept"))
        s_mm, s_kept, s_new, s_max, s_exp, sT_mm, sT_kept, so_mm, so_kept, soT_mm, soT_kept = map(sem, (
            "s_mm", "s_kept", "s_new", "s_max", "s_exp", "sT_mm", "sT_kept", "so_mm", "so_kept", "soT_mm", "soT_kept"))
        kv_ld = [sem("kv_ld0"), sem("kv_ld1")]
        kpe_ld = [sem("kpe_ld0"), sem("kpe_ld1")]
        v_used, omla_mm, cat_kept, h2_stored, h0_stored, ckv_stored, conv_stored, ld_pages = map(sem, (
            "v_used", "omla_mm", "cat_kept", "h2_stored", "h0_stored", "ckv_stored", "conv_stored", "ld_pages"))
        KCH = [(g, kind, c) for g in range(2) for kind in "kv" for c in range(4)]
        QAS = at(M, 6464, 2, NB, 32)
        QPS = at(M, 6976, NB, 32)
        pages = sb("pages", NB * NP, I32)

        def k_slot(i):
            return at(slot_t, 6144 * (1 + i % 2), 4, 2, 512), at(slot_t, 6144 * (1 + i % 2) + 4096, 4, 512)

        def v_slot(i):
            return at(slot_t, 6144 * (1 + i % 2), 4, 4, R)

        def kv_loaded(i):
            return 256 * (i // 2 + 1)

        def kpe_loaded(i):
            return 256 * sum(KCH[j][1] == "k" for j in range(i % 2, i + 1, 2))

        def load_pages(eng, engine_type, i, part):
            g, kind, c = KCH[i]
            if i >= 2:
                pg, pkind, pc = KCH[i - 2]
                if pkind == "k":
                    eng.wait_ge(s_mm, 5 * pg + pc + 1)
                else:
                    eng.wait_ge(v_used, 4 * pg + pc + 1)
            with eng.Fori(0, 4) as j:
                _, page = nc.values_load_multi_w_load_instructions(
                    pages[0:1, bass.ds(j * NP + (g * 64 + c * 4), 4)], engines=[engine_type], min_val=0, max_val=159)
                for n in range(4):
                    if part == "kpe":
                        dst = k_slot(i)[1][0:32, bass.ds(j, 1), n * P:(n + 1) * P].rearrange("p j t -> p (j t)")
                        src = a["kpeT"][bass.ds(page[n], 1)].rearrange("a p t -> (a p) t")
                    elif kind == "k":
                        dst = k_slot(i)[0][:, bass.ds(j, 1), :, n * P:(n + 1) * P].rearrange("p j r t -> p (j r) t")
                        src = a["cacheT"][bass.ds(page[n], 1)].rearrange("a p r t -> (a p) r t")
                    else:
                        dst = v_slot(i)[:, bass.ds(j, 1), n, :].rearrange("p j r -> p (j r)")
                        src = a["cache"][bass.ds(page[n], 1)].rearrange("a p r -> (a p) r")
                    eng.dma_start(dst, src).then_inc((kpe_ld if part == "kpe" else kv_ld)[i % 2], 16)

        def loads_attention(sp):
            sp.wait_ge(ld_pages, 16)
            sp.wait_ge(y_ready, 1)
            sp.wait_ge(sstate_kept, NB)
            sp.wait_ge(h2_stored, 16)
            for i in range(16):
                load_pages(sp, mybir.EngineType.SP, i, "main")
                if i == 1:
                    sp.wait_ge(conv_stored, 32)
                    sp.wait_ge(qpT_mm, 5)
                    sp.dma_start(WOUT, a["w_out"]).then_inc(ld_wout, 16)
                    sp.dma_start(ROWS[:, 0, :], a["rows"][0]).then_inc(ld_rows, 16)
                    sp.dma_start(ROWS[:, 1, :], a["rows_b"][0]).then_inc(ld_rows, 16)

        def products_attention(pe):
            pe.wait_ge(hq_ready, 1)
            pe.wait_ge(ld_wq, 16)
            pe.wait_ge(std_ready, 3)
            pe.wait_ge(sstate_kept, NB)
            for n in range(4):
                for k in range(3):
                    mm = nc.tensor.matmul(ps[n][:, 0:T], WUQN[:, k, n, :], HQ[:, k, :], start=(k == 0), stop=(k == 2))
                mm.then_inc(qn_mm, 1)
            for t, (t0, nt) in enumerate(TILES):
                for k in range(3):
                    mm = nc.tensor.matmul(ps[4 + t][0:nt, 0:256], HQ[:, k, t0:t0 + nt], WUQP[:, k, :],
                                          start=(k == 0), stop=(k == 2))
                mm.then_inc(qp_mm, 1)
            for h in range(H):
                lo = 64 * (h % 2)
                for r in range(2):
                    n = 2 * h + r
                    if n < 4:
                        pe.wait_ge(q_kept, 4)
                    elif n < 7:
                        pe.wait_ge(q_kept, n + 1)
                    elif n >= 8:
                        pe.wait_ge(qa_dve if r else qa_act, h - 3)
                    nc.tensor.matmul(ps[n % 8][:, 0:T], WUK[lo:lo + 64, h // 2, r * P:(r + 1) * P],
                                     QN[lo:lo + 64, h // 2, :], start=True, stop=True).then_inc(qa_mm, 1)
            pe.wait_ge(qa_act, 8)
            pe.wait_ge(qa_dve, 8)
            for n, (t, h0, nh) in enumerate(((0, 0, 4), (0, 4, 4), (1, 0, 4), (1, 4, 4), (2, 0, 8))):
                t0, nt = TILES[t]
                for h in range(nh):
                    mm = nc.tensor.transpose(ps[n][0:32, h * nt:(h + 1) * nt],
                                             QPT[0:nt, t, (h0 + h) * 32:(h0 + h + 1) * 32], ident[0:nt, 0:nt])
                mm.then_inc(qpT_mm, 1)
            pe.wait_ge(qpT_kept, 5)

            def prompt_scores(h):
                b = ps[h % 2]
                if h >= 2:
                    pe.wait_ge(pscore_read, h - 1)
                for lo, q0, n in ((0, 0, P), (P, P, SEQ)):
                    for r in range(2):
                        nc.tensor.matmul(b[:, lo:lo + n], QA[:, r, h, q0:q0 + P], CKT[:, r, 0:n],
                                         start=(r == 0), stop=False)
                    mm = nc.tensor.matmul(b[:, lo:lo + n], QP[0:32, h, q0:q0 + P], KPT[0:32, 0:n],
                                          start=False, stop=True)
                mm.then_inc(pscore_mm, 1)

            def prompt_values(h):
                i = h % 2
                pe.wait_ge(prob_ready, h + 1)
                if h >= 2:
                    pe.wait_ge(probT_kept, h - 1)
                for n in range(3):
                    mm = nc.tensor.transpose(ps[2 + i][:, n * P:(n + 1) * P], PP[:, i, n * P:(n + 1) * P], ident)
                mm.then_inc(probT_mm, 1)
                pe.wait_ge(probT_kept, h + 1)
                if h >= 2:
                    pe.wait_ge(po_kept, h - 1)
                for r in range(2):
                    cr = slice(r * P, (r + 1) * P)
                    nc.tensor.matmul(ps[4 + i][:, r * SEQ:(r + 1) * SEQ], CK[:, 0, cr], PPT[:, i, 0:SEQ],
                                     start=True, stop=False, skip_group_check=True)
                    mm = nc.tensor.matmul(ps[4 + i][:, r * SEQ + P:(r + 1) * SEQ], CK[:, 1, cr], PPT[:, i, SEQ:384],
                                          start=False, stop=True, skip_group_check=True)
                mm.then_inc(po_mm, 1)

            prompt_scores(0)
            prompt_scores(1)
            for h in range(H):
                prompt_values(h)
                if h + 2 < H:
                    prompt_scores(h + 2)

            pe.wait_ge(po_kept, H)
            pe.wait_ge(probT_kept, H)
            for g in range(2):
                for c in range(4):
                    i = 8 * g + c
                    kt, kp = k_slot(i)
                    b = ps[6 + c % 2]
                    pe.wait_ge(kv_ld[i % 2], kv_loaded(i))
                    pe.wait_ge(kpe_ld[i % 2], kpe_loaded(i))
                    if 4 * g + c >= 2:
                        pe.wait_ge(s_kept, 4 * g + c - 1)
                    if c == 0 and g == 1:
                        pe.wait_ge(s_new, 1)
                    for r in range(2):
                        for j in range(4):
                            nc.tensor.matmul(b[32 * j:32 * j + 32, :], QAS[:, r, 4 * g + j, :], kt[:, j, r, :],
                                             start=(r == 0), stop=False, skip_group_check=True)
                    for j in range(4):
                        mm = nc.tensor.matmul(b[32 * j:32 * j + 32, :], QPS[0:32, 4 * g + j, :], kp[0:32, j, :],
                                              start=False, stop=True, skip_group_check=True)
                    mm.then_inc(s_mm, 1)
                pe.wait_ge(s_kept, 4 * g + 3)
                b = ps[6]
                for j in range(4):
                    for r in range(2):
                        nc.tensor.matmul(b[32 * j:32 * j + 32, 0:32], QAS[:, r, 4 * g + j, :], CKT[:, r, SEQ:T],
                                         start=(r == 0), stop=False, skip_group_check=True)
                    mm = nc.tensor.matmul(b[32 * j:32 * j + 32, 0:32], QPS[0:32, 4 * g + j, :],
                                          KPT[0:32, SEQ:T], start=False, stop=True, skip_group_check=True)
                mm.then_inc(s_mm, 1)
                pe.wait_ge(s_exp, g + 1)
                for n in range(4):
                    if n >= 2 or g:
                        pe.wait_ge(sT_kept, 5 * g + n - 1)
                    for m in range(4):
                        mm = nc.tensor.transpose(ps[2 + n % 2][:, m * P:(m + 1) * P],
                                                 S[:, (4 * n + m) * P:(4 * n + m + 1) * P], ident)
                    mm.then_inc(sT_mm, 1)
                if g:
                    pe.wait_ge(soT_kept, 1)
                nc.tensor.transpose(ps[5][0:32, 0:P], S[:, 2048:2080], ident).then_inc(sT_mm, 1)
                pe.wait_ge(sT_kept, 5 * g + 5)
                if g:
                    pe.wait_ge(so_kept, 1)
                for c in range(4):
                    i = 8 * g + 4 + c
                    vt = v_slot(i)
                    pe.wait_ge(kv_ld[i % 2], kv_loaded(i))
                    for n in range(4):
                        for j in range(4):
                            mm = nc.tensor.matmul(ps[4][32 * j:32 * j + 32, 0:R], PT[:, 4 * c + n, 32 * j:32 * j + 32],
                                                  vt[:, j, n, :], start=(c == 0 and n == 0), stop=False,
                                                  skip_group_check=True)
                    mm.then_inc(v_used, 1)
                for j in range(4):
                    mm = nc.tensor.matmul(ps[4][32 * j:32 * j + 32, 0:R], PNT[0:32, 32 * j:32 * j + 32], CK[0:32, 2, :],
                                          start=False, stop=True, skip_group_check=True)
                mm.then_inc(so_mm, 1)
                pe.wait_ge(so_kept, g + 1)
                for r in range(2):
                    mm = nc.tensor.transpose(ps[5][:, r * P:(r + 1) * P], OS[:, r * P:(r + 1) * P], ident)
                mm.then_inc(soT_mm, 1)
            pe.wait_ge(soT_kept, 2)
            for n in range(4):
                if n >= 2:
                    pe.wait_ge(cat_kept, n - 1)
                for hh in range(2):
                    h = 2 * n + hh
                    for r in range(2):
                        mm = nc.tensor.matmul(ps[n % 2][64 * hh:64 * hh + 64, 0:T], WUV[:, r, h * VD:(h + 1) * VD],
                                              QA[:, r, h, :], start=(r == 0), stop=(r == 1))
                mm.then_inc(omla_mm, 1)

        def act_attention(act, steps):
            for n in range(8):
                act.wait_ge(qa_mm, 2 * n + 1)
                nc.scalar.copy(QA[:, 0, n, 0:SEQ], ps[(2 * n) % 8][:, 0:SEQ])
                nc.scalar.copy(QAS[:, 0, :, NS * n:NS * n + NS],
                               ps[(2 * n) % 8][:, SEQ:T].rearrange("p (b s) -> p b s", s=NS)).then_inc(qa_act, 1)
            for n, (t, h0, nh) in enumerate(((0, 0, 4), (0, 4, 4), (1, 0, 4), (1, 4, 4), (2, 0, 8))):
                t0, nt = TILES[t]
                act.wait_ge(qpT_mm, n + 1)
                src = ps[n][0:32, 0:nh * nt]
                if t < 2:
                    op = nc.scalar.copy(QP[0:32, h0:h0 + nh, t0:t0 + nt], src.rearrange("p (h t) -> p h t", h=nh))
                else:
                    op = nc.scalar.copy(QPS[0:32].rearrange("p b (h s) -> p b h s", s=NS),
                                        src.rearrange("p (h b s) -> p b h s", h=nh, s=NS))
                op.then_inc(qpT_kept, 1)

            def exp_head(h):
                i = h % 2
                act.wait_ge(pmax_ready, h + 1)
                nc.scalar.activation(PP[:, i, 0:P], PP[:, i, 0:P], ACT.Exp, bias=MXP[:, i, 0:1],
                                     accum_out=RSP[:, i, 0:1])
                nc.scalar.activation(PP[:, i, P:384], PP[:, i, P:384], ACT.Exp, bias=MXP[:, i, 1:2],
                                     accum_out=RSP[:, i, 1:2]).then_inc(pexp_ready, 1)

            exp_head(0)
            for h in range(H):
                i = h % 2
                if h + 1 < H:
                    exp_head(h + 1)
                act.wait_ge(probT_mm, h + 1)
                if h >= 2:
                    act.wait_ge(po_mm, h - 1)
                nc.scalar.copy(PPT[:, i, :], ps[2 + i][:, 0:384]).then_inc(probT_kept, 1)
                act.wait_ge(po_mm, h + 1)
                nc.scalar.copy(QA[:, :, h, 0:SEQ], ps[4 + i][:, :].rearrange("p (r t) -> p r t", r=2)).then_inc(po_kept, 1)
            act.wait_ge(h0_stored, 16)
            for g in range(2):
                for c in range(4):
                    act.wait_ge(s_mm, 5 * g + c + 1)
                    if c == 0 and g:
                        act.wait_ge(sT_mm, 5)
                    nc.scalar.mul(S[:, c * 512:(c + 1) * 512], ps[6 + c % 2][:, :], SCALE).then_inc(s_kept, 1)
                act.wait_ge(s_max, g + 1)
                nc.scalar.activation(S, S, ACT.Exp, bias=MXS[:, g:g + 1], accum_out=RSS[:, g:g + 1]).then_inc(s_exp, 1)
                for n in range(4):
                    act.wait_ge(sT_mm, 5 * g + n + 1)
                    if g and n == 0:
                        act.wait_ge(so_mm, 1)
                    nc.scalar.copy(PT[:, 4 * n:4 * n + 4, :], ps[2 + n % 2][:, :].rearrange("p (m q) -> p m q", m=4)
                                   ).then_inc(sT_kept, 1)
                act.wait_ge(sT_mm, 5 * g + 5)
                nc.scalar.copy(PNT[0:32], ps[5][0:32, 0:P]).then_inc(sT_kept, 1)
                act.wait_ge(soT_mm, g + 1)
                for r in range(2):
                    op = nc.scalar.copy(QA[:, r, :, SEQ + 16 * g:SEQ + 16 * g + 16].rearrange("p h (j s) -> p j h s", j=4),
                                        ps[5][:, r * P:(r + 1) * P].rearrange("p (j h s) -> p j h s", j=4, h=H))
                op.then_inc(soT_kept, 1)
            for n in range(4):
                act.wait_ge(omla_mm, n + 1)
                nc.scalar.copy(CAT[:, n, :], ps[n % 2][:, 0:T]).then_inc(cat_kept, 1)

        def dve_attention(dve, steps):
            V = nc.vector
            co = cst("cos").rearrange("p (t f) -> p t f", t=3)
            si = cst("sin").rearrange("p (t f) -> p t f", t=3)
            for n in range(4):
                dve.wait_ge(qn_mm, n + 1)
                V.tensor_copy(QN[:, n, :], ps[n][:, 0:T]).then_inc(q_kept, 1)
            for t, (t0, nt) in enumerate(TILES):
                dve.wait_ge(qp_mm, t + 1)
                if t == 2:
                    dve.wait_ge(q_kept, 5)
                q = ps[4 + t][0:nt, 0:256].rearrange("p (h f) -> p h f", h=H)
                out = QPT[0:nt, t, :].rearrange("p (h f) -> p h f", h=H)
                cb = co[0:nt, t, :].unsqueeze(1).to_broadcast([nt, H, 16])
                sb_ = si[0:nt, t, :].unsqueeze(1).to_broadcast([nt, H, 16])
                ta = TMP[0:nt, 2 * (t % 2), :].rearrange("p (h f) -> p h f", h=H)
                tb = TMP[0:nt, 2 * (t % 2) + 1, :].rearrange("p (h f) -> p h f", h=H)
                V.tensor_tensor(out[:, :, 0:16], q[:, :, 0:16], cb, ALU.mult)
                V.tensor_tensor(out[:, :, 16:32], q[:, :, 16:32], cb, ALU.mult)
                V.tensor_tensor(ta, q[:, :, 16:32], sb_, ALU.mult)
                steps.step(V.tensor_tensor(tb, q[:, :, 0:16], sb_, ALU.mult))
                V.tensor_tensor(out[:, :, 0:16], out[:, :, 0:16], ta, ALU.subtract)
                op = V.tensor_tensor(out[:, :, 16:32], out[:, :, 16:32], tb, ALU.add)
                op.then_inc(q_kept, 1)
            for n in range(8):
                dve.wait_ge(qa_mm, 2 * n + 2)
                V.tensor_copy(QA[:, 1, n, 0:SEQ], ps[(2 * n + 1) % 8][:, 0:SEQ])
                V.tensor_copy(QAS[:, 1, :, NS * n:NS * n + NS],
                              ps[(2 * n + 1) % 8][:, SEQ:T].rearrange("p (b s) -> p b s", s=NS)).then_inc(qa_dve, 1)

            def front(h):
                i = h % 2
                dve.wait_ge(pscore_mm, h + 1)
                if h >= 2:
                    dve.wait_ge(probT_mm, h - 1)
                V.scalar_tensor_tensor(PP[:, i, 0:P], ps[i][:, 0:P], SCALE, cst("mask_q"), ALU.mult, ALU.add)
                V.tensor_scalar(PP[:, i, P:SEQ], ps[i][:, P:SEQ], SCALE, None, ALU.mult)
                V.scalar_tensor_tensor(PP[:, i, SEQ:384], ps[i][:, SEQ:384], SCALE, cst("mask_q"), ALU.mult,
                                       ALU.add).then_inc(pscore_read, 1)
                dve.wait_ge(pscore_read, h + 1)
                V.tensor_reduce(MXP[:, i, 0:1], PP[:, i, 0:P], AX, ALU.max)
                steps.step(V.tensor_reduce(MXP[:, i, 1:2], PP[:, i, P:384], AX, ALU.max))
                V.tensor_scalar(MXP[:, i, 0:2], MXP[:, i, 0:2], -1.0, None, ALU.mult).then_inc(pmax_ready, 1)

            front(0)
            for h in range(H):
                i = h % 2
                if h + 1 < H:
                    front(h + 1)
                dve.wait_ge(pexp_ready, h + 1)
                steps.step(V.reciprocal(RSP[:, i, 0:2], RSP[:, i, 0:2]))
                V.tensor_scalar(PP[:, i, 0:P], PP[:, i, 0:P], RSP[:, i, 0:1], None, ALU.mult)
                V.tensor_scalar(PP[:, i, P:384], PP[:, i, P:384], RSP[:, i, 1:2], None, ALU.mult).then_inc(prob_ready, 1)
            dve.wait_ge(h0_stored, 16)
            for g in range(2):
                dve.wait_ge(s_mm, 5 * g + 5)
                if g:
                    dve.wait_ge(sT_mm, 5)
                V.scalar_tensor_tensor(S[:, 2048:2080], ps[6][:, 0:32], SCALE,
                                       cst("mask_new")[:, 32 * g:32 * g + 32], ALU.mult, ALU.add).then_inc(s_new, 1)
                dve.wait_ge(s_new, g + 1)
                dve.wait_ge(s_kept, 4 * g + 4)
                steps.step(V.tensor_reduce(MXS[:, g:g + 1], S, AX, ALU.max))
                V.tensor_scalar(MXS[:, g:g + 1], MXS[:, g:g + 1], -1.0, None, ALU.mult).then_inc(s_max, 1)
                dve.wait_ge(s_exp, g + 1)
                steps.step(V.reciprocal(RSS[:, g:g + 1], RSS[:, g:g + 1]))
                dve.wait_ge(so_mm, g + 1)
                if g:
                    dve.wait_ge(soT_mm, 1)
                V.tensor_scalar(OS, ps[4][:, 0:R], RSS[:, g:g + 1], None, ALU.mult).then_inc(so_kept, 1)

        def pool_attention(pool, store):
            load_kpe(pool)

        def load_kpe(pool):
            pool.wait_ge(ld_pages, 16)
            pool.wait_ge(y_ready, 1)
            pool.wait_ge(sstate_kept, NB)
            pool.wait_ge(h2_stored, 16)
            for i in range(16):
                if KCH[i][1] == "k":
                    load_pages(pool, mybir.EngineType.Pool, i, "kpe")

        out_mm, res_kept, ln_var, ln_std, ln_done, xt_mm, xt_kept = map(sem, (
            "out_mm", "res_kept", "ln_var", "ln_std", "ln_done", "xt_mm", "xt_kept"))
        x1_stored = sem("x1_stored")
        x1_stored_count = 16 * 3
        LNS = small[:, 512:572]

        def out_projection(pe, l, lhs, w):
            for t, (t0, nt) in enumerate(TILES):
                for n in range(2):
                    for k in range(KC):
                        mm = nc.tensor.matmul(ps[2 * t + n][0:nt, :], lhs[:, k, t0:t0 + nt],
                                              w[:, k, n * 512:(n + 1) * 512], start=(k == 0), stop=(k == KC - 1))
                mm.then_inc(out_mm, 1)

        def ln_dve(dve, steps, s, t, nt):
            V = nc.vector
            st = LNS[0:nt, 20 * t:20 * t + 12].rearrange("p (a b) -> p a b", a=2)
            mv, rs = LNS[0:nt, 20 * t + 12:20 * t + 14], LNS[0:nt, 20 * t + 14:20 * t + 15]
            for n in range(2):
                op = V.bn_stats(st[:, n, :], X[0:nt, t, n * 512:(n + 1) * 512])
            steps.step(op)
            V.bn_aggr(mv, st).then_inc(ln_var, 1)
            dve.wait_ge(ln_std, 3 * s + t + 1)
            steps.step(V.reciprocal(rs, rs))
            V.tensor_scalar(X[0:nt, t, :], X[0:nt, t, :], mv[:, 0:1], rs, ALU.subtract, ALU.mult).then_inc(ln_norm, 1)

        ln_norm = sem("ln_norm")

        def ln_act(act, s):
            for t, (t0, nt) in enumerate(TILES):
                act.wait_ge(ln_var, 3 * s + t + 1)
                nc.scalar.activation(LNS[0:nt, 20 * t + 14:20 * t + 15], LNS[0:nt, 20 * t + 13:20 * t + 14], ACT.Sqrt,
                                     bias=cst("eps", nt)).then_inc(ln_std, 1)

        def ln_pool(pool, s, dst, done):
            G = nc.gpsimd
            pool.wait_ge(ld_rows, 32 * (s + 1))
            for t, (t0, nt) in enumerate(TILES):
                pool.wait_ge(ln_norm, 3 * s + t + 1)
                G.tensor_tensor(X[0:nt, t, :], X[0:nt, t, :], ROWS[0:nt, 0, :], ALU.mult).then_inc(pool_step, 1)
                pool.wait_ge(pool_step, 3 * s + t + 1)
                G.tensor_tensor(X[0:nt, t, :], X[0:nt, t, :], ROWS[0:nt, 1, :], ALU.add).then_inc(ln_done, 1)
                pool.wait_ge(ln_done, 3 * s + t + 1)
                pool.dma_start(dst[t0:t0 + nt], X[0:nt, t, :]).then_inc(done, 16)

        def transposes_x(pe, r):
            for k in range(KC):
                if k >= 4:
                    pe.wait_ge(xt_kept, 8 * r + k - 3)
                for t, (t0, nt) in enumerate(TILES):
                    mm = nc.tensor.transpose(ps[k % 4][:, t0:t0 + nt], X[0:nt, t, k * P:(k + 1) * P], ident[0:nt, 0:nt])
                mm.then_inc(xt_mm, 1)

        def keep_xt(act, r):
            for k in range(KC):
                act.wait_ge(xt_mm, 8 * r + k + 1)
                nc.scalar.copy(XT[:, k, :], ps[k % 4][:, 0:T]).then_inc(xt_kept, 1)

        W3 = M[:, 0:6144]
        XGT, HS, HH, HT, YS = (at(M, 6144, 2, KC, 2 * CAP), at(M, 9216, 2, P), at(M, 9472, 2, P), at(M, 9728, 2, P),
                               at(M, 9984, 2, 512))
        XG = at(M, 18432, 2, D)
        RT = M[:, 11008:12288]
        GY = at(M, 12288, 3, 2, D)
        yd = nc.dram_tensor("expert_rows", (SLOT_ROWS, D), F32).ap()
        xd = [nc.dram_tensor(f"x_rows{l}", (T, D), F32).ap() for l in range(2)]
        slots = [nc.dram_tensor(f"slot_tokens{l}", (SLOT_ROWS, 1), I32).ap() for l in range(2)]
        TID, DI = ints[:, 0:3], ints[:, 3:9]
        IDX, IDXX = ints[:, 9:17], ints[0:CAP, 17:17 + MAX_EXTRA]
        XE, XN = ints[:, 25:25 + MAX_EXTRA], ints[:, 33:35]
        tables_ready = sem("tables_ready")
        logit_mm, logit_exp, pick_ready, rank_mm, dest_ready, tok_scattered, xg_zero = map(sem, (
            "logit_mm", "logit_exp", "pick_ready", "rank_mm", "dest_ready", "tok_scattered", "xg_zero"))
        w_ld = [sem(f"w_ld{i}") for i in range(4)]
        gat, ystore = [sem("gat0"), sem("gat1")], [sem("ystore0"), sem("ystore1")]
        idx_ld, xT_mm, xgt_kept, gu_mm, hs_ready, hh_ready, ht_mm, ht_kept, y_mm, ys_kept, gy_ld = map(sem, (
            "idx_ld", "xT_mm", "xgt_kept", "gu_mm", "hs_ready", "hh_ready", "ht_mm", "ht_kept", "y_mm", "ys_kept",
            "gy_ld"))
        EX = [{k: sem(f"extra{l}_{k}") for k in ("w_ld", "gat", "pe", "act", "dve", "ystore")} for l in range(2)]
        EXTRA_STEPS = {"xT_mm": ("pe", 4, 1), "gu_mm": ("pe", 4, 2), "ht_mm": ("pe", 4, 3), "y_mm": ("pe", 4, 4),
                       "hs_ready": ("act", 3, 1), "ht_kept": ("act", 3, 2), "ys_kept": ("act", 3, 3),
                       "xgt_kept": ("dve", 2, 1), "hh_ready": ("dve", 2, 2)}

        def wait_extra(eng, l, step, i):
            who, n, k = EXTRA_STEPS[step]
            eng.wait_ge(EX[l][who], i * n + k)

        def w_slot(s):
            return slot_t[:, 6144 * s:6144 * (s + 1)] if s < 3 else W3

        def weights(s):
            w = w_slot(s)
            return (w[:, 0:4096].rearrange("p (k h f) -> p k h f", k=KC, h=2),
                    w[:, 4096:6144].rearrange("p (h d) -> p h d", h=2))

        def each_item(eng, l, body):
            for u in range(4):
                body(l, 16 * l + u, u)
            with eng.Fori(1, 3) as q:
                for u in range(4):
                    body(l, q * 4 + (16 * l + u), u)
            for u in range(4):
                body(l, 16 * l + 12 + u, u)

        def each_extra(eng, l, body):
            eng.wait_ge(dest_ready, l + 1)
            n_extra = eng.value_load(XN[0:1, l:l + 1], min_val=0, max_val=MAX_EXTRA)
            with eng.Fori(0, MAX_EXTRA) as i:
                with eng.If(i < n_extra):
                    body(i)

        def before(N, n):
            return not (isinstance(N, int) and N < n)

        def loads_moe(sp, l):
            src = a["w_moe"]
            if l == 0:
                sp.wait_ge(v_used, 7)
                sp.wait_ge(v_used, 8)
                for n in (1, 2):
                    sp.dma_start(w_slot(n), src[0, n]).then_inc(w_ld[n], 16)
                sp.wait_ge(omla_mm, 4)
                sp.wait_ge(ckv_stored, 48)
                sp.dma_start(w_slot(0), src[0, 0]).then_inc(w_ld[0], 16)
                sp.wait_ge(out_mm, 3)
                sp.dma_start(w_slot(3), src[0, 3]).then_inc(w_ld[3], 16)
                first_q = 1
            else:
                for n in range(3):
                    sp.wait_ge(y_mm, 13 + n)
                    sp.dma_start(w_slot(n), src[1, n]).then_inc(w_ld[n], 16)
                loads_conformer(sp)
                sp.wait_ge(out_mm, 6)
                sp.dma_start(w_slot(3), src[1, 3]).then_inc(w_ld[3], 16)
                first_q = 1
            sp.wait_ge(ln_done, 6 * l + 3)
            sp.dma_start(ROWS[:, 0, :], a["rows"][2 * l + 1]).then_inc(ld_rows, 16)
            sp.dma_start(ROWS[:, 1, :], a["rows_b"][2 * l + 1]).then_inc(ld_rows, 16)
            with sp.Fori(first_q, 4) as q:
                for u in range(4):
                    sp.wait_ge(y_mm, q * 4 + (16 * l + u - 3))
                    sp.dma_start(w_slot(u), src[l, bass.ds(q * 4 + u, 1)].rearrange("a p f -> (a p) f")
                                 ).then_inc(w_ld[u], 16)
            sp.wait_ge(y_mm, 16 * (l + 1))

            def body(i):
                e = sp.value_load(XE[0:1, bass.ds(i, 1)], min_val=0, max_val=NE - 1)
                sp.wait_ge(EX[l]["gat"], i * 16 + 16)
                sp.dma_start(W3, src[l, bass.ds(e, 1)].rearrange("a p f -> (a p) f")).then_inc(EX[l]["w_ld"], 16)
            each_extra(sp, l, body)
            if l == 0:
                sp.wait_ge(ln_done, 6)
                sp.dma_start(ROWS[:, 0, :], a["rows"][2]).then_inc(ld_rows, 16)
                sp.dma_start(ROWS[:, 1, :], a["rows_b"][2]).then_inc(ld_rows, 16)

        def gathered_transposes(pe, xb):
            for k in range(KC):
                mm = nc.tensor.transpose(ps[k // 4][:, k % 4 * P:(k % 4 + 1) * P], XG[:, xb, k * P:(k + 1) * P], ident)
            return mm

        def gate_up(pe, slot, xb, b):
            wgu, _ = weights(slot)
            for k in range(KC):
                for h in range(2):
                    mm = nc.tensor.matmul(ps[2 + b][64 * h:64 * h + 64, 0:256], XGT[:, xb, k, CAP * b:CAP * b + CAP],
                                          wgu[:, k, h, :], start=(k == 0), stop=(k == KC - 1), skip_group_check=True)
            return mm

        def down(pe, slot, b):
            _, wd = weights(slot)
            for h in range(2):
                for n in range(2):
                    mm = nc.tensor.matmul(ps[6 + b][64 * n:64 * n + 64, :], HT[:, b, h * 64:h * 64 + 64],
                                          wd[:, h, n * 512:(n + 1) * 512], start=(h == 0), stop=(h == 1),
                                          skip_group_check=True)
            return mm

        def products_moe(pe, l):
            pe.wait_ge(ln_done, 6 * l + 3)
            pe.wait_ge(res_kept, 3 * l + 3)
            transposes_x(pe, 2 * l)
            pe.wait_ge(xt_kept, 16 * l + 8)
            if l:
                pe.wait_ge(ys_kept, 16 * l)
            wr = prm("w_router").rearrange("p (k e) -> p k e", k=KC)
            for t, (t0, nt) in enumerate(TILES):
                for k in range(KC):
                    mm = nc.tensor.matmul(ps[6][0:nt, t * NE:(t + 1) * NE], XT[:, k, t0:t0 + nt], wr[:, k, :],
                                          start=(k == 0), stop=(k == KC - 1))
            mm.then_inc(logit_mm, 1)
            pe.wait_ge(pick_ready, l + 1)
            picks = RT[:, 0:48].rearrange("p (t e) -> p t e", t=3)
            for t in range(3):
                for u in range(t + 1):
                    nc.tensor.matmul(ps[7][:, t * NE:(t + 1) * NE], cst("tri_strict") if u == t else ones,
                                     picks[:, u, :], start=(u == 0), stop=(u == t))
            for u in range(3):
                mm = nc.tensor.matmul(ps[7][:, 48:64], ones, picks[:, u, :], start=(u == 0), stop=(u == 2))
            mm.then_inc(rank_mm, 1)
            pe.wait_ge(dest_ready, l + 1)


            def transposes(N, u):
                pe.wait_ge(gat[u // 2], (N - u) * 4 + 16)
                if before(N, 2):
                    pe.wait_ge(xgt_kept, N // 2)
                gathered_transposes(pe, u // 2).then_inc(xT_mm, 1)

            def second_half(N, u):
                b = u % 2
                pe.wait_ge(hh_ready, N + 1)
                if before(N, 2):
                    pe.wait_ge(ht_kept, N - 1)
                nc.tensor.transpose(ps[4 + b][:, 0:P], HH[:, b, :], ident).then_inc(ht_mm, 1)
                pe.wait_ge(ht_kept, N + 1)
                if before(N, 2):
                    pe.wait_ge(ys_kept, N - 1)
                down(pe, u, b).then_inc(y_mm, 1)

            def item(l, N, u):
                pe.wait_ge(w_ld[u], (N - u) * 4 + 16)
                pe.wait_ge(xgt_kept, (N - u % 2) // 2 + 1)
                if before(N, 2):
                    pe.wait_ge(hh_ready, N - 1)
                gate_up(pe, u, u // 2, u % 2).then_inc(gu_mm, 1)
                if u % 2 and not (isinstance(N, int) and N == 16 * l + 15):
                    transposes(N + 1, (u + 1) % 4)
                if not (isinstance(N, int) and N == 16 * l):
                    second_half(N - 1, (u - 1) % 4)

            transposes(16 * l, 0)
            each_item(pe, l, item)
            second_half(16 * l + 15, 3)
            pe.wait_ge(ys_kept, 16 * (l + 1))

            def extra(i):
                x = EX[l]
                pe.wait_ge(x["gat"], i * 16 + 16)
                gathered_transposes(pe, 0).then_inc(x["pe"], 1)
                pe.wait_ge(x["w_ld"], i * 16 + 16)
                wait_extra(pe, l, "xgt_kept", i)
                gate_up(pe, 3, 0, 0).then_inc(x["pe"], 1)
                wait_extra(pe, l, "hh_ready", i)
                nc.tensor.transpose(ps[4][:, 0:P], HH[:, 0, :], ident).then_inc(x["pe"], 1)
                wait_extra(pe, l, "ht_kept", i)
                down(pe, 3, 0).then_inc(x["pe"], 1)
            each_extra(pe, l, extra)

        def act_moe(act, steps, l):
            keep_xt(act, 2 * l)
            act.wait_ge(logit_mm, l + 1)
            act.wait_ge(xg_zero, l + 1)
            lg = RT[:, 48:96].rearrange("p (t e) -> p t e", t=3)
            nc.scalar.activation(lg[:, 0:2, :], ps[6][:, 0:32].rearrange("p (t e) -> p t e", t=2), ACT.Exp, scale=-1.0)
            nc.scalar.activation(lg[0:32, 2, :], ps[6][0:32, 32:48], ACT.Exp, scale=-1.0).then_inc(logit_exp, 1)

            def silu(b):
                return nc.scalar.activation(HS[:, b, :], ps[2 + b][:, 0:P], ACT.Silu)

            def keep_ht(b):
                return nc.scalar.copy(HT[:, b, :], ps[4 + b][:, 0:P])

            def keep_y(b):
                return nc.scalar.copy(YS[:, b, :], ps[6 + b][:, :])

            def store_y(row, b, done):
                for n in range(2):
                    act.dma_start(yd[bass.ds(row, CAP), n * 512:(n + 1) * 512], YS[64 * n:64 * n + 64, b, :]
                                  ).then_inc(done, 16)

            def second_half(N, u):
                b = u % 2
                act.wait_ge(ht_mm, N + 1)
                if before(N, 2):
                    act.wait_ge(y_mm, N - 1)
                keep_ht(b).then_inc(ht_kept, 1)
                act.wait_ge(y_mm, N + 1)
                if before(N, 2):
                    act.wait_ge(ystore[b], (N - u % 2) * 16)
                keep_y(b).then_inc(ys_kept, 1)
                act.wait_ge(ys_kept, N + 1)
                store_y((N - 16 * l) * CAP, b, ystore[b])

            def item(l, N, u):
                act.wait_ge(gu_mm, N + 1)
                if before(N, 2):
                    act.wait_ge(hh_ready, N - 1)
                silu(u % 2).then_inc(hs_ready, 1)
                if not (isinstance(N, int) and N == 16 * l):
                    second_half(N - 1, (u - 1) % 4)

            act.wait_ge(tok_scattered, 96 * (l + 1))
            act.dma_start(IDX, slots[l][0:NE * CAP].rearrange("(n p) o -> p (n o)", p=P),
                          allow_slow_non_contiguous=True).then_inc(idx_ld, 16)
            act.dma_start(IDXX, slots[l][NE * CAP:].rearrange("(n p) o -> p (n o)", p=CAP),
                          allow_slow_non_contiguous=True).then_inc(idx_ld, 16)
            each_item(act, l, item)
            second_half(16 * l + 15, 3)

            def extra(i):
                x = EX[l]
                wait_extra(act, l, "gu_mm", i)
                silu(0).then_inc(x["act"], 1)
                wait_extra(act, l, "ht_mm", i)
                keep_ht(0).then_inc(x["act"], 1)
                wait_extra(act, l, "y_mm", i)
                keep_y(0).then_inc(x["act"], 1)
                wait_extra(act, l, "ys_kept", i)
                store_y(i * CAP + NE * CAP, 0, x["ystore"])
            act.wait_ge(ystore[0], 256 * (l + 1))
            each_extra(act, l, extra)

        def dve_moe(dve, steps, l):
            V = nc.vector
            t3 = lambda off, n=NE: RT[:, off:off + 3 * n].rearrange("p (t e) -> p t e", t=3)
            M12, EXPL, PR, SEL = t3(0), t3(48), t3(96), t3(144)
            O1, O2, W16, SM = t3(192), t3(240), t3(288), t3(336)
            four = RT[:, 384:384 + 8 * 12].rearrange("p (n g) -> p n g", n=8)
            three = RT[:, 480:480 + 8 * 3].rearrange("p (n t) -> p n t", n=8)
            G12 = RT[:, 504:516].rearrange("p (t g) -> p t g", t=3)
            RK_ = t3(520)
            D12 = RT[:, 568:574].rearrange("p (t k) -> p t k", t=3)
            big = lambda x: x.unsqueeze(2)
            if l:
                dve.wait_ge(cconv_stored, 32)
            V.memset(EXPL, 0.0).then_inc(xg_zero, 1)
            dve.wait_ge(logit_exp, l + 1)
            steps.step(V.tensor_scalar(PR, EXPL, 1.0, None, ALU.add))
            steps.step(V.reciprocal(PR, PR))
            steps.step(V.tensor_tensor(SEL, PR, prm("r_bias").unsqueeze(1).to_broadcast([P, 3, NE]), ALU.add))
            s4 = SEL.rearrange("p t (g m) -> p (t g) m", m=4)
            V.tensor_tensor(four[:, 0, :], s4[:, :, 0], s4[:, :, 1], ALU.max)
            V.tensor_tensor(four[:, 1, :], s4[:, :, 0], s4[:, :, 1], ALU.min)
            V.tensor_tensor(four[:, 2, :], s4[:, :, 2], s4[:, :, 3], ALU.max)
            steps.step(V.tensor_tensor(four[:, 3, :], s4[:, :, 2], s4[:, :, 3], ALU.min))
            V.tensor_tensor(four[:, 4, :], four[:, 0, :], four[:, 2, :], ALU.max)
            V.tensor_tensor(four[:, 5, :], four[:, 0, :], four[:, 2, :], ALU.min)
            steps.step(V.tensor_tensor(four[:, 6, :], four[:, 1, :], four[:, 3, :], ALU.max))
            steps.step(V.tensor_tensor(four[:, 5, :], four[:, 5, :], four[:, 6, :], ALU.max))
            steps.step(V.tensor_tensor(four[:, 7, :], four[:, 4, :], four[:, 5, :], ALU.add))

            def first_largest(values, out, prio, n, tmp, tmp3):
                steps.step(V.tensor_reduce(tmp3, values, AX, ALU.max))
                steps.step(V.tensor_tensor(tmp, values, big(tmp3).to_broadcast([P, 3, n]), ALU.is_equal))
                steps.step(V.tensor_tensor(tmp, tmp, prio.unsqueeze(1).to_broadcast([P, 3, n]), ALU.mult))
                steps.step(V.tensor_reduce(tmp3, tmp, AX, ALU.max))
                steps.step(V.tensor_tensor(out, tmp, big(tmp3).to_broadcast([P, 3, n]), ALU.is_equal))

            grp = four[:, 7, :].rearrange("p (t g) -> p t g", t=3)
            tmp4 = four[:, 0, :].rearrange("p (t g) -> p t g", t=3)
            first_largest(grp, G12, cst("prio4"), 4, tmp4, three[:, 0, :])
            gflat = G12.rearrange("p t g -> p (t g)")
            steps.step(V.tensor_scalar(four[:, 1, :], gflat, 1.0, -NEG, ALU.subtract, ALU.mult))
            smv = SM.rearrange("p t (g m) -> p (t g) m", m=4)
            steps.step(V.tensor_tensor(smv, s4, gflat.unsqueeze(2).to_broadcast([P, 12, 4]), ALU.mult))
            steps.step(V.tensor_tensor(smv, smv, four[:, 1, :].unsqueeze(2).to_broadcast([P, 12, 4]), ALU.add))
            first_largest(SM, O1, cst("prio16"), NE, W16, three[:, 0, :])
            steps.step(V.scalar_tensor_tensor(SM, O1, 2 * NEG, SM, ALU.mult, ALU.add))
            first_largest(SM, O2, cst("prio16"), NE, W16, three[:, 0, :])
            valid = cst("valid").unsqueeze(2).to_broadcast([P, 3, NE])
            V.tensor_tensor(O1, O1, valid, ALU.mult)
            steps.step(V.tensor_tensor(O2, O2, valid, ALU.mult))
            V.tensor_tensor(M12, O1, O2, ALU.add).then_inc(pick_ready, 1)
            for k, o_ in enumerate((O1, O2)):
                steps.step(V.tensor_tensor(W16, PR, o_, ALU.mult))
                steps.step(V.tensor_reduce(three[:, 1 + k, :], W16, AX, ALU.add))
            steps.step(V.tensor_tensor(three[:, 3, :], three[:, 1, :], three[:, 2, :], ALU.add))
            steps.step(V.tensor_scalar(three[:, 3, :], three[:, 3, :], 1e-30, None, ALU.max))
            steps.step(V.reciprocal(three[:, 3, :], three[:, 3, :]))
            V.tensor_tensor(three[:, 4, :], three[:, 1, :], three[:, 3, :], ALU.mult)
            V.tensor_tensor(three[:, 5, :], three[:, 2, :], three[:, 3, :], ALU.mult)
            dve.wait_ge(rank_mm, l + 1)
            FL = RT[:, 600:664].rearrange("p (e j) -> p e j", e=NE)
            EXT, CUM, BASE = RT[:, 664:680], RT[:, 680:696], RT[:, 696:712]
            steps.step(V.tensor_tensor(FL, ps[7][:, 48:64].unsqueeze(2).to_broadcast([P, NE, 4]),
                                       cst("item_thr").rearrange("p (e j) -> p e j", e=NE), ALU.is_gt))
            steps.step(V.tensor_reduce(EXT, FL, AX, ALU.add))
            steps.step(V.tensor_tensor_scan(CUM, EXT, EXT, 0.0, ALU.add, ALU.bypass))
            V.tensor_copy(XN[0:1, l:l + 1], CUM[0:1, 15:16])
            steps.step(V.tensor_tensor(BASE, CUM, EXT, ALU.subtract))
            steps.step(V.tensor_scalar(BASE, BASE, float(CAP), float((NE - 1) * CAP), ALU.mult, ALU.add))
            steps.step(V.tensor_tensor(BASE, BASE, cst("row_of"), ALU.subtract))
            rank = ps[7][:, 0:48].rearrange("p (t e) -> p t e", t=3)
            steps.step(V.scalar_tensor_tensor(W16, rank, float(CAP), BASE.unsqueeze(1).to_broadcast([P, 3, NE]),
                                              ALU.is_ge, ALU.mult))
            steps.step(V.tensor_tensor(W16, W16, cst("row_of").unsqueeze(1).to_broadcast([P, 3, NE]), ALU.add))
            steps.step(V.tensor_tensor(RK_, rank, W16, ALU.add))
            for k, o_ in enumerate((O1, O2)):
                steps.step(V.tensor_tensor(W16, RK_, o_, ALU.mult))
                steps.step(V.tensor_reduce(D12[:, :, k], W16, AX, ALU.add))
            steps.step(V.tensor_copy(DI.rearrange("p (t k) -> p t k", t=3), D12))
            ended = RT[0:1, 712:712 + MAX_EXTRA * NE].rearrange("p (i e) -> p i e", i=MAX_EXTRA)
            out8 = RT[0:1, 1264:1272]
            steps.step(V.tensor_tensor(ended, CUM[0:1].unsqueeze(1).to_broadcast([1, MAX_EXTRA, NE]),
                                       cst("item_k", 1).unsqueeze(2).to_broadcast([1, MAX_EXTRA, NE]), ALU.is_le))
            steps.step(V.tensor_reduce(out8, ended, AX, ALU.add))
            V.tensor_copy(XE[0:1], out8).then_inc(dest_ready, 1)
            dve.wait_ge(dest_ready, l + 1)
            for t, (t0, nt) in enumerate(TILES):
                dve.wait_ge(x1_stored, 48 * (l + 1))
                dve.wait_ge(xt_kept, 16 * l + 8)
                op = V.tensor_scalar(X[0:nt, t, :], X[0:nt, t, :], ALPHA, None, ALU.mult)
            steps.step(op)

            def keep_xgt(xb):
                for n in range(2):
                    op = V.tensor_copy(XGT[:, xb, 4 * n:4 * n + 4], ps[n][:, :].rearrange("p (k s) -> p k s", k=4))
                return op

            def gate(b):
                return V.tensor_tensor(HH[:, b, :], HS[:, b, :], ps[2 + b][:, P:256], ALU.mult)

            def keep(N, u):
                dve.wait_ge(xT_mm, N // 2 + 1)
                if before(N, 4):
                    dve.wait_ge(gu_mm, N - 2)
                keep_xgt(u // 2).then_inc(xgt_kept, 1)

            def item(l, N, u):
                if u % 2 and not (isinstance(N, int) and N == 16 * l + 15):
                    keep(N + 1, (u + 1) % 4)
                dve.wait_ge(hs_ready, N + 1)
                if before(N, 2):
                    dve.wait_ge(ht_mm, N - 1)
                gate(u % 2).then_inc(hh_ready, 1)

            keep(16 * l, 0)
            each_item(dve, l, item)

            def extra(i):
                x = EX[l]
                wait_extra(dve, l, "xT_mm", i)
                keep_xgt(0).then_inc(x["dve"], 1)
                wait_extra(dve, l, "hs_ready", i)
                gate(0).then_inc(x["dve"], 1)
            each_extra(dve, l, extra)
            for t, (t0, nt) in enumerate(TILES):
                dve.wait_ge(gy_ld, 96 * (l + 1))
                for k in range(2):
                    op = V.scalar_tensor_tensor(X[0:nt, t, :], GY[0:nt, t, k, :], three[0:nt, 4 + k, t:t + 1], X[0:nt, t, :],
                                                ALU.mult, ALU.add)
                    steps.step(op)
                ln_dve(dve, steps, 2 * l + 1, t, nt)

        def pool_moe(pool, l):
            G = nc.gpsimd
            pool.wait_ge(out_mm, 3 * (l + 1))
            if l == 0:
                G.memset(XG, 0.0).then_inc(zeroed, 1)
                pool.wait_ge(zeroed, 2)
                for n in range(4):
                    pool.dma_start(yd[NE * CAP + n * P:NE * CAP + (n + 1) * P], XG[:, n % 2, :]).then_inc(tables_ready, 16)
                pool.wait_ge(tables_ready, 112)
            pool.wait_ge(tables_ready, 112)
            pool.wait_ge(x1_stored, 48 * (l + 1))
            pool.wait_ge(dest_ready, l + 1)
            for t, (t0, nt) in enumerate(TILES):
                for k in range(2):
                    pool.indirect_dma_start(out=slots[l], out_offset=bass.IndirectOffsetOnAxis(
                        ap=DI[0:nt, 2 * t + k:2 * t + k + 1], axis=0), in_=TID[0:nt, t:t + 1], in_offset=None
                        ).then_inc(tok_scattered, 16)
            pool.wait_ge(tok_scattered, 96 * (l + 1))

            pool.wait_ge(idx_ld, 32 * (l + 1))

            def gather(b, rows, idx, done):
                pool.indirect_dma_start(out=XG[0:rows, b, :], out_offset=None, in_=xd[l],
                                        in_offset=bass.IndirectOffsetOnAxis(ap=idx, axis=0),
                                        bounds_check=T - 1, oob_is_err=False).then_inc(done, 16)

            for n in range(NE // 2):
                if n >= 2:
                    pool.wait_ge(xT_mm, 8 * l + n - 1)
                gather(n % 2, P, IDX[:, n:n + 1], gat[n % 2])
            pool.wait_ge(ystore[0], 256 * (l + 1))
            pool.wait_ge(ystore[1], 256 * (l + 1))
            n_extra = pool.value_load(XN[0:1, l:l + 1], min_val=0, max_val=MAX_EXTRA)
            for i in range(MAX_EXTRA):
                with pool.If(n_extra > i):
                    gather(0, CAP, IDXX[:, i:i + 1], EX[l]["gat"])
                    pool.wait_ge(EX[l]["ystore"], 32 * (i + 1))
            for t, (t0, nt) in enumerate(TILES):
                for k in range(2):
                    pool.indirect_dma_start(out=GY[0:nt, t, k, :], out_offset=None, in_=yd,
                                            in_offset=bass.IndirectOffsetOnAxis(
                                                ap=DI[0:nt, 2 * t + k:2 * t + k + 1], axis=0)).then_inc(gy_ld, 16)

        def products_layer_out(pe, l):
            if l == 0:
                pe.wait_ge(cat_kept, 4)
                pe.wait_ge(ld_wout, 16)
                pe.wait_ge(y_ready, 1)
                out_projection(pe, 0, CAT, WOUT)
            else:
                pe.wait_ge(cn_ready, 8)
                pe.wait_ge(ld_cout, 16)
                out_projection(pe, 1, CV, CWO)
            products_moe(pe, l)

        def act_layer_out(act, steps, l):
            ln_act(act, 2 * l)
            act_moe(act, steps, l)
            ln_act(act, 2 * l + 1)

        def dve_layer_out(dve, steps, l):
            V = nc.vector
            dve.wait_ge(ld_x, 48)
            if l:
                dve.wait_ge(ld_bout, 16)
                dve.wait_ge(xt_kept, 16)
                dve.wait_ge(xf_stored, 48)
            for t, (t0, nt) in enumerate(TILES):
                dve.wait_ge(out_mm, 3 * l + t + 1)
                for n in range(2):
                    xv = X[0:nt, t, n * 512:(n + 1) * 512]
                    op = V.scalar_tensor_tensor(xv, xv, ALPHA, ps[2 * t + n][0:nt, :], ALU.mult, ALU.add)
                op.then_inc(res_kept, 1)
                dve.wait_ge(res_kept, 3 * l + t + 1)
                if l:
                    steps.step(V.tensor_tensor(X[0:nt, t, :], X[0:nt, t, :], BOUT[0:nt], ALU.add))
                ln_dve(dve, steps, 2 * l, t, nt)
            dve_moe(dve, steps, l)

        xf_stored, cconv_stored = sem("xf_stored"), sem("cconv_stored")

        def pool_layer_out(pool, store, l):
            if l == 0:
                for n in range(2):
                    pool.dma_start(slots[n], a["nobody"]).then_inc(tables_ready, 16)
                pool.dma_start(TID, a["token_ids"]).then_inc(tables_ready, 16)
            ln_pool(pool, 2 * l, xd[l], x1_stored)
            pool_moe(pool, l)
            if l == 0:
                ln_pool(pool, 1, xf, xf_stored)
            else:
                ln_pool(pool, 3, o["y"], stored)
                n_stored[0] += 3

        xf = nc.dram_tensor("x_between", (T, D), F32).ap()

        CWO = at(M, 0, KC, D)
        VP = at(M, 8192, KC, HIST + SEQ)
        VS = at(M, 10480, KC, NB, HIST + NS)
        CV = at(M, 12656, KC, T)
        CQ = at(M, 14960, KC, T)
        PROD = M[:, 17264:18256]
        CW = at(M, 18432, 4, KC, P)
        MU, RC = M[:, 22528:22816], M[:, 22816:23104]
        BOUT = M[:, 23104:24128]
        SG = at(M, 17264, 2, T)
        ld_cout, ld_chist, glu_mm, sig_ready, v_ready, dw_ready, mean_kept, cn_ready = map(sem, (
            "ld_cout", "ld_chist", "glu_mm", "sig_ready", "v_ready", "dw_ready", "mean_kept", "cn_ready"))

        def loads_conformer(sp):
            sp.wait_ge(ln_norm, 6)
            sp.wait_ge(zeroed, 3)
            sp.dma_start(VS[:, :, :, 0:HIST], a["conf_hist"]).then_inc(ld_chist, 16)
            for n in range(16):
                if n >= 4:
                    sp.wait_ge(glu_mm, n - 3)
                sp.dma_start(CW[:, n % 4], a["w_conf"][n // 2 + 8 * (n % 2)]).then_inc(ld_win[n % 4], 16)
            sp.dma_start(CWO, a["w_conf_out"]).then_inc(ld_cout, 16)
            sp.dma_start(BOUT, a["rows"][4]).then_inc(ld_bout, 16)

        def products_conformer(pe):
            pe.wait_ge(ln_done, 6)
            transposes_x(pe, 1)
            pe.wait_ge(xt_kept, 16)
            for n in range(16):
                pe.wait_ge(ld_win[n % 4], 16 * ((15 - n % 4 + 3) // 4 + n // 4 + 1))
                if n >= 8:
                    pe.wait_ge(v_ready, (n - 8) // 2 + 1)
                for k in range(KC):
                    mm = nc.tensor.matmul(ps[n % 8][:, 0:T], CW[:, n % 4, k, :], XT[:, k, :], start=(k == 0),
                                          stop=(k == KC - 1))
                mm.then_inc(glu_mm, 1)
            pe.wait_ge(v_ready, 8)
            for k in range(KC):
                pe.wait_ge(dw_ready, k + 1)
                mm = nc.tensor.matmul(ps[0][:, 0:T], ones, CV[:, k, :], start=(k == 0), stop=(k == KC - 1))
            mm.then_inc(sum_mm, 1)
            pe.wait_ge(sq_ready, 8)
            for k in range(KC):
                mm = nc.tensor.matmul(ps[1][:, 0:T], ones, CQ[:, k, :], start=(k == 0), stop=(k == KC - 1))
            mm.then_inc(sum_mm, 1)
            pe.wait_ge(std_ready, 4)

        def act_conformer(act, steps):
            bi = prm("b_in")
            keep_xt(act, 1)
            for k in range(8):
                act.wait_ge(glu_mm, 2 * k + 2)
                if k >= 2:
                    act.wait_ge(v_ready, k - 1)
                nc.scalar.activation(SG[:, k % 2, :], ps[(2 * k + 1) % 8][:, 0:T], ACT.Sigmoid,
                                     bias=bi[:, 8 + k:9 + k]).then_inc(sig_ready, 1)
            act.wait_ge(mean_kept, 1)
            nc.scalar.activation(CQ, CV, ACT.Square).then_inc(sq_ready, 1)
            act.wait_ge(sum_mm, 4)
            nc.scalar.activation(RC, ps[1][:, 0:T], ACT.Sqrt, bias=eps, scale=1.0 / D).then_inc(std_ready, 1)
            act.wait_ge(mean_kept, 2)
            for k in range(8):
                nc.scalar.activation(CV[:, k, :], CV[:, k, :], ACT.Silu, bias=prm("bn")[:, k:k + 1],
                                     scale=prm("gn")[:, k:k + 1]).then_inc(cn_ready, 1)

        def dve_conformer(dve, steps):
            V = nc.vector
            bi = prm("b_in")
            dw = prm("dw_w").rearrange("p (c k) -> p c k", k=KW)
            dve.wait_ge(zeroed, 3)
            dve.wait_ge(ld_chist, 16)
            for k in range(8):
                dve.wait_ge(sig_ready, k + 1)
                b = ps[(2 * k) % 8]
                V.scalar_tensor_tensor(VP[:, k, HIST:], b[:, 0:SEQ], bi[:, k:k + 1], SG[:, k % 2, 0:SEQ], ALU.add, ALU.mult)
                V.scalar_tensor_tensor(VS[:, k, :, HIST:], b[:, SEQ:T].rearrange("p (b s) -> p b s", s=NS), bi[:, k:k + 1],
                                       SG[:, k % 2, SEQ:T].rearrange("p (b s) -> p b s", s=NS), ALU.add, ALU.mult
                                       ).then_inc(v_ready, 1)
            dve.wait_ge(v_ready, 8)
            for k in range(8):
                cp = CV[:, k, 0:SEQ]
                steps.step(V.tensor_scalar(cp, VP[:, k, 0:SEQ], dw[:, k, 0:1], prm("dw_b")[:, k:k + 1], ALU.mult, ALU.add))
                for j in range(1, KW):
                    steps.step(V.scalar_tensor_tensor(cp, VP[:, k, j:j + SEQ], dw[:, k, j:j + 1], cp, ALU.mult, ALU.add))
                for half_ in range(2):
                    pv = PROD[:, 0:16 * KW].rearrange("p (b s j) -> p b s j", b=4, s=NS)
                    for s in range(NS):
                        op = V.tensor_tensor(pv[:, :, s, :], VS[:, k, 4 * half_:4 * half_ + 4, s:s + KW],
                                             dw[:, k, :].unsqueeze(1).to_broadcast([P, 4, KW]), ALU.mult)
                    steps.step(op)
                    cs = CV[:, k, SEQ + 16 * half_:SEQ + 16 * half_ + 16]
                    steps.step(V.tensor_reduce(cs, PROD[:, 0:16 * KW].rearrange("p (a j) -> p a j", j=KW), AX, ALU.add))
                cs = CV[:, k, SEQ:T]
                V.tensor_scalar(cs, cs, prm("dw_b")[:, k:k + 1], None, ALU.add).then_inc(dw_ready, 1)
            dve.wait_ge(dw_ready, 8)
            dve.wait_ge(sum_mm, 3)
            steps.step(V.tensor_scalar(MU, ps[0][:, 0:T], 1.0 / D, None, ALU.mult))
            V.tensor_tensor(CV, CV, MU.unsqueeze(1).to_broadcast([P, KC, T]), ALU.subtract).then_inc(mean_kept, 1)
            dve.wait_ge(std_ready, 4)
            steps.step(V.reciprocal(RC, RC))
            dve.wait_ge(mean_kept, 1)
            V.tensor_tensor(CV, CV, RC.unsqueeze(1).to_broadcast([P, KC, T]), ALU.mult).then_inc(mean_kept, 1)

        def pool_conformer(pool, store):
            G = nc.gpsimd
            pool.wait_ge(ln_norm, 6)
            G.memset(VP[:, :, 0:HIST], 0.0).then_inc(zeroed, 1)
            pool.wait_ge(v_ready, 8)
            pool.wait_ge(ld_chist, 16)
            store(o["cconv_p"], VP[:, :, SEQ:SEQ + HIST], cconv_stored)
            store(o["cconv_s"], VS[:, :, :, NS:], cconv_stored)

        block = ctx.enter_context(nc.Block())

        @block.sync
        def _(sp):
            sp.dma_start(XT, a["xT"]).then_inc(ld_xT, 16)
            sp.dma_start(WTOK, a["w_tok"]).then_inc(ld_wtok, 16)
            for n in range(4):
                sp.dma_start(WIN[:, n], a["w_ch"][n]).then_inc(ld_win[n], 16)
            sp.dma_start(C[:], a["consts"]).then_inc(ld_const, 16)
            sp.dma_start(PM[:], a["params"]).then_inc(ld_const, 16)
            sp.wait_ge(zeroed, 1)
            sp.dma_start(XS[:, :, :, 0:3], a["conv_hist"]).then_inc(ld_hist, 16)
            for n in range(4, 15):
                sp.wait_ge(piece_mm, n - 3)
                sp.dma_start(WIN[:, n % 4], a["w_ch"][n]).then_inc(ld_win[n % 4], 16)
            sp.dma_start(slot_t[:, 0:4352], a["w_q"]).then_inc(ld_wq, 16)
            for t, (t0, nt) in enumerate(TILES):
                sp.dma_start(X[0:nt, t, :], a["x"][t0:t0 + nt]).then_inc(ld_x, 16)
            sp.wait_ge(piece_mm, 15)
            sp.dma_start(H0, a["state"]).then_inc(ld_h0, 16)
            loads_attention(sp)
            loads_moe(sp, 0)
            loads_moe(sp, 1)

        @block.tensor
        def _(pe):
            pe.wait_ge(ld_xT, 16)
            pe.wait_ge(ld_wtok, 16)
            for t, (t0, nt) in enumerate(TILES):
                for k in range(KC):
                    mm = nc.tensor.matmul(ps[4 + t][0:nt, 0:296], XT[:, k, t0:t0 + nt], WTOK[:, k, :],
                                          start=(k == 0), stop=(k == KC - 1))
                mm.then_inc(tok_mm, 1)
            for n in range(15):
                pe.wait_ge(ld_win[n % 4], 16 * (n // 4 + 1))
                if 4 <= n < 7:
                    pe.wait_ge(hq_kept, n - 3)
                elif n >= 7:
                    pe.wait_ge(ch_kept, n - 6)
                for k in range(KC):
                    mm = nc.tensor.matmul(ps[n % 4][:, 0:T], WIN[:, n % 4, k, :], XT[:, k, :],
                                          start=(k == 0), stop=(k == KC - 1))
                mm.then_inc(piece_mm, 1)
            pe.wait_ge(sq_ready, 6)
            for k in range(3):
                mm = nc.tensor.matmul(ps[7][:, 0:T], ones, SQ[:, k, :], start=(k == 0), stop=(k == 2))
            mm.then_inc(sum_mm, 1)
            pe.wait_ge(kv_ready, 1)
            pe.wait_ge(tok_kept, 3)
            for t, (t0, nt) in enumerate(TILES):
                for r in range(2):
                    nc.tensor.transpose(ps[4 + r][:, t0:t0 + nt], CK[0:nt, t, r * P:(r + 1) * P], ident[0:nt, 0:nt])
                mm = nc.tensor.transpose(ps[6][0:32, t0:t0 + nt], KPE[0:nt, t, :], ident[0:nt, 0:nt])
            mm.then_inc(kvT_mm, 1)
            pe.wait_ge(dtA_ready, 1)
            pe.wait_ge(std_ready, 2)
            b = ps[7]
            for c in range(2):
                nc.tensor.matmul(b[:, 8 * c:8 * c + 8], cst("tri"), DTA[:, c, :], start=True, stop=True)
                nc.tensor.matmul(b[:, 16 + 8 * c:24 + 8 * c], ones, DTA[:, c, :], start=True, stop=True)
            nc.tensor.matmul(b[:, 32:96], ones[0:32, :], DTAM[0:32].rearrange("p b h -> p (b h)"), start=True, stop=True)
            nc.tensor.matmul(b[0:32, 96:104], cst("tri_s", 32), DTA[0:32, 2, :], start=True, stop=True)
            nc.tensor.matmul(b[0:32, 104:112], cst("blk_s", 32), DTA[0:32, 2, :], start=True,
                             stop=True).then_inc(acs_mm, 1)
            pe.wait_ge(ch_kept, 12)
            for h in range(H):
                if h >= 4:
                    pe.wait_ge(seg_ready, h - 3)
                    pe.wait_ge(e_ready, h - 3)
                for c in range(2):
                    nc.tensor.matmul(ps[h % 4][:, c * P:(c + 1) * P], DTA[:, c, h:h + 1].to_broadcast([P, P]),
                                     cst("tri"), start=True, stop=True)
                nc.tensor.matmul(ps[h % 4][:, SEQ:T], DTA[0:32, 2, h:h + 1].to_broadcast([32, P]),
                                 cst("tri_s", 32), start=True, stop=True).then_inc(row_mm, 1)
            pe.wait_ge(xb_ready, 1)
            pe.wait_ge(kvT_kept, 1)
            for t, (t0, nt) in enumerate(TILES):
                for k in range(4):
                    mm = nc.tensor.transpose(ps[4 + t][0:nt, k * P:(k + 1) * P], XB[:, k, t0:t0 + nt], ident)
                mm.then_inc(xs_mm, 1)
            for t, (t0, nt) in enumerate(TILES):
                pe.wait_ge(acs_kept, 1) if t == 0 else pe.wait_ge(dx_ready, t)
                bank = ps[7] if t == 0 else ps[3 + t]
                for k in range(2):
                    mm = nc.tensor.transpose(bank[0:nt, k * P:(k + 1) * P], XB[:, 4 + k, t0:t0 + nt], ident)
                mm.then_inc(bt_mm, 1)
            pe.wait_ge(dx_ready, 3)
            pe.wait_ge(bt_kept, 1)
            for g in range(2):
                bank = ps[6 + g]
                for c in range(2):
                    nc.tensor.matmul(bank[:, c * P:(c + 1) * P], XB[:, 4 + g, c * P:(c + 1) * P],
                                     XB[:, 6 + g, c * P:(c + 1) * P], start=True, stop=True)
                nc.tensor.matmul(bank[0:32, SEQ:T], XB[:, 4 + g, SEQ:T], XB[:, 6 + g, SEQ:T],
                                 start=True, stop=True).then_inc(cb_mm, 1)
            pe.wait_ge(m_ready, 2)
            pe.wait_ge(seg_ready, H)
            pe.wait_ge(e_ready, H)
            for c, (t0, nt) in enumerate(TILES):
                for h in range(H):
                    mm = nc.tensor.matmul(ps[c][64 * (h % 2):64 * (h % 2) + 64, (h // 2) * nt:(h // 2 + 1) * nt],
                                          DX[0:nt, c, h * 64:(h + 1) * 64], L[0:nt, h, t0:t0 + nt],
                                          start=True, stop=True)
                mm.then_inc(ydiag_mm, 1)
            pe.wait_ge(bt_kept, 3)
            for c in range(2):
                for g in range(2):
                    mm = nc.tensor.matmul(ps[4 + c][:, g * 256:(g + 1) * 256], BTOK[:, c, g * P:(g + 1) * P],
                                          DXE[:, c, g * 256:(g + 1) * 256], start=True, stop=True)
                mm.then_inc(state_mm, 1)
            pe.wait_ge(h1_ready, 1)
            for q in range(4):
                mm = nc.tensor.matmul(ps[3][:, q * P:(q + 1) * P], H1[:, q * P:(q + 1) * P],
                                      XB[:, 6 + q // 2, P:SEQ], start=True, stop=True)
            mm.then_inc(yoff_mm, 1)
            pe.wait_ge(ld_h0, 16)
            for s in range(NB):
                for q in range(4):
                    mm = nc.tensor.matmul(ps[6][:, q * 32 + s * NS:q * 32 + (s + 1) * NS],
                                          H0[:, s, q * P:(q + 1) * P],
                                          XB[:, 6 + q // 2, SEQ + s * NS:SEQ + (s + 1) * NS], start=True, stop=True)
            mm.then_inc(yoff_mm, 1)
            pe.wait_ge(bm_ready, 1)
            pe.wait_ge(h2_ready, 1)
            for s in range(NB):
                if s >= 3:
                    pe.wait_ge(sstate_kept, s - 2)
                for g in range(2):
                    mm = nc.tensor.matmul(ps[(7, 4, 5)[s % 3]][:, g * 256:(g + 1) * 256],
                                          BM[0:32, s, g * P:(g + 1) * P], DXE[0:32, 2, g * 256:(g + 1) * 256],
                                          start=True, stop=True)
                mm.then_inc(sstate_mm, 1)
            pe.wait_ge(sq_ready, 7)
            for g in range(2):
                for k in range(2):
                    mm = nc.tensor.matmul(ps[g][:, 0:T], ones, SQ[:, 2 * g + k, :], start=(k == 0), stop=(k == 1))
            mm.then_inc(sum_mm, 1)
            products_attention(pe)
            products_layer_out(pe, 0)
            products_conformer(pe)
            products_layer_out(pe, 1)

        @block.scalar
        def _(act):
            steps = Chain(act, act_step)
            act.wait_ge(ld_const, 32)
            act.wait_ge(zeroed, 1)
            for t, (t0, nt) in enumerate(TILES):
                act.wait_ge(tok_kept, 3)
                op = nc.scalar.activation(T1[0:nt, t, 0:R], TK[0:nt, t, 0:R], ACT.Square, accum_out=SS[0:nt, t:t + 1])
                op.then_inc(sq_ready, 1)
            for k in range(3):
                act.wait_ge(hq_kept, k + 1)
                nc.scalar.activation(SQ[:, k, :], HQ[:, k, :], ACT.Square).then_inc(sq_ready, 1)
            act.wait_ge(sq_ready, 3)
            nc.scalar.activation(RK, SS, ACT.Sqrt, bias=eps, scale=1.0 / R).then_inc(std_ready, 1)
            for n in range(4):
                act.wait_ge(piece_mm, 4 + n)
                nc.scalar.activation(ZT[:, n, :], ps[(3 + n) % 4][:, 0:T], ACT.Silu).then_inc(ch_kept, 1)
            for n in range(8):
                act.wait_ge(piece_mm, 8 + n)
                bank = ps[(7 + n) % 4]
                nc.scalar.copy(XP[:, n, 3:3 + SEQ], bank[:, 0:SEQ])
                nc.scalar.copy(XS[:, n, :, 3:7], bank[:, SEQ:T].rearrange("p (b s) -> p b s", s=NS)).then_inc(ch_kept, 1)
            act.wait_ge(sum_mm, 1)
            nc.scalar.activation(T1[:, 3, :], ps[7][:, 0:T], ACT.Sqrt, bias=eps, scale=1.0 / QL).then_inc(std_ready, 1)
            act.wait_ge(dt_z, 1)
            steps.step(nc.scalar.activation(T3, T3, ACT.Exp))
            nc.scalar.activation(NA, prm("a_log"), ACT.Exp)
            nc.scalar.activation(T3, T3, ACT.Ln, bias=1.0).then_inc(dt_ln, 1)
            for n in range(8):
                act.wait_ge(conv_ready, n + 1)
                op = nc.scalar.activation(XB[:, n, :], XB[:, n, :], ACT.Silu)
            op.then_inc(xb_ready, 1)
            act.wait_ge(acs_kept, 1)
            nc.scalar.activation(TOE[:, 0:16], TOE[:, 0:16], ACT.Exp)
            nc.scalar.activation(TOE[0:32, 16:24], TOE[0:32, 16:24], ACT.Exp)
            nc.scalar.activation(DEC, ACS[:, 16:96], ACT.Exp).then_inc(dec_ready, 1)
            for h in range(H):
                act.wait_ge(seg_ready, h + 1)
                lo = 64 * (h % 2)
                nc.scalar.activation(E[lo:lo + 64, h // 2, :], ps[h % 4][lo:lo + 64, 0:T], ACT.Exp).then_inc(e_ready, 1)
                nc.scalar.activation(L[:, h, 0:SEQ], L[:, h, 0:SEQ], ACT.Exp)
                nc.scalar.activation(L[0:32, h, SEQ:T], L[0:32, h, SEQ:T], ACT.Exp).then_inc(decay_ready, 1)
            for t, (t0, nt) in enumerate(TILES):
                act.wait_ge(bt_mm, t + 1)
                bank = ps[7] if t == 0 else ps[3 + t]
                nc.scalar.copy(BTOK[0:nt, t, :], bank[0:nt, 0:256]).then_inc(bt_kept, 1)
            act.wait_ge(state_mm, 1)
            nc.scalar.copy(H1, ps[4][:, :]).then_inc(h1_ready, 1)
            act.wait_ge(y_gated, 1)
            nc.scalar.activation(SQ, Y, ACT.Square).then_inc(sq_ready, 1)
            act.wait_ge(sum_mm, 2)
            for g in range(2):
                op = nc.scalar.activation(RG[:, g, :], ps[g][:, 0:T], ACT.Sqrt, bias=eps, scale=1.0 / 256)
            op.then_inc(std_ready, 1)
            act_attention(act, steps)
            act_layer_out(act, steps, 0)
            act_conformer(act, steps)
            act_layer_out(act, steps, 1)

        @block.vector
        def _(dve):
            steps = Chain(dve, dve_step)
            V = nc.vector
            dve.wait_ge(zeroed, 1)
            for t, (t0, nt) in enumerate(TILES):
                dve.wait_ge(tok_mm, t + 1)
                V.tensor_copy(TK[0:nt, t, :], ps[4 + t][0:nt, 0:296]).then_inc(tok_kept, 1)
            for k in range(3):
                dve.wait_ge(piece_mm, k + 1)
                V.tensor_copy(HQ[:, k, :], ps[k][:, 0:T]).then_inc(hq_kept, 1)
            dve.wait_ge(ld_const, 32)
            dve.wait_ge(tok_kept, 3)
            co = cst("cos").rearrange("p (t f) -> p t f", t=3)
            si = cst("sin").rearrange("p (t f) -> p t f", t=3)
            ka, kb = TK[:, :, 256:272], TK[:, :, 272:288]
            V.tensor_tensor(KPE[:, :, 0:16], ka, co, ALU.mult)
            V.tensor_tensor(KPE[:, :, 16:32], kb, co, ALU.mult)
            V.tensor_tensor(KT[:, :, 0:16], kb, si, ALU.mult)
            steps.step(V.tensor_tensor(KT[:, :, 16:32], ka, si, ALU.mult))
            V.tensor_tensor(KPE[:, :, 0:16], KPE[:, :, 0:16], KT[:, :, 0:16], ALU.subtract)
            steps.step(V.tensor_tensor(KPE[:, :, 16:32], KPE[:, :, 16:32], KT[:, :, 16:32], ALU.add))
            steps.step(V.tensor_tensor(TDT, TK[:, :, 288:296], prm("dt_bias").unsqueeze(1).to_broadcast([P, 3, 8]),
                                       ALU.add))
            V.scalar_tensor_tensor(T3, TDT, -1.0, TDT, ALU.mult, ALU.min).then_inc(dt_z, 1)
            dve.wait_ge(std_ready, 1)
            steps.step(V.reciprocal(RK, RK))
            for t, (t0, nt) in enumerate(TILES):
                op = V.scalar_tensor_tensor(CK[0:nt, t, :], TK[0:nt, t, 0:R], RK[0:nt, t:t + 1], prm("g_kv")[0:nt],
                                            ALU.mult, ALU.mult)
            op.then_inc(kv_ready, 1)
            dve.wait_ge(ld_hist, 16)
            cw = prm("conv_w").rearrange("p (c k) -> p c k", k=4)
            cb = prm("conv_b")
            for n in range(8):
                dve.wait_ge(ch_kept, 5 + n)
                xsv = CS[:, n, :].rearrange("p (b s) -> p b s", s=NS)
                V.tensor_scalar(XB[:, n, 0:SEQ], XP[:, n, 0:SEQ], cw[:, n, 0:1], cb[:, n:n + 1], ALU.mult, ALU.add)
                steps.step(V.tensor_scalar(xsv, XS[:, n, :, 0:4], cw[:, n, 0:1], cb[:, n:n + 1], ALU.mult, ALU.add))
                for k in range(1, 4):
                    V.scalar_tensor_tensor(XB[:, n, 0:SEQ], XP[:, n, k:k + SEQ], cw[:, n, k:k + 1], XB[:, n, 0:SEQ],
                                           ALU.mult, ALU.add)
                    dst = xsv if k < 3 else XB[:, n, SEQ:T].rearrange("p (b s) -> p b s", s=NS)
                    op = V.scalar_tensor_tensor(dst, XS[:, n, :, k:k + 4], cw[:, n, k:k + 1], xsv, ALU.mult, ALU.add)
                    steps.step(op) if k < 3 else op.then_inc(conv_ready, 1)
                if n == 1:
                    dve.wait_ge(dt_ln, 1)
                    steps.step(V.scalar_tensor_tensor(DT, TDT, 0.0, T3, ALU.max, ALU.add))
                    steps.step(V.tensor_tensor(DTA, DT, NA.unsqueeze(1).to_broadcast([P, 3, 8]), ALU.mult))
                    steps.step(V.tensor_scalar(DTA, DTA, -1.0, None, ALU.mult))
                    V.tensor_tensor(DTAM[0:32], DTA[0:32, 2, :].unsqueeze(1).to_broadcast([32, NB, 8]),
                                    cst("bmask", 32).unsqueeze(2).to_broadcast([32, NB, 8]), ALU.mult).then_inc(dtA_ready, 1)
                if n == 3:
                    dve.wait_ge(std_ready, 2)
                    steps.step(V.reciprocal(T1[:, 3, :], T1[:, 3, :]))
                    for k in range(3):
                        op = V.scalar_tensor_tensor(HQ[:, k, :], HQ[:, k, :], prm("g_q")[:, k:k + 1], T1[:, 3, :],
                                                    ALU.mult, ALU.mult)
                    op.then_inc(hq_ready, 1)
                if n == 5:
                    dve.wait_ge(kvT_mm, 1)
                    for r in range(2):
                        V.tensor_copy(CKT[:, r, :], ps[4 + r][:, 0:T])
                    V.tensor_copy(KPT[0:32], ps[6][0:32, 0:T]).then_inc(kvT_kept, 1)
            dve.wait_ge(acs_mm, 1)
            V.tensor_copy(ACS[:, 0:96], ps[7][:, 0:96])
            steps.step(V.tensor_copy(ACS[0:32, 96:112], ps[7][0:32, 96:112]))
            V.tensor_tensor(TOE[:, 0:16], ACS[:, 16:32], ACS[:, 0:16], ALU.subtract)
            V.tensor_tensor(TOE[0:32, 16:24], ACS[0:32, 104:112], ACS[0:32, 96:104], ALU.subtract).then_inc(acs_kept, 1)
            for h in range(H):
                dve.wait_ge(row_mm, h + 1)
                for c in range(2):
                    V.scalar_tensor_tensor(L[:, h, c * P:(c + 1) * P], ps[h % 4][:, c * P:(c + 1) * P],
                                           ACS[:, 8 * c + h:8 * c + h + 1], cst("mask_ssd"), ALU.subtract, ALU.add)
                V.scalar_tensor_tensor(L[0:32, h, SEQ:T], ps[h % 4][0:32, SEQ:T], ACS[0:32, 96 + h:97 + h],
                                       cst("mask_ssd_s", 32), ALU.subtract, ALU.add).then_inc(seg_ready, 1)
            dve.wait_ge(dec_ready, 1)
            for t, (t0, nt) in enumerate(TILES):
                dve.wait_ge(xs_mm, t + 1)
                dxv = DX[0:nt, t, :].rearrange("p (h d) -> p h d", h=H)
                steps.step(V.tensor_tensor(dxv, ps[4 + t][0:nt, :].rearrange("p (h d) -> p h d", h=H),
                                           DT[0:nt, t, :].unsqueeze(2).to_broadcast([nt, H, 64]), ALU.mult))
                V.tensor_tensor(DXE[0:nt, t, :].rearrange("p (h d) -> p h d", h=H), dxv,
                                TOE[0:nt, 8 * t:8 * t + 8].unsqueeze(2).to_broadcast([nt, H, 64]),
                                ALU.mult).then_inc(dx_ready, 1)
            dve.wait_ge(decay_ready, H)
            for g in range(2):
                dve.wait_ge(cb_mm, g + 1)
                for c, (t0, nt) in enumerate(TILES):
                    lv = L[0:nt, 4 * g:4 * g + 4, t0:t0 + nt]
                    op = V.tensor_tensor(lv, lv, ps[6 + g][0:nt, t0:t0 + nt].unsqueeze(1).to_broadcast([nt, 4, nt]), ALU.mult)
                op.then_inc(m_ready, 1)
            for q in range(4):
                op = V.tensor_scalar(Y[:, q, :], XB[:, q, :], prm("d_skip")[:, q:q + 1], None, ALU.mult)
            steps.step(op)
            for c, (t0, nt) in enumerate(TILES):
                dve.wait_ge(ydiag_mm, c + 1)
                yv = Y[:, :, t0:t0 + nt]
                op = V.tensor_tensor(yv, yv, ps[c][:, 0:4 * nt].rearrange("p (q t) -> p q t", q=4), ALU.add)
            steps.step(op)
            for c, bank in ((1, 3), (2, 6)):
                t0, nt = TILES[c]
                dve.wait_ge(yoff_mm, c)
                dve.wait_ge(e_ready, H)
                steps.step(V.tensor_tensor(T1[:, :, t0:t0 + nt], E[:, :, t0:t0 + nt],
                                           ps[bank][:, 0:4 * nt].rearrange("p (q t) -> p q t", q=4), ALU.mult))
                steps.step(V.tensor_tensor(Y[:, :, t0:t0 + nt], Y[:, :, t0:t0 + nt], T1[:, :, t0:t0 + nt], ALU.add))
            V.tensor_tensor(Y, Y, ZT, ALU.mult).then_inc(y_gated, 1)
            dve.wait_ge(h1_ready, 1)
            dve.wait_ge(state_mm, 2)
            h2v = H2.rearrange("p (h d) -> p h d", h=H)
            steps.step(V.tensor_tensor(h2v, H1.rearrange("p (h d) -> p h d", h=H),
                                       DEC[:, 8:16].unsqueeze(2).to_broadcast([P, H, 64]), ALU.mult))
            V.tensor_tensor(H2, H2, ps[5][:, :], ALU.add).then_inc(h2_ready, 1)
            h0v = H0.rearrange("p b (h d) -> p (b h) d", d=64)
            steps.step(V.tensor_tensor(h0v, h0v, DEC[:, 16:80].unsqueeze(2).to_broadcast([P, 64, 64]), ALU.mult))
            for s in range(NB):
                dve.wait_ge(sstate_mm, s + 1)
                V.tensor_tensor(H0[:, s, :], H0[:, s, :], ps[(7, 4, 5)[s % 3]][:, :], ALU.add).then_inc(sstate_kept, 1)
            dve.wait_ge(std_ready, 3)
            steps.step(V.reciprocal(RG, RG))
            for q in range(4):
                op = V.scalar_tensor_tensor(CAT[:, 4 + q, :], Y[:, q, :], prm("g_y")[:, q:q + 1], RG[:, q // 2, :],
                                            ALU.mult, ALU.mult)
            op.then_inc(y_ready, 1)
            dve_attention(dve, steps)
            dve_layer_out(dve, steps, 0)
            dve_conformer(dve, steps)
            dve_layer_out(dve, steps, 1)

        @block.gpsimd
        def _(pool):
            G = nc.gpsimd
            G.memset(XS[:], 0.0)
            G.memset(XP[:, :, 0:3], 0.0)
            G.memset(SS, 1.0)
            G.memset(X[:, 2, :], 0.0)
            G.memset(TK[:, 2, :], 0.0).then_inc(zeroed, 1)

            pool.dma_start(pages[0:1, :], a["pages"]).then_inc(ld_pages, 16)

            def store(dst, src, done=None):
                if done is None:
                    n_stored[0] += 1
                pool.dma_start(dst, src).then_inc(stored if done is None else done, 16)

            pool.wait_ge(kv_ready, 1)
            for t in range(2):
                store(o["ckv_p"][t * P:(t + 1) * P], CK[:, t, :], ckv_stored)
                store(o["kpe_p"][t * P:(t + 1) * P], KPE[:, t, :])
            store(o["ckv_s"], CK[0:32, 2, :], ckv_stored)
            store(o["kpe_s"], KPE[0:32, 2, :])
            pool.wait_ge(ch_kept, 12)
            pool.wait_ge(ld_hist, 16)
            store(o["sconv_p"], XP[:, :, SEQ:SEQ + 3], conv_stored)
            store(o["sconv_s"], XS[:, :, :, 4:7], conv_stored)
            pool.wait_ge(bt_kept, 3)
            G.tensor_tensor(BM[0:32], BTOK[0:32, 2, :].unsqueeze(1).to_broadcast([32, NB, 256]),
                            cst("bmask", 32).unsqueeze(2).to_broadcast([32, NB, 256]), ALU.mult).then_inc(bm_ready, 1)
            pool.wait_ge(h2_ready, 1)
            store(o["ssm_p"], H2, h2_stored)
            pool.wait_ge(sstate_kept, NB)
            store(o["ssm_s"], H0, h0_stored)
            pool_attention(pool, store)
            pool_layer_out(pool, store, 0)
            pool_conformer(pool, store)
            pool_layer_out(pool, store, 1)
            pool.wait_ge(stored, 16 * n_stored[0])
            pool.wait_ge(ckv_stored, 48)
            pool.wait_ge(conv_stored, 32)
            pool.wait_ge(h2_stored, 16)
            pool.wait_ge(h0_stored, 16)
            pool.wait_ge(cconv_stored, 32)


INPUTS = [("x", (T, D)), ("xT", (P, KC, T)), ("w_tok", (P, KC, 296)), ("w_ch", (15, P, KC, P)), ("consts", (P, NCONST)),
          ("params", (P, NPARAM)), ("conv_hist", (P, KC, NB, 3)), ("w_q", (P, 4352)), ("state", (P, NB, 512)),
          ("cacheT", (160, P, 2, P)), ("kpeT", (160, E_PE, P)), ("cache", (160, P, R)), ("pages", (1, NB * NP)),
          ("w_out", (P, KC, D)), ("rows", (5, P, D)), ("rows_b", (4, P, D)), ("w_moe", (2, NE, P, 6144)),
          ("w_conf", (16, P, KC, P)), ("conf_hist", (P, KC, NB, HIST)), ("w_conf_out", (P, KC, D)),
          ("nobody", (SLOT_ROWS, 1)), ("token_ids", (P, 3))]
OUTPUTS = [("y", (T, D)), ("ckv_p", (SEQ, R)), ("kpe_p", (SEQ, E_PE)), ("ssm_p", (P, 512)), ("sconv_p", (P, KC, 3)),
           ("cconv_p", (P, KC, HIST)), ("ckv_s", (32, R)), ("kpe_s", (32, E_PE)), ("ssm_s", (P, NB, 512)),
           ("sconv_s", (P, KC, NB, 3)), ("cconv_s", (P, KC, NB, HIST))]
INT_INPUTS = ("pages", "nobody", "token_ids")


def lay_out(v):
    f = np.ascontiguousarray
    chunks = lambda w: f(w.reshape(-1, P, w.shape[-1]).transpose(1, 0, 2))
    cols = lambda x: f(x.reshape(-1, P).T)
    bcast = lambda x: np.broadcast_to(x, (P,) + x.shape)
    w = v["w_in_ab"][0]
    x = np.concatenate([v["x_prompt"][0], v["x_sample"].reshape(32, D)])
    d = {"x": x, "xT": chunks(f(x.T)), "consts": constants()}
    d["w_tok"] = chunks(np.concatenate([w[:, 384:672], w[:, 2208:2216]], axis=1))
    w_ch = np.concatenate([w[:, 0:384], w[:, 672:2208]], axis=1)
    pieces = lambda m: f(m.reshape(KC, P, -1, P).transpose(2, 1, 0, 3))
    d["w_ch"] = pieces(w_ch)
    uq = v["w_uq"][0]
    uqn = chunks(f(uq[:, :, :64].reshape(QL, 512))).reshape(P, -1)
    uqp = chunks(f(uq[:, :, 64:].reshape(QL, 256))).reshape(P, -1)
    uk = f(v["w_uk"][0].transpose(1, 2, 0).reshape(4, P, R).transpose(1, 0, 2)).reshape(P, -1)
    uv = chunks(v["w_uv"][0].reshape(R, 512)).reshape(P, -1)
    d["w_q"] = np.concatenate([uqn, uqp, uk, uv], axis=1)
    d["conv_hist"] = f(v["state_ssm_conv"][0].reshape(NB, 3, KC, P).transpose(3, 2, 0, 1))
    d["state"] = f(v["state_ssm"][0].transpose(3, 0, 1, 2).reshape(P, NB, 512))
    d["cacheT"] = f(v["cache_ckv"][0].reshape(-1, P, 2, P).transpose(0, 3, 2, 1))
    d["kpeT"] = f(v["cache_kpe"][0].transpose(0, 2, 1))
    d["cache"] = v["cache_ckv"][0]
    d["pages"] = v["page_table"].reshape(1, NB * NP)
    d["w_out"] = chunks(v["w_out_ab"][0])
    d["rows"] = np.stack([bcast(r) for r in (v["ln_mix_g"][0], v["ln_ffn_g"][0], v["ln_mix_g"][1], v["ln_ffn_g"][1],
                                             v["conf_b_out"][0])])
    d["rows_b"] = np.stack([bcast(r) for r in (v["ln_mix_b"][0], v["ln_ffn_b"][0], v["ln_mix_b"][1], v["ln_ffn_b"][1])])
    halves = lambda m: m.reshape(2, NE, KC, P, 2, 1, P)
    gu = np.concatenate([halves(v["moe_w_gate"]), halves(v["moe_w_up"])], axis=5)
    gu = gu.transpose(0, 1, 3, 2, 4, 5, 6).reshape(2, NE, P, 4096)
    down = v["moe_w_down"].reshape(2, NE, 2, P, D).transpose(0, 1, 3, 2, 4).reshape(2, NE, P, 2048)
    d["w_moe"] = np.concatenate([gu, down], axis=3)
    d["w_conf"] = pieces(v["conf_w_in"][0])
    d["conf_hist"] = f(v["state_conf_conv"][0].reshape(NB, HIST, KC, P).transpose(3, 2, 0, 1))
    d["w_conf_out"] = chunks(v["conf_w_out"][0])
    d["nobody"] = np.full((SLOT_ROWS, 1), NOBODY, np.int32)
    ids = np.arange(3 * P, dtype=np.int32).reshape(3, P).T
    d["token_ids"] = f(ids)
    taps = lambda x: f(x.T.reshape(KC, P, -1).transpose(1, 0, 2)).reshape(P, -1)
    parts = {"g_q": cols(v["g_q_norm"][0]), "conv_w": taps(v["ssm_conv_w"][0]), "conv_b": cols(v["ssm_conv_b"][0]),
             "g_y": cols(v["ssm_norm_g"][0]), "d_skip": cols(np.repeat(v["ssm_d"][0], 64)),
             "dt_bias": bcast(v["ssm_dt_bias"][0]), "a_log": bcast(v["ssm_a_log"][0]), "b_in": cols(v["conf_b_in"][0]),
             "dw_w": taps(v["conf_dw_w"][0]), "dw_b": cols(v["conf_dw_b"][0]), "gn": cols(v["conf_norm_g"][0]),
             "bn": cols(v["conf_norm_b"][0]), "r_bias": bcast(v["router_bias"]),
             "w_router": chunks(v["w_router"]).reshape(P, -1), "g_kv": bcast(v["g_kv_norm"][0])}
    d["params"] = np.concatenate([parts[name] for name in PARAM], axis=1)
    return d


def kernel(**inputs):
    from concourse import bacc
    from concourse.bass_utils import run_bass_kernel_spmd

    nc = bacc.Bacc("TRN2", target_bir_lowering=False, num_devices=1)
    laid = lay_out({k: np.asarray(x) for k, x in inputs.items()})
    arrays, a, o = {}, {}, {}
    for name, shape in INPUTS:
        arrays[f"in_{name}"] = np.ascontiguousarray(laid[name].reshape(shape))
        dt = I32 if name in INT_INPUTS else F32
        a[name] = nc.dram_tensor(f"in_{name}", shape, dt, kind="ExternalInput").ap()
    for name, shape in OUTPUTS:
        o[name] = nc.dram_tensor(f"out_{name}", shape, F32, kind="ExternalOutput").ap()
    hybrid_trunk(nc, a, o)
    res = run_bass_kernel_spmd(nc, [arrays], core_ids=[0]).results[0]
    r = {name: np.asarray(res[f"out_{name}"]) for name, _ in OUTPUTS}
    rows = lambda x: x.transpose(2, 1, 0).reshape(1, 1, x.shape[2], -1)
    srows = lambda x: x.transpose(2, 3, 1, 0).reshape(1, NB, x.shape[3], -1)
    return (r["y"][:SEQ].reshape(1, SEQ, D), r["y"][SEQ:].reshape(NB, NS, D),
            r["ckv_p"].reshape(1, 1, SEQ, R), r["kpe_p"].reshape(1, 1, SEQ, E_PE),
            r["ssm_p"].reshape(P, 8, 64).transpose(1, 2, 0).reshape(1, 1, 8, 64, P), rows(r["sconv_p"]),
            rows(r["cconv_p"]), r["ckv_s"].reshape(1, NB, NS, R), r["kpe_s"].reshape(1, NB, NS, E_PE),
            r["ssm_s"].reshape(P, NB, 8, 64).transpose(1, 2, 3, 0).reshape(1, NB, 8, 64, P),
            srows(r["sconv_s"]), srows(r["cconv_s"]))
```

```python
from contextlib import ExitStack

import numpy as np

import concourse.bass as bass
from concourse import mybir

F32 = mybir.dt.float32
I32 = mybir.dt.int32
ALU = mybir.AluOpType
ACT = mybir.ActivationFunctionType
AX = mybir.AxisListType.X

P = 128
D = 1024
KC = D // P
SEQ = 256
NB, NS = 8, 4
T = SEQ + NB * NS
TILES = ((0, 128), (128, 128), (256, 32))
H = 8
QL, R, E_PE, VD = 384, 256, 32, 64
NSTATE = 128
NP = 16
NEG = -1.0e30
EPS = 1e-6
ALPHA = 4.0 ** 0.25
SCALE = 96.0 ** -0.5
NE = 16
CAP = 64
MAX_EXTRA = 8
SLOT_ROWS = (NE + MAX_EXTRA) * CAP
NOBODY = 1 << 20
KW = 31
HIST = KW - 1


def const_layout():
    widths = [("ident", P), ("ones", P), ("tri", P), ("tri_strict", P), ("mask_ssd", P), ("mask_q", P),
              ("tri_s", 32), ("blk_s", 32), ("mask_ssd_s", 32), ("bmask", NB), ("mask_new", 64),
              ("cos", 48), ("sin", 48), ("row_of", NE), ("prio16", NE), ("prio4", 4), ("valid", 3),
              ("eps", 1), ("item_thr", 64), ("item_k", MAX_EXTRA)]
    at, cols = 0, {}
    for name, w in widths:
        cols[name] = (at, at + w)
        at += w
    return cols, at


CONST, NCONST = const_layout()


def constants():
    c = np.zeros((P, NCONST), np.float32)
    i = np.arange(P)

    def put(name, value):
        a, b = CONST[name]
        value = np.asarray(value, np.float32)
        c[:value.shape[0], a:b] = value.reshape(value.shape[0], b - a)

    put("ident", np.eye(P))
    put("ones", np.ones((P, P)))
    put("tri", i[:, None] <= i[None, :])
    put("tri_strict", i[:, None] < i[None, :])
    put("mask_ssd", np.where(i[:, None] <= i[None, :], 0.0, NEG))
    put("mask_q", np.where(i[None, :] <= i[:, None], 0.0, NEG))
    k = np.arange(32)
    same = (k[:, None] // NS) == (k[None, :] // NS)
    put("tri_s", same & (k[:, None] <= k[None, :]))
    put("blk_s", same)
    put("mask_ssd_s", np.where(same & (k[:, None] <= k[None, :]), 0.0, NEG))
    put("bmask", (k[:, None] // NS) == np.arange(NB)[None, :])
    row_b, row_s = i // 32, i % NS
    new = np.zeros((P, 2, 32), np.float32)
    for g in range(2):
        ok = ((k[None, :] // NS) == (4 * g + row_b[:, None])) & ((k[None, :] % NS) <= row_s[:, None])
        new[:, g] = np.where(ok, 0.0, NEG)
    put("mask_new", new)
    pos = np.zeros((P, 3))
    pos[:, 0], pos[:, 1] = i, i + P
    pos[:32, 2] = NP * P + k % NS
    inv = np.float32(10000.0) ** (-np.arange(16, dtype=np.float32) / np.float32(16))
    ang = pos.astype(np.float32)[:, :, None] * inv[None, None, :]
    put("cos", np.cos(ang))
    put("sin", np.sin(ang))
    put("row_of", np.broadcast_to(np.arange(NE) * CAP, (P, NE)))
    put("prio16", np.broadcast_to(NE - np.arange(NE), (P, NE)))
    put("prio4", np.broadcast_to(4 - np.arange(4), (P, 4)))
    valid = np.ones((P, 3))
    valid[32:, 2] = 0
    put("valid", valid)
    put("eps", np.full((P, 1), EPS))
    put("item_thr", np.broadcast_to(np.tile(np.arange(1, 5) * CAP, NE), (P, 64)))
    put("item_k", np.broadcast_to(np.arange(MAX_EXTRA), (P, MAX_EXTRA)))
    return c


def param_layout():
    widths = [("g_q", 3), ("conv_w", 32), ("conv_b", 8), ("g_y", 4), ("d_skip", 4), ("dt_bias", 8),
              ("a_log", 8), ("b_in", 16), ("dw_w", 8 * KW), ("dw_b", 8), ("gn", 8), ("bn", 8),
              ("r_bias", NE), ("w_router", KC * NE), ("g_kv", R)]
    at, cols = 0, {}
    for name, w in widths:
        cols[name] = (at, at + w)
        at += w
    return cols, at


PARAM, NPARAM = param_layout()


class Chain:

    def __init__(self, engine, sem):
        self.engine, self.sem, self.count = engine, sem, 0

    def step(self, instruction):
        self.count += 1
        instruction.then_inc(self.sem, 1)
        self.engine.wait_ge(self.sem, self.count)


def hybrid_trunk(nc, a, o):
    ctx = ExitStack()
    with ctx:
        def sb(name, cols, dt=F32):
            return ctx.enter_context(nc.sbuf_tensor(name, [P, cols], dt))

        def sem(name):
            return ctx.enter_context(nc.semaphore(name))

        ps = [ctx.enter_context(nc.psum_tensor(f"bank{i}", [P, 512], F32)) for i in range(8)]
        X = sb("x_tok", 3 * D)[:].rearrange("p (t d) -> p t d", t=3)
        xT_t = sb("x_ch", KC * T)
        XT = xT_t[:].rearrange("p (c t) -> p c t", c=KC)
        ROWS = sb("rows", 2 * D)[:].rearrange("p (r d) -> p r d", r=2)
        C = sb("consts", NCONST)
        PM = sb("params", NPARAM)
        slot_t = sb("slots", 3 * 6144)
        M = sb("mixer", 24472)
        small = sb("small", 640)
        ints = sb("ints", 64, I32)

        def cst(name, rows=P):
            lo, hi = CONST[name]
            return C[0:rows, lo:hi]

        def prm(name):
            lo, hi = PARAM[name]
            return PM[:, lo:hi]

        def at(t, off, *dims):
            n = int(np.prod(dims))
            v = t[:, off:off + n]
            if len(dims) == 1:
                return v
            names = "abcd"[:len(dims)]
            return v.rearrange(f"p ({' '.join(names)}) -> p {' '.join(names)}", **dict(zip(names[1:], dims[1:])))

        ident, ones = cst("ident"), cst("ones")

        WUQN = at(slot_t, 0, 3, 4, P)
        WUQP = at(slot_t, 1536, 3, 256)
        WUK = at(slot_t, 2304, 4, R)
        WUV = at(slot_t, 3328, 2, H * VD)
        CK = at(slot_t, 4352, 3, R)
        CKT = at(slot_t, 5120, 2, T)
        KPT = at(slot_t, 5696, T)
        S1 = 6144
        DX = at(slot_t, S1, 3, 512)
        DXE = at(slot_t, S1 + 1536, 3, 512)
        BTOK = at(slot_t, S1 + 3072, 3, 256)
        BM = at(slot_t, S1 + 3840, NB, 256)
        L = at(slot_t, S1 + 5888, H, T)
        E = at(slot_t, S1 + 8192, 4, T)
        H1 = at(slot_t, S1 + 9344, 512)
        H2 = at(slot_t, S1 + 9856, 512)
        Y = at(slot_t, S1 + 10368, 4, T)
        RG = at(slot_t, S1 + 11520, 2, T)
        WIN = at(M, 0, 4, KC, P)
        WTOK = at(M, 4096, KC, 296)
        H0 = at(M, 0, NB, 512)
        T1 = at(M, 4096, 4, T)
        SQ = at(M, 5248, 4, T)
        TK = at(M, 6464, 3, 296)
        HQ = at(M, 7352, 3, T)
        CAT = at(M, 8216, KC, T)
        QN = at(M, 10520, 4, T)
        QA = at(M, 11672, 2, H, T)
        XP = at(M, 16280, KC, 3 + SEQ)
        XS = at(M, 18352, KC, NB, 7)
        XB = at(M, 18800, KC, T)
        ZT = at(M, 21104, 4, T)
        CS = at(M, 22256, KC, NB * NS)
        QPT = at(M, 22512, 3, 256)
        TMP = at(M, 23280, 4, 128)
        WOUT = at(M, 16280, KC, D)
        QP = at(xT_t, 0, H, T)
        S = at(M, 0, 2080)
        PT = at(M, 2080, NP, P)
        PNT = at(M, 4128, P)
        OS = at(M, 4256, R)
        PP = at(M, 4512, 2, 384)
        PPT = at(M, 5280, 2, 384)

        SS, RK, TDT = small[:, 0:3], small[:, 3:6], at(small, 8, 3, 8)
        DT, DTA, T3 = at(small, 32, 3, 8), at(small, 56, 3, 8), at(small, 80, 3, 8)
        NA = small[:, 104:112]
        ACS, TOE, DEC = small[:, 112:224], small[:, 224:248], small[:, 248:328]
        DTAM = at(small, 328, NB, 8)
        KPE = at(small, 392, 3, 32)
        KT = at(small, 488, 3, 32)
        BST, MV, RST = at(small, 584, 2, 6), small[:, 596:598], small[:, 598:600]
        MXP, RSP = at(small, 600, 2, 4), at(small, 608, 2, 4)
        MXS, RSS = small[:, 616:620], small[:, 620:624]

        ld_const, ld_x, ld_xT, ld_wtok, ld_wq, ld_hist = map(sem, (
            "ld_const", "ld_x", "ld_xT", "ld_wtok", "ld_wq", "ld_hist"))
        ld_h0, ld_wout, ld_rows = map(sem, ("ld_h0", "ld_wout", "ld_rows"))
        ring_ld = [sem(f"ring_ld{i}") for i in range(4)]
        zeroed, tok_mm, tok_kept, piece_mm, hq_kept, ch_kept = map(sem, (
            "zeroed", "tok_mm", "tok_kept", "piece_mm", "hq_kept", "ch_kept"))
        sq_ready, sum_mm, std_ready, hq_ready, kv_ready, kvT_mm, kvT_kept = map(sem, (
            "sq_ready", "sum_mm", "std_ready", "hq_ready", "kv_ready", "kvT_mm", "kvT_kept"))
        conv_ready, xb_ready, dt_z, dt_ln, dtA_ready = map(sem, (
            "conv_ready", "xb_ready", "dt_z", "dt_ln", "dtA_ready"))
        acs_kept, row_mm, seg_ready, decay_ready, e_ready = map(sem, (
            "acs_kept", "row_mm", "seg_ready", "decay_ready", "e_ready"))
        xs_mm, dx_ready, bt_mm, bt_kept, bm_ready, cb_mm, m_ready = map(sem, (
            "xs_mm", "dx_ready", "bt_mm", "bt_kept", "bm_ready", "cb_mm", "m_ready"))
        ydiag_mm, state_mm, h1_ready, yoff_mm, h2_ready, sstate_mm, sstate_kept = map(sem, (
            "ydiag_mm", "state_mm", "h1_ready", "yoff_mm", "h2_ready", "sstate_mm", "sstate_kept"))
        y_gated, y_ready = map(sem, ("y_gated", "y_ready"))
        stored = sem("stored")
        dve_step, act_step, pool_step = map(sem, ("dve_step", "act_step", "pool_step"))
        n_stored = [0]

        eps = cst("eps")

        qn_mm, q_kept, kvT_act, qa_mm, qa_act, qa_dve, qpT_mm, qpT_kept = map(sem, (
            "qn_mm", "q_kept", "kvT_act", "qa_mm", "qa_act", "qa_dve", "qpT_mm", "qpT_kept"))
        pscore_mm, pmax_ready, pexp_ready, prob_ready, probT_mm, probT_kept, po_mm, po_kept = map(sem, (
            "pscore_mm", "pmax_ready", "pexp_ready", "prob_ready", "probT_mm", "probT_kept", "po_mm",
            "po_kept"))
        s_mm, s_kept, s_new, s_max, s_exp, sT_mm, sT_kept, so_mm, so_kept, soT_mm, soT_kept = map(sem, (
            "s_mm", "s_kept", "s_new", "s_max", "s_exp", "sT_mm", "sT_kept", "so_mm", "so_kept", "soT_mm", "soT_kept"))
        slot_ld = [sem(f"slot_ld{n}") for n in range(6)]
        kv_ld = ring_ld + slot_ld[0:4]
        v_used, omla_mm, cat_kept, h2_stored, h0_stored, ckv_stored, conv_stored, ld_pages = map(sem, (
            "v_used", "omla_mm", "cat_kept", "h2_stored", "h0_stored", "ckv_stored", "conv_stored", "ld_pages"))
        QAS = at(M, 6464, 2, NB, 32)
        QPS = at(M, 6976, NB, 32)
        pages = sb("pages", NB * NP, I32)

        NCH, ROW = 8, R + E_PE
        PAGES = [at(slot_t, 6144 + n * 8 * ROW, 4, 2, ROW) for n in range(5)] + [
            at(M, 16280 + n * 8 * ROW, 4, 2, ROW) for n in range(3)]
        V_ORDER = ((0, 1, 2, 3, 4, 5, 6, 7), (5, 6, 7, 0, 1, 2, 3, 4))
        KTR = [at(slot_t, 0, 4, 2, 256), ROWS.rearrange("p a (b t) -> p (a b) t", t=256).rearrange("p (j r) t -> p j r t", r=2)]
        KTE = [at(M, 23192, 2, 512), at(M, 10520, 2, 512)]

        def chunk_loaded(g, c):
            before_ = 16 * len(range(c, 15, 4)) if c < 4 else 0
            return before_ + 128 * (g + 1)

        def loads_attention(sp):
            sp.wait_ge(ld_pages, 16)
            sp.wait_ge(y_ready, 1)
            sp.wait_ge(sstate_kept, NB)
            sp.wait_ge(h2_stored, 16)
            for g in range(2):
                for c in range(NCH):
                    if g == 0 and c == 5:
                        sp.wait_ge(conv_stored, 32)
                        sp.wait_ge(qpT_mm, 5)
                    if g == 1:
                        sp.wait_ge(v_used, c + 1)
                    for half_ in range(2):
                        lo = (g * NCH + c) * 8 + 4 * half_
                        _, page = nc.values_load_multi_w_load_instructions(
                            pages[0:1, lo:lo + 4], engines=[mybir.EngineType.SP], min_val=0, max_val=159)
                        for n in range(4):
                            sp.dma_start(PAGES[c][:, 2 * half_ + n // 2, n % 2, :],
                                         a["cache"][bass.ds(page[n], 1)].rearrange("a p r -> (a p) r")
                                         ).then_inc(kv_ld[c], 16)
            sp.wait_ge(v_used, NCH + 3)
            sp.dma_start(ROWS[:, 0, :], a["rows"][0]).then_inc(ld_rows, 16)
            sp.dma_start(ROWS[:, 1, :], a["rows_b"][0]).then_inc(ld_rows, 16)
            sp.dma_start(WOUT, a["w_out"]).then_inc(ld_wout, 16)

        def products_attention(pe):
            pe.wait_ge(hq_ready, 1)
            pe.wait_ge(ld_wq, 16)
            pe.wait_ge(std_ready, 3)
            pe.wait_ge(sstate_kept, NB)
            for n in range(4):
                for k in range(3):
                    mm = nc.tensor.matmul(ps[n][:, 0:T], WUQN[:, k, n, :], HQ[:, k, :], start=(k == 0), stop=(k == 2))
                mm.then_inc(qn_mm, 1)
            for t, (t0, nt) in enumerate(TILES):
                for k in range(3):
                    mm = nc.tensor.matmul(ps[4 + t][0:nt, 0:256], HQ[:, k, t0:t0 + nt], WUQP[:, k, :],
                                          start=(k == 0), stop=(k == 2))
                mm.then_inc(qn_mm, 1)
            for h in range(H):
                lo = 64 * (h % 2)
                for r in range(2):
                    n = 2 * h + r
                    if n < 4:
                        pe.wait_ge(q_kept, 4)
                    elif n < 7:
                        pe.wait_ge(q_kept, n + 1)
                    elif n >= 8:
                        pe.wait_ge(qa_dve if r else qa_act, h - 3)
                    nc.tensor.matmul(ps[n % 8][:, 0:T], WUK[lo:lo + 64, h // 2, r * P:(r + 1) * P],
                                     QN[lo:lo + 64, h // 2, :], start=True, stop=True).then_inc(qa_mm, 1)
            pe.wait_ge(qa_act, 8)
            pe.wait_ge(qa_dve, 8)
            for n, (t, h0, nh) in enumerate(((0, 0, 4), (0, 4, 4), (1, 0, 4), (1, 4, 4), (2, 0, 8))):
                t0, nt = TILES[t]
                for h in range(nh):
                    mm = nc.tensor.transpose(ps[n][0:32, h * nt:(h + 1) * nt],
                                             QPT[0:nt, t, (h0 + h) * 32:(h0 + h + 1) * 32], ident[0:nt, 0:nt])
                mm.then_inc(qpT_mm, 1)
            pe.wait_ge(qpT_kept, 5)

            def prompt_scores(h):
                b = ps[h % 2]
                if h >= 2:
                    pe.wait_ge(pexp_ready, h - 1)
                for lo, q0, n in ((0, 0, P), (P, P, SEQ)):
                    for r in range(2):
                        nc.tensor.matmul(b[:, lo:lo + n], QA[:, r, h, q0:q0 + P], CKT[:, r, 0:n],
                                         start=(r == 0), stop=False, skip_group_check=True)
                    nc.tensor.matmul(b[:, lo + n - P:lo + n], ident, cst("mask_q"), start=False, stop=False,
                                     skip_group_check=True)
                    mm = nc.tensor.matmul(b[:, lo:lo + n], QP[0:32, h, q0:q0 + P], KPT[0:32, 0:n],
                                          start=False, stop=True, skip_group_check=True)
                mm.then_inc(pscore_mm, 1)

            def prompt_values(h):
                i = h % 2
                pe.wait_ge(prob_ready, h + 1)
                if h >= 2:
                    pe.wait_ge(probT_kept, h - 1)
                for n in range(3):
                    mm = nc.tensor.transpose(ps[2 + i][:, n * P:(n + 1) * P], PP[:, i, n * P:(n + 1) * P], ident)
                mm.then_inc(probT_mm, 1)
                pe.wait_ge(probT_kept, h + 1)
                if h >= 2:
                    pe.wait_ge(po_kept, h - 1)
                for r in range(2):
                    cr = slice(r * P, (r + 1) * P)
                    nc.tensor.matmul(ps[4 + i][:, r * SEQ:(r + 1) * SEQ], CK[:, 0, cr], PPT[:, i, 0:SEQ],
                                     start=True, stop=False, skip_group_check=True)
                    mm = nc.tensor.matmul(ps[4 + i][:, r * SEQ + P:(r + 1) * SEQ], CK[:, 1, cr], PPT[:, i, SEQ:384],
                                          start=False, stop=True, skip_group_check=True)
                mm.then_inc(po_mm, 1)

            def prompt_attention():
                pe.wait_ge(so_kept, 1)
                pe.wait_ge(soT_kept, 1)
                prompt_scores(0)
                prompt_scores(1)
                for h in range(H):
                    if h + 2 < H:
                        prompt_scores(h + 2)
                    prompt_values(h)
                pe.wait_ge(po_kept, H)
                pe.wait_ge(probT_kept, H)

            def key_transposes(g, c):
                n = NCH * g + c
                pe.wait_ge(kv_ld[c], chunk_loaded(g, c))
                if n:
                    pe.wait_ge(kvT_act, n)
                    pe.wait_ge(kvT_kept, n + 1)
                for j in range(4):
                    for pg in range(2):
                        for r in range(2):
                            nc.tensor.transpose(ps[j][:, r * 256 + pg * P:r * 256 + (pg + 1) * P],
                                                PAGES[c][:, j, pg, r * P:(r + 1) * P], ident)
                        mm = nc.tensor.transpose(ps[4 + j // 2][0:32, (j % 2 * 2 + pg) * P:(j % 2 * 2 + pg + 1) * P],
                                                 PAGES[c][:, j, pg, R:ROW], ident)
                mm.then_inc(kvT_mm, 1)

            for g in range(2):
                key_transposes(g, 0)
                for c in range(NCH):
                    if c + 1 < NCH:
                        key_transposes(g, c + 1)
                    kr, ke = KTR[c % 2], KTE[c % 2]
                    b, t0 = ps[6 + c // 2 % 2], c % 2 * 256
                    pe.wait_ge(kvT_act, NCH * g + c + 1)
                    pe.wait_ge(kvT_kept, NCH * g + c + 2)
                    if c % 2 == 0 and 4 * g + c // 2 >= 2:
                        pe.wait_ge(s_kept, 4 * g + c // 2 - 1)
                    if c == 0 and g == 1:
                        pe.wait_ge(s_new, 1)
                    for r in range(2):
                        for j in range(4):
                            nc.tensor.matmul(b[32 * j:32 * j + 32, t0:t0 + 256], QAS[:, r, 4 * g + j, :], kr[:, j, r, :],
                                             start=(r == 0), stop=False, skip_group_check=True)
                    for j in range(4):
                        mm = nc.tensor.matmul(b[32 * j:32 * j + 32, t0:t0 + 256], QPS[0:32, 4 * g + j, :],
                                              ke[0:32, j // 2, j % 2 * 256:j % 2 * 256 + 256],
                                              start=False, stop=True, skip_group_check=True)
                    mm.then_inc(s_mm, 1)
                pe.wait_ge(s_kept, 4 * g + 3)
                b = ps[6]
                for j in range(4):
                    for r in range(2):
                        nc.tensor.matmul(b[32 * j:32 * j + 32, 0:32], QAS[:, r, 4 * g + j, :], CKT[:, r, SEQ:T],
                                         start=(r == 0), stop=False, skip_group_check=True)
                    mm = nc.tensor.matmul(b[32 * j:32 * j + 32, 0:32], QPS[0:32, 4 * g + j, :],
                                          KPT[0:32, SEQ:T], start=False, stop=True, skip_group_check=True)
                mm.then_inc(s_mm, 1)
                pe.wait_ge(s_exp, g + 1)
                for n in range(4):
                    if n >= 2 or g:
                        pe.wait_ge(sT_kept, 5 * g + n - 1)
                    for m in range(4):
                        mm = nc.tensor.transpose(ps[2 + n % 2][:, m * P:(m + 1) * P],
                                                 S[:, (4 * n + m) * P:(4 * n + m + 1) * P], ident)
                    mm.then_inc(sT_mm, 1)
                nc.tensor.transpose(ps[5][0:32, 0:P], S[:, 2048:2080], ident).then_inc(sT_mm, 1)
                pe.wait_ge(sT_kept, 5 * g + 5)
                for m, c in enumerate(V_ORDER[g]):
                    for pg in range(2):
                        for j in range(4):
                            mm = nc.tensor.matmul(ps[4][32 * j:32 * j + 32, 0:R], PT[:, 2 * c + pg, 32 * j:32 * j + 32],
                                                  PAGES[c][:, j, pg, 0:R], start=(m == 0 and pg == 0), stop=False,
                                                  skip_group_check=True)
                    mm.then_inc(v_used, 1)
                for j in range(4):
                    mm = nc.tensor.matmul(ps[4][32 * j:32 * j + 32, 0:R], PNT[0:32, 32 * j:32 * j + 32], CK[0:32, 2, :],
                                          start=False, stop=True, skip_group_check=True)
                mm.then_inc(so_mm, 1)
                pe.wait_ge(so_kept, g + 1)
                for r in range(2):
                    mm = nc.tensor.transpose(ps[5][:, r * P:(r + 1) * P], OS[:, r * P:(r + 1) * P], ident)
                mm.then_inc(soT_mm, 1)
                if g == 0:
                    prompt_attention()
            pe.wait_ge(soT_kept, 2)
            for n in range(4):
                if n >= 2:
                    pe.wait_ge(cat_kept, n - 1)
                for hh in range(2):
                    h = 2 * n + hh
                    for r in range(2):
                        mm = nc.tensor.matmul(ps[n % 2][64 * hh:64 * hh + 64, 0:T], WUV[:, r, h * VD:(h + 1) * VD],
                                              QA[:, r, h, :], start=(r == 0), stop=(r == 1))
                mm.then_inc(omla_mm, 1)

        def act_attention(act, steps):
            for n in range(8):
                act.wait_ge(qa_mm, 2 * n + 1)
                nc.scalar.copy(QA[:, 0, n, 0:SEQ], ps[(2 * n) % 8][:, 0:SEQ])
                nc.scalar.copy(QAS[:, 0, :, NS * n:NS * n + NS],
                               ps[(2 * n) % 8][:, SEQ:T].rearrange("p (b s) -> p b s", s=NS)).then_inc(qa_act, 1)
            for n, (t, h0, nh) in enumerate(((0, 0, 4), (0, 4, 4), (1, 0, 4), (1, 4, 4), (2, 0, 8))):
                t0, nt = TILES[t]
                act.wait_ge(qpT_mm, n + 1)
                src = ps[n][0:32, 0:nh * nt]
                if t < 2:
                    op = nc.scalar.copy(QP[0:32, h0:h0 + nh, t0:t0 + nt], src.rearrange("p (h t) -> p h t", h=nh))
                else:
                    op = nc.scalar.copy(QPS[0:32].rearrange("p b (h s) -> p b h s", s=NS),
                                        src.rearrange("p (h b s) -> p b h s", h=nh, s=NS))
                op.then_inc(qpT_kept, 1)

            def exp_head(h):
                i = h % 2
                act.wait_ge(pmax_ready, h + 1)
                if h >= 2:
                    act.wait_ge(probT_mm, h - 1)
                nc.scalar.activation(PP[:, i, 0:P], ps[i][:, 0:P], ACT.Exp, bias=MXP[:, i, 0:1], scale=SCALE,
                                     accum_out=RSP[:, i, 0:1])
                nc.scalar.activation(PP[:, i, P:384], ps[i][:, P:384], ACT.Exp, bias=MXP[:, i, 1:2], scale=SCALE,
                                     accum_out=RSP[:, i, 1:2]).then_inc(pexp_ready, 1)

            def prompt_attention():
                exp_head(0)
                for h in range(H):
                    i = h % 2
                    if h + 1 < H:
                        exp_head(h + 1)
                    act.wait_ge(probT_mm, h + 1)
                    if h >= 2:
                        act.wait_ge(po_mm, h - 1)
                    nc.scalar.copy(PPT[:, i, :], ps[2 + i][:, 0:384]).then_inc(probT_kept, 1)
                    act.wait_ge(po_mm, h + 1)
                    nc.scalar.copy(QA[:, :, h, 0:SEQ], ps[4 + i][:, :].rearrange("p (r t) -> p r t", r=2)
                                   ).then_inc(po_kept, 1)

            act.wait_ge(h0_stored, 16)

            def keep_scores(g, m):
                act.wait_ge(s_mm, 9 * g + 2 * m + 2)
                if m == 0 and g:
                    act.wait_ge(sT_mm, 5)
                nc.scalar.mul(S[:, m * 512:(m + 1) * 512], ps[6 + m % 2][:, :], SCALE).then_inc(s_kept, 1)

            for g in range(2):
                for c in range(NCH):
                    act.wait_ge(kvT_mm, NCH * g + c + 3)
                    if c >= 2 or g:
                        act.wait_ge(s_mm, 9 * g + max(c - 1, 0))
                    for j in (2, 3):
                        nc.scalar.copy(KTR[c % 2][:, j], ps[j][:, :].rearrange("p (r t) -> p r t", r=2))
                    nc.scalar.copy(KTE[c % 2][0:32, 1], ps[5][0:32, :]).then_inc(kvT_act, 1)
                    if c % 2 == 0 and c:
                        keep_scores(g, c // 2 - 1)
                keep_scores(g, 3)
                act.wait_ge(s_max, g + 1)
                nc.scalar.activation(S, S, ACT.Exp, bias=MXS[:, g:g + 1], accum_out=RSS[:, g:g + 1]).then_inc(s_exp, 1)
                for n in range(4):
                    act.wait_ge(sT_mm, 5 * g + n + 1)
                    if g and n == 0:
                        act.wait_ge(so_mm, 1)
                    nc.scalar.copy(PT[:, 4 * n:4 * n + 4, :], ps[2 + n % 2][:, :].rearrange("p (m q) -> p m q", m=4)
                                   ).then_inc(sT_kept, 1)
                act.wait_ge(sT_mm, 5 * g + 5)
                nc.scalar.copy(PNT[0:32], ps[5][0:32, 0:P]).then_inc(sT_kept, 1)
                act.wait_ge(soT_mm, g + 1)
                for r in range(2):
                    op = nc.scalar.copy(QA[:, r, :, SEQ + 16 * g:SEQ + 16 * g + 16].rearrange("p h (j s) -> p j h s", j=4),
                                        ps[5][:, r * P:(r + 1) * P].rearrange("p (j h s) -> p j h s", j=4, h=H))
                op.then_inc(soT_kept, 1)
                if g == 0:
                    prompt_attention()
            for n in range(4):
                act.wait_ge(omla_mm, n + 1)
                nc.scalar.copy(CAT[:, n, :], ps[n % 2][:, 0:T]).then_inc(cat_kept, 1)

        def dve_attention(dve, steps):
            V = nc.vector
            co = cst("cos").rearrange("p (t f) -> p t f", t=3)
            si = cst("sin").rearrange("p (t f) -> p t f", t=3)
            for n in range(4):
                dve.wait_ge(qn_mm, n + 1)
                V.tensor_copy(QN[:, n, :], ps[n][:, 0:T]).then_inc(q_kept, 1)
            for t, (t0, nt) in enumerate(TILES):
                dve.wait_ge(qn_mm, t + 5)
                if t == 2:
                    dve.wait_ge(q_kept, 5)
                q = ps[4 + t][0:nt, 0:256].rearrange("p (h f) -> p h f", h=H)
                out = QPT[0:nt, t, :].rearrange("p (h f) -> p h f", h=H)
                cb = co[0:nt, t, :].unsqueeze(1).to_broadcast([nt, H, 16])
                sb_ = si[0:nt, t, :].unsqueeze(1).to_broadcast([nt, H, 16])
                ta = TMP[0:nt, 2 * (t % 2), :].rearrange("p (h f) -> p h f", h=H)
                tb = TMP[0:nt, 2 * (t % 2) + 1, :].rearrange("p (h f) -> p h f", h=H)
                V.tensor_tensor(out[:, :, 0:16], q[:, :, 0:16], cb, ALU.mult)
                V.tensor_tensor(out[:, :, 16:32], q[:, :, 16:32], cb, ALU.mult)
                V.tensor_tensor(ta, q[:, :, 16:32], sb_, ALU.mult)
                steps.step(V.tensor_tensor(tb, q[:, :, 0:16], sb_, ALU.mult))
                V.tensor_tensor(out[:, :, 0:16], out[:, :, 0:16], ta, ALU.subtract)
                op = V.tensor_tensor(out[:, :, 16:32], out[:, :, 16:32], tb, ALU.add)
                op.then_inc(q_kept, 1)
            for n in range(8):
                dve.wait_ge(qa_mm, 2 * n + 2)
                V.tensor_copy(QA[:, 1, n, 0:SEQ], ps[(2 * n + 1) % 8][:, 0:SEQ])
                V.tensor_copy(QAS[:, 1, :, NS * n:NS * n + NS],
                              ps[(2 * n + 1) % 8][:, SEQ:T].rearrange("p (b s) -> p b s", s=NS)).then_inc(qa_dve, 1)

            def front(h):
                i = h % 2
                dve.wait_ge(pscore_mm, h + 1)
                V.tensor_reduce(MXP[:, i, 0:1], ps[i][:, 0:P], AX, ALU.max)
                steps.step(V.tensor_reduce(MXP[:, i, 1:2], ps[i][:, P:384], AX, ALU.max))
                V.tensor_scalar(MXP[:, i, 0:2], MXP[:, i, 0:2], -SCALE, None, ALU.mult).then_inc(pmax_ready, 1)

            def prompt_attention():
                front(0)
                for h in range(H):
                    i = h % 2
                    if h + 1 < H:
                        front(h + 1)
                    dve.wait_ge(pexp_ready, h + 1)
                    steps.step(V.reciprocal(RSP[:, i, 0:2], RSP[:, i, 0:2]))
                    V.tensor_scalar(PP[:, i, 0:P], PP[:, i, 0:P], RSP[:, i, 0:1], None, ALU.mult)
                    V.tensor_scalar(PP[:, i, P:384], PP[:, i, P:384], RSP[:, i, 1:2], None, ALU.mult
                                    ).then_inc(prob_ready, 1)

            dve.wait_ge(h0_stored, 16)
            for g in range(2):
                for c in range(NCH):
                    dve.wait_ge(kvT_mm, NCH * g + c + 3)
                    if c >= 2 or g:
                        dve.wait_ge(s_mm, 9 * g + max(c - 1, 0))
                    for j in (0, 1):
                        V.tensor_copy(KTR[c % 2][:, j], ps[j][:, :].rearrange("p (r t) -> p r t", r=2))
                    V.tensor_copy(KTE[c % 2][0:32, 0], ps[4][0:32, :]).then_inc(kvT_kept, 1)
                dve.wait_ge(s_mm, 9 * g + 9)
                if g:
                    dve.wait_ge(sT_mm, 5)
                V.scalar_tensor_tensor(S[:, 2048:2080], ps[6][:, 0:32], SCALE,
                                       cst("mask_new")[:, 32 * g:32 * g + 32], ALU.mult, ALU.add).then_inc(s_new, 1)
                dve.wait_ge(s_new, g + 1)
                dve.wait_ge(s_kept, 4 * g + 4)
                steps.step(V.tensor_reduce(MXS[:, g:g + 1], S, AX, ALU.max))
                V.tensor_scalar(MXS[:, g:g + 1], MXS[:, g:g + 1], -1.0, None, ALU.mult).then_inc(s_max, 1)
                dve.wait_ge(s_exp, g + 1)
                steps.step(V.reciprocal(RSS[:, g:g + 1], RSS[:, g:g + 1]))
                dve.wait_ge(so_mm, g + 1)
                if g:
                    dve.wait_ge(soT_mm, 1)
                V.tensor_scalar(OS, ps[4][:, 0:R], RSS[:, g:g + 1], None, ALU.mult).then_inc(so_kept, 1)
                if g == 0:
                    prompt_attention()

        out_mm, res_kept, ln_var, ln_std, ln_done, xt_mm, xt_kept = map(sem, (
            "out_mm", "res_kept", "ln_var", "ln_std", "ln_done", "xt_mm", "xt_kept"))
        x1_stored = sem("x1_stored")
        ln_norm = sem("ln_norm")
        LNS = small[:, 512:572]

        def ln_finished(eng, s, t):
            eng.wait_ge(*((ln_norm, 3 * s + 3) if t == 2 else (ln_done, 2 * s + t + 1)))

        def out_projection(pe, l, lhs, w, t):
            t0, nt = TILES[t]
            for n in range(2):
                for k in range(KC):
                    mm = nc.tensor.matmul(ps[2 * t + n][0:nt, :], lhs[:, k, t0:t0 + nt],
                                          w[:, k, n * 512:(n + 1) * 512], start=(k == 0), stop=(k == KC - 1))
            mm.then_inc(out_mm, 1)

        def ln_dve(dve, steps, s, t, nt):
            V = nc.vector
            st = LNS[0:nt, 20 * t:20 * t + 12].rearrange("p (a b) -> p a b", a=2)
            mv, rs = LNS[0:nt, 20 * t + 12:20 * t + 14], LNS[0:nt, 20 * t + 14:20 * t + 15]
            x = X[0:nt, t, :]
            for n in range(2):
                op = V.bn_stats(st[:, n, :], X[0:nt, t, n * 512:(n + 1) * 512])
            steps.step(op)
            V.bn_aggr(mv, st).then_inc(ln_var, 1)
            if t == 2:
                dve.wait_ge(ld_rows, 32 * (s + 1))
                dve.wait_ge(ln_var, 3 * s + 3)
                steps.step(V.scalar_tensor_tensor(x, x, mv[:, 0:1], ROWS[0:nt, 0, :], ALU.subtract, ALU.mult))
            dve.wait_ge(ln_std, 3 * s + t + 1)
            steps.step(V.reciprocal(rs, rs))
            if t == 2:
                op = V.scalar_tensor_tensor(x, x, rs, ROWS[0:nt, 1, :], ALU.mult, ALU.add)
            else:
                op = V.tensor_scalar(x, x, mv[:, 0:1], rs, ALU.subtract, ALU.mult)
            op.then_inc(ln_norm, 1)

        def ln_act(act, s, t):
            nt = TILES[t][1]
            act.wait_ge(ln_var, 3 * s + t + 1)
            nc.scalar.activation(LNS[0:nt, 20 * t + 14:20 * t + 15], LNS[0:nt, 20 * t + 13:20 * t + 14], ACT.Sqrt,
                                 bias=cst("eps", nt)).then_inc(ln_std, 1)

        def ln_pool(pool, s, dst=None, done=None):
            G = nc.gpsimd
            pool.wait_ge(ld_rows, 32 * (s + 1))
            for t, (t0, nt) in enumerate(TILES):
                if t < 2:
                    pool.wait_ge(ln_norm, 3 * s + t + 1)
                    G.tensor_tensor(X[0:nt, t, :], X[0:nt, t, :], ROWS[0:nt, 0, :], ALU.mult).then_inc(pool_step, 1)
                    pool.wait_ge(pool_step, 2 * s + t + 1)
                    G.tensor_tensor(X[0:nt, t, :], X[0:nt, t, :], ROWS[0:nt, 1, :], ALU.add).then_inc(ln_done, 1)
                if dst is not None:
                    ln_finished(pool, s, t)
                    pool.dma_start(dst[t0:t0 + nt], X[0:nt, t, :]).then_inc(done, 16)

        def transposes_x(pe, s, r, t):
            t0, nt = TILES[t]
            ln_finished(pe, s, t)
            if t == 1:
                pe.wait_ge(xt_kept, 3 * r + 1)
            for k in range(KC):
                bank, lo = (ps[0], k * nt) if t == 2 else (ps[6 + k // 4], k % 4 * P)
                mm = nc.tensor.transpose(bank[:, lo:lo + nt], X[0:nt, t, k * P:(k + 1) * P], ident[0:nt, 0:nt])
            mm.then_inc(xt_mm, 1)

        def keep_xt(act, r, t):
            t0, nt = TILES[t]
            act.wait_ge(xt_mm, 3 * r + t + 1)
            if t == 2:
                op = nc.scalar.copy(XT[:, :, t0:t0 + nt], ps[0][:, 0:KC * nt].rearrange("p (k t) -> p k t", k=KC))
            else:
                for n in range(2):
                    op = nc.scalar.copy(XT[:, 4 * n:4 * n + 4, t0:t0 + nt],
                                        ps[6 + n][:, :].rearrange("p (k t) -> p k t", k=4))
            op.then_inc(xt_kept, 1)

        NW = 6
        HS, HH, HT, YS = (at(M, 6144, 2, P), at(M, 6400, 2, P), at(M, 6656, 2, P), at(M, 6912, 2, 512))
        RT = M[:, 7936:9216]
        XG = at(M, 9216, 2, D)
        GY = at(M, 12184, 3, 2, D)
        XGT = at(xT_t, 0, 2, KC, 2 * CAP)
        yd = nc.dram_tensor("expert_rows", (SLOT_ROWS, D), F32).ap()
        xd = [nc.dram_tensor(f"x_rows{l}", (T, D), F32).ap() for l in range(2)]
        slots = [nc.dram_tensor(f"slot_tokens{l}", (SLOT_ROWS, 1), I32).ap() for l in range(2)]
        TID, DI = ints[:, 0:3], ints[:, 3:9]
        IDX, IDXX = ints[:, 9:17], ints[0:CAP, 17:17 + MAX_EXTRA]
        XE, XN = ints[:, 25:25 + MAX_EXTRA], ints[:, 33:35]
        tables_ready = sem("tables_ready")
        logit_mm, logit_exp, pick_ready, rank_mm, dest_ready, tok_scattered, xg_zero = map(sem, (
            "logit_mm", "logit_exp", "pick_ready", "rank_mm", "dest_ready", "tok_scattered", "xg_zero"))
        w_ld = slot_ld
        gat, ystore = [sem("gat0"), sem("gat1")], [sem("ystore0"), sem("ystore1")]
        idx_ld, xT_mm, xgt_kept, gu_mm, hs_ready, hh_ready, ht_mm, ht_kept, y_mm, ys_kept, gy_ld = map(sem, (
            "idx_ld", "xT_mm", "xgt_kept", "gu_mm", "hs_ready", "hh_ready", "ht_mm", "ht_kept", "y_mm", "ys_kept",
            "gy_ld"))
        EX = [{k: sem(f"extra{l}_{k}") for k in ("w_ld0", "w_ld1", "gat", "pe", "act", "dve", "ystore0", "ystore1")}
              for l in range(2)]
        EXTRA_STEPS = {"xT_mm": ("pe", 4, 1), "gu_mm": ("pe", 4, 2), "ht_mm": ("pe", 4, 3), "y_mm": ("pe", 4, 4),
                       "hs_ready": ("act", 3, 1), "ht_kept": ("act", 3, 2), "ys_kept": ("act", 3, 3),
                       "xgt_kept": ("dve", 2, 1), "hh_ready": ("dve", 2, 2)}

        def wait_extra(eng, l, step, i):
            who, n, k = EXTRA_STEPS[step]
            eng.wait_ge(EX[l][who], i * n + k)

        def w_slot(n):
            n = n % NW
            return slot_t[:, 6144 * n:6144 * (n + 1)] if n < 3 else M[:, (0, 18328, 12184)[n - 3]:][:, 0:6144]

        def w_loaded(l, n):
            pages_ = chunk_loaded(1, 4) if n % NW < 4 else 0
            return pages_ + 16 * (l * len(range(n % NW, NE, NW)) + n // NW + 1)

        def x_slot(u):
            return w_slot(15) if u else w_slot(5)

        def weights(w):
            return (w[:, 0:4096].rearrange("p (k h f) -> p k h f", k=KC, h=2),
                    w[:, 4096:6144].rearrange("p (h d) -> p h d", h=2))

        def each_extra(eng, l, body):
            eng.wait_ge(dest_ready, l + 1)
            n_extra = eng.value_load(XN[0:1, l:l + 1], min_val=0, max_val=MAX_EXTRA)
            with eng.If(n_extra > 0):
                body(0, 0)
                with eng.If(n_extra > 1):
                    body(1, 1)
                    with eng.Fori(1, MAX_EXTRA // 2) as q:
                        for u in range(2):
                            with eng.If(q * 2 + u < n_extra):
                                body(q * 2 + u, u)

        def before(N, n):
            return not (isinstance(N, int) and N < n)

        def loads_moe(sp, l):
            src = a["w_moe"]

            def load(layer, n):
                sp.dma_start(w_slot(n), src[layer, n]).then_inc(w_ld[n % NW], 16)

            if l == 0:
                sp.wait_ge(v_used, 2 * NCH)
                load(0, 1)
                load(0, 2)
                sp.wait_ge(omla_mm, 4)
                sp.wait_ge(ckv_stored, 48)
                load(0, 0)
            else:
                loads_conformer(sp)
                for n in range(3):
                    load(1, n)
            sp.wait_ge(out_mm, 3 * l + 3)
            load(l, 3)
            sp.wait_ge(ln_var, 6 * l + 3)
            sp.wait_ge(x1_stored, 48 * (l + 1))
            load(l, 4)
            sp.wait_ge(ln_done, 4 * l + 2)
            sp.wait_ge(ln_norm, 6 * l + 3)
            sp.dma_start(ROWS[:, 0, :], a["rows"][2 * l + 1]).then_inc(ld_rows, 16)
            sp.dma_start(ROWS[:, 1, :], a["rows_b"][2 * l + 1]).then_inc(ld_rows, 16)
            if l:
                sp.wait_ge(conv_stored, 64)
            sp.wait_ge(gat[1], 16 * (4 * l + 1))
            load(l, 5)
            for n in range(NW, NE):
                sp.wait_ge(y_mm, 16 * l + n - NW + 1)
                load(l, n)

            def body(i, u):
                e = sp.value_load(XE[0:1, bass.ds(i, 1)], min_val=0, max_val=NE - 1)
                sp.wait_ge(y_mm, 16 * l + (16 if u else 12))
                sp.wait_ge(EX[l]["gat"], i * 16 + 16)
                sp.dma_start(x_slot(u), src[l, bass.ds(e, 1)].rearrange("a p f -> (a p) f")
                             ).then_inc(EX[l][f"w_ld{u}"], 16)
            each_extra(sp, l, body)

        def gathered_transposes(pe, xb):
            for k in range(KC):
                mm = nc.tensor.transpose(ps[k // 4][:, k % 4 * P:(k % 4 + 1) * P], XG[:, xb, k * P:(k + 1) * P], ident)
            return mm

        def gate_up(pe, w, xb, b):
            wgu, _ = weights(w)
            for k in range(KC):
                for h in range(2):
                    mm = nc.tensor.matmul(ps[2 + b][64 * h:64 * h + 64, 0:256], XGT[:, xb, k, CAP * b:CAP * b + CAP],
                                          wgu[:, k, h, :], start=(k == 0), stop=(k == KC - 1), skip_group_check=True)
            return mm

        def down(pe, w, b):
            _, wd = weights(w)
            for h in range(2):
                for n in range(2):
                    mm = nc.tensor.matmul(ps[6 + b][64 * n:64 * n + 64, :], HT[:, b, h * 64:h * 64 + 64],
                                          wd[:, h, n * 512:(n + 1) * 512], start=(h == 0), stop=(h == 1),
                                          skip_group_check=True)
            return mm

        def router_products(pe, l, t):
            t0, nt = TILES[t]
            transposes_x(pe, 2 * l, 2 * l, t)
            pe.wait_ge(xt_kept, 6 * l + t + 1)
            wr = prm("w_router").rearrange("p (k e) -> p k e", k=KC)
            for k in range(KC):
                mm = nc.tensor.matmul(ps[1][0:nt, t * NE:(t + 1) * NE], XT[:, k, t0:t0 + nt], wr[:, k, :],
                                      start=(k == 0), stop=(k == KC - 1))
            if t == 2:
                mm.then_inc(logit_mm, 1)

        def products_moe(pe, l):
            pe.wait_ge(pick_ready, l + 1)
            picks = RT[:, 0:48].rearrange("p (t e) -> p t e", t=3)
            for t in range(3):
                for u in range(t + 1):
                    nc.tensor.matmul(ps[7][:, t * NE:(t + 1) * NE], cst("tri_strict") if u == t else ones,
                                     picks[:, u, :], start=(u == 0), stop=(u == t))
            for u in range(3):
                mm = nc.tensor.matmul(ps[7][:, 48:64], ones, picks[:, u, :], start=(u == 0), stop=(u == 2))
            mm.then_inc(rank_mm, 1)
            pe.wait_ge(dest_ready, l + 1)


            def transposes(n):
                N, xb = 16 * l + n, n // 2 % 2
                pe.wait_ge(gat[xb], 16 * (N // 4 + 1))
                if N:
                    pe.wait_ge(xgt_kept, N // 2)
                gathered_transposes(pe, xb).then_inc(xT_mm, 1)

            def second_half(n):
                N, b = 16 * l + n, n % 2
                pe.wait_ge(hh_ready, N + 1)
                if N >= 2:
                    pe.wait_ge(ht_kept, N - 1)
                nc.tensor.transpose(ps[4 + b][:, 0:P], HH[:, b, :], ident).then_inc(ht_mm, 1)
                pe.wait_ge(ht_kept, N + 1)
                if N >= 2:
                    pe.wait_ge(ys_kept, N - 1)
                down(pe, w_slot(n), b).then_inc(y_mm, 1)

            transposes(0)
            for n in range(NE):
                N = 16 * l + n
                pe.wait_ge(w_ld[n % NW], w_loaded(l, n))
                pe.wait_ge(xgt_kept, N // 2 + 1)
                if N >= 2:
                    pe.wait_ge(hh_ready, N - 1)
                gate_up(pe, w_slot(n), n // 2 % 2, n % 2).then_inc(gu_mm, 1)
                if n % 2 and n + 1 < NE:
                    transposes(n + 1)
                if n:
                    second_half(n - 1)
            second_half(NE - 1)
            pe.wait_ge(ys_kept, 16 * (l + 1))

            def extra(i, u):
                x = EX[l]
                pe.wait_ge(x["gat"], i * 16 + 16)
                gathered_transposes(pe, u).then_inc(x["pe"], 1)
                pe.wait_ge(x[f"w_ld{u}"], (i - u) * 8 + 16)
                wait_extra(pe, l, "xgt_kept", i)
                gate_up(pe, x_slot(u), 0, 0).then_inc(x["pe"], 1)
                wait_extra(pe, l, "hh_ready", i)
                nc.tensor.transpose(ps[4][:, 0:P], HH[:, 0, :], ident).then_inc(x["pe"], 1)
                wait_extra(pe, l, "ht_kept", i)
                down(pe, x_slot(u), 0).then_inc(x["pe"], 1)
            each_extra(pe, l, extra)

        def act_moe(act, steps, l):
            act.wait_ge(logit_mm, l + 1)
            act.wait_ge(xg_zero, l + 1)
            lg = RT[:, 48:96].rearrange("p (t e) -> p t e", t=3)
            nc.scalar.activation(lg[:, 0:2, :], ps[1][:, 0:32].rearrange("p (t e) -> p t e", t=2), ACT.Exp, scale=-1.0)
            nc.scalar.activation(lg[0:32, 2, :], ps[1][0:32, 32:48], ACT.Exp, scale=-1.0).then_inc(logit_exp, 1)

            def silu(b):
                return nc.scalar.activation(HS[:, b, :], ps[2 + b][:, 0:P], ACT.Silu)

            def keep_ht(b):
                return nc.scalar.copy(HT[:, b, :], ps[4 + b][:, 0:P])

            def keep_y(b, to):
                return nc.scalar.copy(YS[:, to, :], ps[6 + b][:, :])

            def store_y(row, b, done):
                for n in range(2):
                    act.dma_start(yd[bass.ds(row, CAP), n * 512:(n + 1) * 512], YS[64 * n:64 * n + 64, b, :]
                                  ).then_inc(done, 16)

            def second_half(n):
                N, b = 16 * l + n, n % 2
                act.wait_ge(ht_mm, N + 1)
                if N >= 2:
                    act.wait_ge(y_mm, N - 1)
                keep_ht(b).then_inc(ht_kept, 1)
                act.wait_ge(y_mm, N + 1)
                if N >= 2:
                    act.wait_ge(ystore[b], N // 2 * 32)
                keep_y(b, b).then_inc(ys_kept, 1)
                act.wait_ge(ys_kept, N + 1)
                store_y(n * CAP, b, ystore[b])

            act.wait_ge(tok_scattered, 96 * (l + 1))
            act.dma_start(IDX, slots[l][0:NE * CAP].rearrange("(n p) o -> p (n o)", p=P),
                          allow_slow_non_contiguous=True).then_inc(idx_ld, 16)
            act.dma_start(IDXX, slots[l][NE * CAP:].rearrange("(n p) o -> p (n o)", p=CAP),
                          allow_slow_non_contiguous=True).then_inc(idx_ld, 16)
            for n in range(NE):
                N = 16 * l + n
                act.wait_ge(gu_mm, N + 1)
                if N >= 2:
                    act.wait_ge(hh_ready, N - 1)
                silu(n % 2).then_inc(hs_ready, 1)
                if n:
                    second_half(n - 1)
            second_half(NE - 1)

            def extra(i, u):
                x = EX[l]
                wait_extra(act, l, "gu_mm", i)
                silu(0).then_inc(x["act"], 1)
                wait_extra(act, l, "ht_mm", i)
                keep_ht(0).then_inc(x["act"], 1)
                wait_extra(act, l, "y_mm", i)
                if before(i, 2):
                    act.wait_ge(x[f"ystore{u}"], (i - u) * 16)
                keep_y(0, u).then_inc(x["act"], 1)
                wait_extra(act, l, "ys_kept", i)
                store_y(i * CAP + NE * CAP, u, x[f"ystore{u}"])
            act.wait_ge(ystore[0], 256 * (l + 1))
            act.wait_ge(ystore[1], 256 * (l + 1))
            each_extra(act, l, extra)

        def dve_moe(dve, steps, l):
            V = nc.vector
            t3 = lambda off, n=NE: RT[:, off:off + 3 * n].rearrange("p (t e) -> p t e", t=3)
            M12, EXPL, PR, SEL = t3(0), t3(48), t3(96), t3(144)
            O1, O2, W16, SM = t3(192), t3(240), t3(288), t3(336)
            four = RT[:, 384:384 + 8 * 12].rearrange("p (n g) -> p n g", n=8)
            three = RT[:, 480:480 + 8 * 3].rearrange("p (n t) -> p n t", n=8)
            G12 = RT[:, 504:516].rearrange("p (t g) -> p t g", t=3)
            RK_ = t3(520)
            D12 = RT[:, 568:574].rearrange("p (t k) -> p t k", t=3)
            big = lambda x: x.unsqueeze(2)
            if l:
                dve.wait_ge(conv_stored, 64)
            V.memset(EXPL, 0.0).then_inc(xg_zero, 1)
            dve.wait_ge(logit_exp, l + 1)
            steps.step(V.tensor_scalar(PR, EXPL, 1.0, None, ALU.add))
            steps.step(V.reciprocal(PR, PR))
            steps.step(V.tensor_tensor(SEL, PR, prm("r_bias").unsqueeze(1).to_broadcast([P, 3, NE]), ALU.add))
            s4 = SEL.rearrange("p t (g m) -> p (t g) m", m=4)
            V.tensor_tensor(four[:, 0, :], s4[:, :, 0], s4[:, :, 1], ALU.max)
            V.tensor_tensor(four[:, 1, :], s4[:, :, 0], s4[:, :, 1], ALU.min)
            V.tensor_tensor(four[:, 2, :], s4[:, :, 2], s4[:, :, 3], ALU.max)
            steps.step(V.tensor_tensor(four[:, 3, :], s4[:, :, 2], s4[:, :, 3], ALU.min))
            V.tensor_tensor(four[:, 4, :], four[:, 0, :], four[:, 2, :], ALU.max)
            V.tensor_tensor(four[:, 5, :], four[:, 0, :], four[:, 2, :], ALU.min)
            steps.step(V.tensor_tensor(four[:, 6, :], four[:, 1, :], four[:, 3, :], ALU.max))
            steps.step(V.tensor_tensor(four[:, 5, :], four[:, 5, :], four[:, 6, :], ALU.max))
            steps.step(V.tensor_tensor(four[:, 7, :], four[:, 4, :], four[:, 5, :], ALU.add))

            def first_largest(values, out, prio, n, tmp, tmp3):
                steps.step(V.tensor_reduce(tmp3, values, AX, ALU.max))
                steps.step(V.tensor_tensor(tmp, values, big(tmp3).to_broadcast([P, 3, n]), ALU.is_equal))
                steps.step(V.tensor_tensor(tmp, tmp, prio.unsqueeze(1).to_broadcast([P, 3, n]), ALU.mult))
                steps.step(V.tensor_reduce(tmp3, tmp, AX, ALU.max))
                steps.step(V.tensor_tensor(out, tmp, big(tmp3).to_broadcast([P, 3, n]), ALU.is_equal))

            grp = four[:, 7, :].rearrange("p (t g) -> p t g", t=3)
            tmp4 = four[:, 0, :].rearrange("p (t g) -> p t g", t=3)
            first_largest(grp, G12, cst("prio4"), 4, tmp4, three[:, 0, :])
            gflat = G12.rearrange("p t g -> p (t g)")
            steps.step(V.tensor_scalar(four[:, 1, :], gflat, 1.0, -NEG, ALU.subtract, ALU.mult))
            smv = SM.rearrange("p t (g m) -> p (t g) m", m=4)
            steps.step(V.tensor_tensor(smv, s4, gflat.unsqueeze(2).to_broadcast([P, 12, 4]), ALU.mult))
            steps.step(V.tensor_tensor(smv, smv, four[:, 1, :].unsqueeze(2).to_broadcast([P, 12, 4]), ALU.add))
            first_largest(SM, O1, cst("prio16"), NE, W16, three[:, 0, :])
            steps.step(V.scalar_tensor_tensor(SM, O1, 2 * NEG, SM, ALU.mult, ALU.add))
            first_largest(SM, O2, cst("prio16"), NE, W16, three[:, 0, :])
            valid = cst("valid").unsqueeze(2).to_broadcast([P, 3, NE])
            V.tensor_tensor(O1, O1, valid, ALU.mult)
            steps.step(V.tensor_tensor(O2, O2, valid, ALU.mult))
            V.tensor_tensor(M12, O1, O2, ALU.add).then_inc(pick_ready, 1)
            for k, o_ in enumerate((O1, O2)):
                steps.step(V.tensor_tensor(W16, PR, o_, ALU.mult))
                steps.step(V.tensor_reduce(three[:, 1 + k, :], W16, AX, ALU.add))
            steps.step(V.tensor_tensor(three[:, 3, :], three[:, 1, :], three[:, 2, :], ALU.add))
            steps.step(V.tensor_scalar(three[:, 3, :], three[:, 3, :], 1e-30, None, ALU.max))
            steps.step(V.reciprocal(three[:, 3, :], three[:, 3, :]))
            V.tensor_tensor(three[:, 4, :], three[:, 1, :], three[:, 3, :], ALU.mult)
            V.tensor_tensor(three[:, 5, :], three[:, 2, :], three[:, 3, :], ALU.mult)
            dve.wait_ge(rank_mm, l + 1)
            FL = RT[:, 600:664].rearrange("p (e j) -> p e j", e=NE)
            EXT, CUM, BASE = RT[:, 664:680], RT[:, 680:696], RT[:, 696:712]
            steps.step(V.tensor_tensor(FL, ps[7][:, 48:64].unsqueeze(2).to_broadcast([P, NE, 4]),
                                       cst("item_thr").rearrange("p (e j) -> p e j", e=NE), ALU.is_gt))
            steps.step(V.tensor_reduce(EXT, FL, AX, ALU.add))
            steps.step(V.tensor_tensor_scan(CUM, EXT, EXT, 0.0, ALU.add, ALU.bypass))
            V.tensor_copy(XN[0:1, l:l + 1], CUM[0:1, 15:16])
            steps.step(V.tensor_tensor(BASE, CUM, EXT, ALU.subtract))
            steps.step(V.tensor_scalar(BASE, BASE, float(CAP), float((NE - 1) * CAP), ALU.mult, ALU.add))
            steps.step(V.tensor_tensor(BASE, BASE, cst("row_of"), ALU.subtract))
            rank = ps[7][:, 0:48].rearrange("p (t e) -> p t e", t=3)
            steps.step(V.scalar_tensor_tensor(W16, rank, float(CAP), BASE.unsqueeze(1).to_broadcast([P, 3, NE]),
                                              ALU.is_ge, ALU.mult))
            steps.step(V.tensor_tensor(W16, W16, cst("row_of").unsqueeze(1).to_broadcast([P, 3, NE]), ALU.add))
            steps.step(V.tensor_tensor(RK_, rank, W16, ALU.add))
            for k, o_ in enumerate((O1, O2)):
                steps.step(V.tensor_tensor(W16, RK_, o_, ALU.mult))
                steps.step(V.tensor_reduce(D12[:, :, k], W16, AX, ALU.add))
            steps.step(V.tensor_copy(DI.rearrange("p (t k) -> p t k", t=3), D12))
            ended = RT[0:1, 712:712 + MAX_EXTRA * NE].rearrange("p (i e) -> p i e", i=MAX_EXTRA)
            out8 = RT[0:1, 1264:1272]
            steps.step(V.tensor_tensor(ended, CUM[0:1].unsqueeze(1).to_broadcast([1, MAX_EXTRA, NE]),
                                       cst("item_k", 1).unsqueeze(2).to_broadcast([1, MAX_EXTRA, NE]), ALU.is_le))
            steps.step(V.tensor_reduce(out8, ended, AX, ALU.add))
            V.tensor_copy(XE[0:1], out8).then_inc(dest_ready, 1)
            dve.wait_ge(dest_ready, l + 1)
            for t, (t0, nt) in enumerate(TILES):
                dve.wait_ge(x1_stored, 48 * (l + 1))
                dve.wait_ge(xt_kept, 6 * l + 3)
                op = V.tensor_scalar(X[0:nt, t, :], X[0:nt, t, :], ALPHA, None, ALU.mult)
            steps.step(op)

            def keep_xgt(xb):
                for n in range(2):
                    op = V.tensor_copy(XGT[:, xb, 4 * n:4 * n + 4], ps[n][:, :].rearrange("p (k s) -> p k s", k=4))
                return op

            def gate(b):
                return V.tensor_tensor(HH[:, b, :], HS[:, b, :], ps[2 + b][:, P:256], ALU.mult)

            def keep(n):
                N = 16 * l + n
                dve.wait_ge(xT_mm, N // 2 + 1)
                if N >= 4:
                    dve.wait_ge(gu_mm, N - 2)
                keep_xgt(n // 2 % 2).then_inc(xgt_kept, 1)

            keep(0)
            for n in range(NE):
                N = 16 * l + n
                if n % 2 and n + 1 < NE:
                    keep(n + 1)
                dve.wait_ge(hs_ready, N + 1)
                if N >= 2:
                    dve.wait_ge(ht_mm, N - 1)
                gate(n % 2).then_inc(hh_ready, 1)

            def extra(i, u):
                x = EX[l]
                wait_extra(dve, l, "xT_mm", i)
                keep_xgt(0).then_inc(x["dve"], 1)
                wait_extra(dve, l, "hs_ready", i)
                gate(0).then_inc(x["dve"], 1)
            each_extra(dve, l, extra)
            for t, (t0, nt) in enumerate(TILES):
                dve.wait_ge(gy_ld, 96 * (l + 1))
                for k in range(2):
                    op = V.scalar_tensor_tensor(X[0:nt, t, :], GY[0:nt, t, k, :], three[0:nt, 4 + k, t:t + 1], X[0:nt, t, :],
                                                ALU.mult, ALU.add)
                    steps.step(op)
                ln_dve(dve, steps, 2 * l + 1, t, nt)

        def pool_moe(pool, l):
            G = nc.gpsimd
            pool.wait_ge(out_mm, 3 * (l + 1))
            if l == 0:
                G.memset(XG, 0.0).then_inc(zeroed, 1)
                pool.wait_ge(zeroed, 2)
                for n in range(4):
                    pool.dma_start(yd[NE * CAP + n * P:NE * CAP + (n + 1) * P], XG[:, n % 2, :]).then_inc(tables_ready, 16)
                pool.wait_ge(tables_ready, 112)
            pool.wait_ge(tables_ready, 112)
            pool.wait_ge(dest_ready, l + 1)
            for t, (t0, nt) in enumerate(TILES):
                for k in range(2):
                    pool.indirect_dma_start(out=slots[l], out_offset=bass.IndirectOffsetOnAxis(
                        ap=DI[0:nt, 2 * t + k:2 * t + k + 1], axis=0), in_=TID[0:nt, t:t + 1], in_offset=None
                        ).then_inc(tok_scattered, 16)
            pool.wait_ge(tok_scattered, 96 * (l + 1))

            pool.wait_ge(idx_ld, 32 * (l + 1))
            pool.wait_ge(x1_stored, 48 * (l + 1))

            def gather(b, rows, idx, done):
                pool.indirect_dma_start(out=XG[0:rows, b, :], out_offset=None, in_=xd[l],
                                        in_offset=bass.IndirectOffsetOnAxis(ap=idx, axis=0),
                                        bounds_check=T - 1, oob_is_err=False).then_inc(done, 16)

            for n in range(NE // 2):
                if n >= 2:
                    pool.wait_ge(xT_mm, 8 * l + n - 1)
                gather(n % 2, P, IDX[:, n:n + 1], gat[n % 2])
            n_extra = pool.value_load(XN[0:1, l:l + 1], min_val=0, max_val=MAX_EXTRA)
            x = EX[l]

            def extras_from(i):
                with pool.If(n_extra > i):
                    if i:
                        pool.wait_ge(x["gat"], 16 * i)
                    if i < 2:
                        pool.wait_ge(xT_mm, 8 * l + 7 + i)
                    else:
                        pool.wait_ge(x["pe"], 4 * (i - 1))
                    gather(i % 2, CAP, IDXX[:, i:i + 1], x["gat"])
                    if i + 1 < MAX_EXTRA:
                        extras_from(i + 1)
                    pool.wait_ge(x[f"ystore{i % 2}"], 32 * (i // 2 + 1))

            extras_from(0)
            pool.wait_ge(ystore[0], 256 * (l + 1))
            pool.wait_ge(ystore[1], 256 * (l + 1))
            for t, (t0, nt) in enumerate(TILES):
                for k in range(2):
                    pool.indirect_dma_start(out=GY[0:nt, t, k, :], out_offset=None, in_=yd,
                                            in_offset=bass.IndirectOffsetOnAxis(
                                                ap=DI[0:nt, 2 * t + k:2 * t + k + 1], axis=0)).then_inc(gy_ld, 16)

        def products_layer_out(pe, l):
            if l == 0:
                pe.wait_ge(cat_kept, 4)
                pe.wait_ge(ld_wout, 16)
                pe.wait_ge(y_ready, 1)
                lhs, w = CAT, WOUT
            else:
                pe.wait_ge(cn_ready, 8)
                pe.wait_ge(ld_wout, 48)
                lhs, w = CV, CWO
            out_projection(pe, l, lhs, w, 0)
            out_projection(pe, l, lhs, w, 1)
            router_products(pe, l, 0)
            out_projection(pe, l, lhs, w, 2)
            router_products(pe, l, 1)
            router_products(pe, l, 2)
            products_moe(pe, l)

        def act_layer_out(act, steps, l):
            for t in range(3):
                ln_act(act, 2 * l, t)
                keep_xt(act, 2 * l, t)
            act_moe(act, steps, l)
            for t in range(3):
                ln_act(act, 2 * l + 1, t)

        def dve_layer_out(dve, steps, l):
            V = nc.vector
            dve.wait_ge(ld_x, 48)
            if l:
                dve.wait_ge(ld_wout, 48)
                dve.wait_ge(xt_kept, 6)
            for t, (t0, nt) in enumerate(TILES):
                dve.wait_ge(out_mm, 3 * l + t + 1)
                for n in range(2):
                    xv = X[0:nt, t, n * 512:(n + 1) * 512]
                    op = V.scalar_tensor_tensor(xv, xv, ALPHA, ps[2 * t + n][0:nt, :], ALU.mult, ALU.add)
                op.then_inc(res_kept, 1)
                dve.wait_ge(res_kept, 3 * l + t + 1)
                if l:
                    steps.step(V.tensor_tensor(X[0:nt, t, :], X[0:nt, t, :], BOUT[0:nt], ALU.add))
                ln_dve(dve, steps, 2 * l, t, nt)
            dve_moe(dve, steps, l)


        def pool_layer_out(pool, store, l):
            if l == 0:
                for n in range(2):
                    pool.dma_start(slots[n], a["nobody"]).then_inc(tables_ready, 16)
                pool.dma_start(TID, a["token_ids"]).then_inc(tables_ready, 16)
            ln_pool(pool, 2 * l, xd[l], x1_stored)
            pool_moe(pool, l)
            if l == 0:
                ln_pool(pool, 1)
            else:
                ln_pool(pool, 3, o["y"], stored)
                n_stored[0] += 3


        CWO = at(M, 0, KC, D)
        VP = at(M, 8192, KC, HIST + SEQ)
        VS = at(M, 10480, KC, HIST + NS, NB)
        CV = at(M, 12656, KC, T)
        CQ = at(M, 14960, KC, T)
        PE_TAPS = 9
        DIAG = at(M, 14960, 2, PE_TAPS, P)
        PROD = at(M, 18432, 4, NB, NS, KW)
        CW = at(M, 18432, 4, KC, P)
        MU, RC = M[:, 22528:22816], M[:, 22816:23104]
        BOUT = M[:, 23104:24128]
        SG = at(M, 17264, 2, T)
        diag_ready, tap_mm, prod_ready = sem("diag_ready"), sem("tap_mm"), sem("prod_ready")
        glu_mm, sig_ready, v_ready, dw_ready, mean_kept, cn_ready = map(sem, (
            "glu_mm", "sig_ready", "v_ready", "dw_ready", "mean_kept", "cn_ready"))

        def loads_conformer(sp):
            sp.wait_ge(gy_ld, 96)
            for n in range(16):
                if n == 4:
                    sp.wait_ge(ln_norm, 6)
                    sp.wait_ge(zeroed, 3)
                    sp.dma_start(VS[:, :, 0:HIST, :], a["conf_hist"]).then_inc(ld_hist, 16)
                if n >= 4:
                    sp.wait_ge(glu_mm, n - 3)
                sp.dma_start(CW[:, n % 4], a["w_conf"][n // 2 + 8 * (n % 2)]).then_inc(ring_ld[n % 4], 16)
            sp.dma_start(CWO, a["w_conf_out"]).then_inc(ld_wout, 16)
            sp.wait_ge(ln_done, 4)
            sp.wait_ge(ln_norm, 6)
            sp.dma_start(ROWS[:, 0, :], a["rows"][2]).then_inc(ld_rows, 16)
            sp.dma_start(ROWS[:, 1, :], a["rows_b"][2]).then_inc(ld_rows, 16)
            sp.dma_start(BOUT, a["rows"][4]).then_inc(ld_wout, 16)

        def products_conformer(pe):
            for t in range(3):
                transposes_x(pe, 1, 1, t)
            pe.wait_ge(xt_kept, 6)
            for n in range(16):
                pe.wait_ge(ring_ld[n % 4], chunk_loaded(1, n % 4) + 16 * (n // 4 + 1))
                if n >= 8:
                    pe.wait_ge(v_ready, (n - 8) // 2 + 1)
                for k in range(KC):
                    mm = nc.tensor.matmul(ps[n % 8][:, 0:T], CW[:, n % 4, k, :], XT[:, k, :], start=(k == 0),
                                          stop=(k == KC - 1))
                mm.then_inc(glu_mm, 1)
            pe.wait_ge(v_ready, 8)
            for k in range(KC):
                pe.wait_ge(diag_ready, k + 1)
                for j in range(PE_TAPS):
                    tap = KW - PE_TAPS + j
                    mm = nc.tensor.matmul(ps[4 + k // 2][:, k % 2 * SEQ:(k % 2 + 1) * SEQ], DIAG[:, k % 2, j, :],
                                          VP[:, k, tap:tap + SEQ], start=(j == 0), stop=(j == PE_TAPS - 1),
                                          skip_group_check=True)
                mm.then_inc(tap_mm, 1)
            pe.wait_ge(dw_ready, 2 * KC + 1)
            for k in range(KC):
                mm = nc.tensor.matmul(ps[0][:, 0:T], ones, CV[:, k, :], start=(k == 0), stop=(k == KC - 1))
            mm.then_inc(sum_mm, 1)
            pe.wait_ge(sq_ready, 8)
            for k in range(KC):
                mm = nc.tensor.matmul(ps[1][:, 0:T], ones, CQ[:, k, :], start=(k == 0), stop=(k == KC - 1))
            mm.then_inc(sum_mm, 1)
            pe.wait_ge(std_ready, 4)

        def act_conformer(act, steps):
            bi = prm("b_in")
            dw = prm("dw_w").rearrange("p (c k) -> p c k", k=KW)

            def diagonals(k):
                for j in range(PE_TAPS):
                    tap = KW - PE_TAPS + j
                    op = nc.scalar.activation(DIAG[:, k % 2, j, :], ident, ACT.Copy, scale=dw[:, k, tap:tap + 1])
                op.then_inc(diag_ready, 1)

            for t in range(3):
                keep_xt(act, 1, t)
            for k in range(8):
                act.wait_ge(glu_mm, 2 * k + 2)
                if k >= 2:
                    act.wait_ge(v_ready, k - 1)
                nc.scalar.activation(SG[:, k % 2, :], ps[(2 * k + 1) % 8][:, 0:T], ACT.Sigmoid,
                                     bias=bi[:, 8 + k:9 + k]).then_inc(sig_ready, 1)
            for k in range(KC):
                if k >= 2:
                    act.wait_ge(tap_mm, k - 1)
                diagonals(k)
            act.wait_ge(tap_mm, KC)
            act.wait_ge(mean_kept, 1)
            nc.scalar.activation(CQ, CV, ACT.Square).then_inc(sq_ready, 1)
            act.wait_ge(sum_mm, 4)
            nc.scalar.activation(RC, ps[1][:, 0:T], ACT.Sqrt, bias=eps, scale=1.0 / D).then_inc(std_ready, 1)
            act.wait_ge(mean_kept, 2)
            for k in range(8):
                nc.scalar.activation(CV[:, k, :], CV[:, k, :], ACT.Silu, bias=prm("bn")[:, k:k + 1],
                                     scale=prm("gn")[:, k:k + 1]).then_inc(cn_ready, 1)

        def dve_conformer(dve, steps):
            V = nc.vector
            bi = prm("b_in")
            dw = prm("dw_w").rearrange("p (c k) -> p c k", k=KW)
            dve.wait_ge(zeroed, 3)
            dve.wait_ge(ld_hist, 32)

            def glu(k):
                dve.wait_ge(sig_ready, k + 1)
                b = ps[(2 * k) % 8]
                V.scalar_tensor_tensor(VP[:, k, HIST:], b[:, 0:SEQ], bi[:, k:k + 1], SG[:, k % 2, 0:SEQ], ALU.add, ALU.mult)
                V.scalar_tensor_tensor(VS[:, k, HIST:, :], b[:, SEQ:T].rearrange("p (b s) -> p s b", s=NS), bi[:, k:k + 1],
                                       SG[:, k % 2, SEQ:T].rearrange("p (b s) -> p s b", s=NS), ALU.add, ALU.mult
                                       ).then_inc(v_ready, 1)

            def tap(k, j):
                cp = CV[:, k, 0:SEQ]
                if j == 0:
                    return V.tensor_scalar(cp, VP[:, k, 0:SEQ], dw[:, k, 0:1], prm("dw_b")[:, k:k + 1], ALU.mult, ALU.add)
                return V.scalar_tensor_tensor(cp, VP[:, k, j:j + SEQ], dw[:, k, j:j + 1], cp, ALU.mult, ALU.add)

            glu(0)
            glu(1)
            for k in range(0, KC, 2):
                dve.wait_ge(v_ready, k + 2)
                for j in range(KW - PE_TAPS):
                    for c in (k, k + 1):
                        if j:
                            dve.wait_ge(dve_step, steps.count - 1)
                        steps.count += 1
                        tap(c, j).then_inc(dve_step, 1)
                    if j in (5, 14) and k + 2 < KC:
                        glu(k + 2 + (j == 14))
            dve.wait_ge(dve_step, steps.count)
            for k in range(KC):
                dve.wait_ge(tap_mm, 2 * (k // 2) + 2)
                cp = CV[:, k, 0:SEQ]
                V.tensor_tensor(cp, cp, ps[4 + k // 2][:, k % 2 * SEQ:(k % 2 + 1) * SEQ], ALU.add).then_inc(dw_ready, 1)
            for k in range(KC):
                dve.wait_ge(prod_ready, k + 1)
                V.tensor_reduce(CV[:, k, SEQ:T], PROD[:, k % 4].rearrange("p b s j -> p (b s) j"), AX, ALU.add
                                ).then_inc(dw_ready, 1)
            dve.wait_ge(dw_ready, 2 * KC)
            V.tensor_tensor(CV[:, :, SEQ:T], CV[:, :, SEQ:T], prm("dw_b").unsqueeze(2).to_broadcast([P, KC, T - SEQ]),
                            ALU.add).then_inc(dw_ready, 1)
            dve.wait_ge(dw_ready, 2 * KC + 1)
            dve.wait_ge(sum_mm, 3)
            steps.step(V.tensor_scalar(MU, ps[0][:, 0:T], 1.0 / D, None, ALU.mult))
            V.tensor_tensor(CV, CV, MU.unsqueeze(1).to_broadcast([P, KC, T]), ALU.subtract).then_inc(mean_kept, 1)
            dve.wait_ge(std_ready, 4)
            steps.step(V.reciprocal(RC, RC))
            dve.wait_ge(mean_kept, 1)
            V.tensor_tensor(CV, CV, RC.unsqueeze(1).to_broadcast([P, KC, T]), ALU.mult).then_inc(mean_kept, 1)

        def pool_conformer(pool, store):
            G = nc.gpsimd
            pool.wait_ge(ln_norm, 6)
            G.memset(VP[:, :, 0:HIST], 0.0).then_inc(zeroed, 1)
            pool.wait_ge(ld_hist, 32)
            pool.wait_ge(glu_mm, 16)
            pool.wait_ge(v_ready, 8)
            dw = prm("dw_w").rearrange("p (c k) -> p c k", k=KW)
            for k in range(KC):
                if k >= 4:
                    pool.wait_ge(dw_ready, KC + k - 3)
                for s in range(NS):
                    op = G.tensor_tensor(PROD[:, k % 4, :, s, :], VS[:, k, s:s + KW, :].rearrange("p j b -> p b j"),
                                         dw[:, k, :].unsqueeze(1).to_broadcast([P, NB, KW]), ALU.mult)
                op.then_inc(prod_ready, 1)
            store(o["cconv_p"], VP[:, :, SEQ:SEQ + HIST], conv_stored)
            store(o["cconv_s"], VS[:, :, NS:, :], conv_stored)

        block = ctx.enter_context(nc.Block())

        @block.sync
        def _(sp):
            sp.dma_start(XT, a["xT"]).then_inc(ld_xT, 16)
            sp.dma_start(WTOK, a["w_tok"]).then_inc(ld_wtok, 16)
            for n in range(4):
                sp.dma_start(WIN[:, n], a["w_ch"][n]).then_inc(ring_ld[n], 16)
            sp.dma_start(C[:], a["consts"]).then_inc(ld_const, 16)
            sp.dma_start(PM[:], a["params"]).then_inc(ld_const, 16)
            sp.wait_ge(zeroed, 1)
            sp.dma_start(XS[:, :, :, 0:3], a["conv_hist"]).then_inc(ld_hist, 16)
            for n in range(4, 15):
                sp.wait_ge(piece_mm, n - 3)
                sp.dma_start(WIN[:, n % 4], a["w_ch"][n]).then_inc(ring_ld[n % 4], 16)
            sp.dma_start(slot_t[:, 0:4352], a["w_q"]).then_inc(ld_wq, 16)
            for t, (t0, nt) in enumerate(TILES):
                sp.dma_start(X[0:nt, t, :], a["x"][t0:t0 + nt]).then_inc(ld_x, 16)
            sp.wait_ge(piece_mm, 15)
            sp.dma_start(H0, a["state"]).then_inc(ld_h0, 16)
            loads_attention(sp)
            loads_moe(sp, 0)
            loads_moe(sp, 1)

        @block.tensor
        def _(pe):
            pe.wait_ge(ld_xT, 16)
            pe.wait_ge(ld_wtok, 16)
            for t, (t0, nt) in enumerate(TILES):
                for k in range(KC):
                    mm = nc.tensor.matmul(ps[4 + t][0:nt, 0:296], XT[:, k, t0:t0 + nt], WTOK[:, k, :],
                                          start=(k == 0), stop=(k == KC - 1))
                mm.then_inc(tok_mm, 1)
            def latents():
                pe.wait_ge(sq_ready, 6)
                for k in range(3):
                    mm = nc.tensor.matmul(ps[7][:, 0:T], ones, SQ[:, k, :], start=(k == 0), stop=(k == 2))
                mm.then_inc(sum_mm, 1)
                pe.wait_ge(kv_ready, 1)
                pe.wait_ge(tok_kept, 3)
                for t, (t0, nt) in enumerate(TILES):
                    for r in range(2):
                        nc.tensor.transpose(ps[4 + r][:, t0:t0 + nt], CK[0:nt, t, r * P:(r + 1) * P], ident[0:nt, 0:nt])
                    mm = nc.tensor.transpose(ps[6][0:32, t0:t0 + nt], KPE[0:nt, t, :], ident[0:nt, 0:nt])
                mm.then_inc(kvT_mm, 1)

            def log_decays():
                pe.wait_ge(dtA_ready, 1)
                pe.wait_ge(std_ready, 2)
                b = ps[7]
                for c in range(2):
                    nc.tensor.matmul(b[:, 8 * c:8 * c + 8], cst("tri"), DTA[:, c, :], start=True, stop=True)
                    nc.tensor.matmul(b[:, 16 + 8 * c:24 + 8 * c], ones, DTA[:, c, :], start=True, stop=True)
                nc.tensor.matmul(b[:, 32:96], ones[0:32, :], DTAM[0:32].rearrange("p b h -> p (b h)"), start=True, stop=True)
                nc.tensor.matmul(b[0:32, 96:104], cst("tri_s", 32), DTA[0:32, 2, :], start=True, stop=True)
                nc.tensor.matmul(b[0:32, 104:112], cst("blk_s", 32), DTA[0:32, 2, :], start=True,
                                 stop=True).then_inc(kvT_mm, 1)

            for n in range(15):
                pe.wait_ge(ring_ld[n % 4], 16 * (n // 4 + 1))
                if 4 <= n < 7:
                    pe.wait_ge(hq_kept, n - 3)
                elif n >= 7:
                    pe.wait_ge(ch_kept, n - 6)
                for k in range(KC):
                    mm = nc.tensor.matmul(ps[n % 4][:, 0:T], WIN[:, n % 4, k, :], XT[:, k, :],
                                          start=(k == 0), stop=(k == KC - 1))
                mm.then_inc(piece_mm, 1)
                if n == 7:
                    latents()
                if n == 9:
                    log_decays()
            pe.wait_ge(ch_kept, 12)
            for h in range(H):
                if h >= 4:
                    pe.wait_ge(seg_ready, h - 3)
                    pe.wait_ge(e_ready, h - 3)
                for c in range(2):
                    nc.tensor.matmul(ps[h % 4][:, c * P:(c + 1) * P], DTA[:, c, h:h + 1].to_broadcast([P, P]),
                                     cst("tri"), start=True, stop=True)
                nc.tensor.matmul(ps[h % 4][:, SEQ:T], DTA[0:32, 2, h:h + 1].to_broadcast([32, P]),
                                 cst("tri_s", 32), start=True, stop=True).then_inc(row_mm, 1)
            pe.wait_ge(xb_ready, 1)
            pe.wait_ge(kvT_kept, 1)
            for t, (t0, nt) in enumerate(TILES):
                for k in range(4):
                    mm = nc.tensor.transpose(ps[4 + t][0:nt, k * P:(k + 1) * P], XB[:, k, t0:t0 + nt], ident)
                mm.then_inc(xs_mm, 1)
            for t, (t0, nt) in enumerate(TILES):
                pe.wait_ge(acs_kept, 1) if t == 0 else pe.wait_ge(dx_ready, t)
                bank = ps[7] if t == 0 else ps[3 + t]
                for k in range(2):
                    mm = nc.tensor.transpose(bank[0:nt, k * P:(k + 1) * P], XB[:, 4 + k, t0:t0 + nt], ident)
                mm.then_inc(bt_mm, 1)
            pe.wait_ge(dx_ready, 3)
            pe.wait_ge(bt_kept, 1)
            for g in range(2):
                bank = ps[6 + g]
                for c in range(2):
                    nc.tensor.matmul(bank[:, c * P:(c + 1) * P], XB[:, 4 + g, c * P:(c + 1) * P],
                                     XB[:, 6 + g, c * P:(c + 1) * P], start=True, stop=True)
                nc.tensor.matmul(bank[0:32, SEQ:T], XB[:, 4 + g, SEQ:T], XB[:, 6 + g, SEQ:T],
                                 start=True, stop=True).then_inc(cb_mm, 1)
            pe.wait_ge(seg_ready, H)
            pe.wait_ge(e_ready, H)
            pe.wait_ge(ld_h0, 16)
            for s in range(NB):
                for q in range(4):
                    mm = nc.tensor.matmul(ps[2][:, P + q * 32 + s * NS:P + q * 32 + (s + 1) * NS],
                                          H0[:, s, q * P:(q + 1) * P],
                                          XB[:, 6 + q // 2, SEQ + s * NS:SEQ + (s + 1) * NS], start=True, stop=True)
            mm.then_inc(yoff_mm, 1)
            pe.wait_ge(m_ready, 2)
            for c, (t0, nt) in enumerate(TILES):
                for h in range(H):
                    mm = nc.tensor.matmul(ps[c][64 * (h % 2):64 * (h % 2) + 64, (h // 2) * nt:(h // 2 + 1) * nt],
                                          DX[0:nt, c, h * 64:(h + 1) * 64], L[0:nt, h, t0:t0 + nt],
                                          start=True, stop=True)
                mm.then_inc(ydiag_mm, 1)
            pe.wait_ge(bt_kept, 3)
            for c in range(2):
                for g in range(2):
                    mm = nc.tensor.matmul(ps[4 + c][:, g * 256:(g + 1) * 256], BTOK[:, c, g * P:(g + 1) * P],
                                          DXE[:, c, g * 256:(g + 1) * 256], start=True, stop=True)
                mm.then_inc(state_mm, 1)
            pe.wait_ge(h1_ready, 1)
            for q in range(4):
                mm = nc.tensor.matmul(ps[3][:, q * P:(q + 1) * P], H1[:, q * P:(q + 1) * P],
                                      XB[:, 6 + q // 2, P:SEQ], start=True, stop=True)
            mm.then_inc(yoff_mm, 1)
            pe.wait_ge(sq_ready, 7)
            for g in range(2):
                for k in range(2):
                    mm = nc.tensor.matmul(ps[g][:, 0:T], ones, SQ[:, 2 * g + k, :], start=(k == 0), stop=(k == 1))
            mm.then_inc(sum_mm, 1)
            pe.wait_ge(bm_ready, 1)
            pe.wait_ge(h2_ready, 1)
            for s in range(NB):
                if s >= 3:
                    pe.wait_ge(sstate_kept, s - 2)
                for g in range(2):
                    mm = nc.tensor.matmul(ps[(7, 4, 5)[s % 3]][:, g * 256:(g + 1) * 256],
                                          BM[0:32, s, g * P:(g + 1) * P], DXE[0:32, 2, g * 256:(g + 1) * 256],
                                          start=True, stop=True)
                mm.then_inc(sstate_mm, 1)
            products_attention(pe)
            products_layer_out(pe, 0)
            products_conformer(pe)
            products_layer_out(pe, 1)

        @block.scalar
        def _(act):
            steps = Chain(act, act_step)
            act.wait_ge(ld_const, 32)
            act.wait_ge(zeroed, 1)
            for t, (t0, nt) in enumerate(TILES):
                act.wait_ge(tok_kept, 3)
                op = nc.scalar.activation(T1[0:nt, t, 0:R], TK[0:nt, t, 0:R], ACT.Square, accum_out=SS[0:nt, t:t + 1])
                op.then_inc(sq_ready, 1)
            for k in range(3):
                act.wait_ge(hq_kept, k + 1)
                nc.scalar.activation(SQ[:, k, :], HQ[:, k, :], ACT.Square).then_inc(sq_ready, 1)
            act.wait_ge(sq_ready, 3)
            nc.scalar.activation(RK, SS, ACT.Sqrt, bias=eps, scale=1.0 / R).then_inc(std_ready, 1)
            act.wait_ge(dt_z, 1)
            steps.step(nc.scalar.activation(T3, T3, ACT.Exp))
            nc.scalar.activation(NA, prm("a_log"), ACT.Exp)
            nc.scalar.activation(T3, T3, ACT.Ln, bias=1.0).then_inc(dt_ln, 1)
            for n in range(4):
                act.wait_ge(piece_mm, 4 + n)
                nc.scalar.activation(ZT[:, n, :], ps[(3 + n) % 4][:, 0:T], ACT.Silu).then_inc(ch_kept, 1)
            for n in range(8):
                act.wait_ge(piece_mm, 8 + n)
                bank = ps[(7 + n) % 4]
                if n == 1:
                    act.wait_ge(sum_mm, 1)
                    nc.scalar.activation(T1[:, 3, :], ps[7][:, 0:T], ACT.Sqrt, bias=eps, scale=1.0 / QL).then_inc(std_ready, 1)
                nc.scalar.copy(XP[:, n, 3:3 + SEQ], bank[:, 0:SEQ])
                nc.scalar.copy(XS[:, n, :, 3:7], bank[:, SEQ:T].rearrange("p (b s) -> p b s", s=NS)).then_inc(ch_kept, 1)
            for n in range(8):
                act.wait_ge(conv_ready, n + 1)
                op = nc.scalar.activation(XB[:, n, :], XB[:, n, :], ACT.Silu)
            op.then_inc(xb_ready, 1)
            act.wait_ge(acs_kept, 1)
            nc.scalar.activation(TOE[:, 0:16], TOE[:, 0:16], ACT.Exp)
            nc.scalar.activation(TOE[0:32, 16:24], TOE[0:32, 16:24], ACT.Exp)
            nc.scalar.activation(DEC, ACS[:, 16:96], ACT.Exp).then_inc(decay_ready, 1)
            for h in range(H):
                act.wait_ge(seg_ready, h + 1)
                lo = 64 * (h % 2)
                nc.scalar.activation(E[lo:lo + 64, h // 2, :], ps[h % 4][lo:lo + 64, 0:T], ACT.Exp).then_inc(e_ready, 1)
                nc.scalar.activation(L[:, h, 0:SEQ], L[:, h, 0:SEQ], ACT.Exp)
                nc.scalar.activation(L[0:32, h, SEQ:T], L[0:32, h, SEQ:T], ACT.Exp).then_inc(decay_ready, 1)
            for t, (t0, nt) in enumerate(TILES):
                act.wait_ge(bt_mm, t + 1)
                bank = ps[7] if t == 0 else ps[3 + t]
                nc.scalar.copy(BTOK[0:nt, t, :], bank[0:nt, 0:256]).then_inc(bt_kept, 1)
            act.wait_ge(state_mm, 1)
            nc.scalar.copy(H1, ps[4][:, :]).then_inc(h1_ready, 1)
            act.wait_ge(y_gated, 1)
            nc.scalar.activation(SQ, Y, ACT.Square).then_inc(sq_ready, 1)
            act.wait_ge(sum_mm, 2)
            for g in range(2):
                op = nc.scalar.activation(RG[:, g, :], ps[g][:, 0:T], ACT.Sqrt, bias=eps, scale=1.0 / 256)
            op.then_inc(std_ready, 1)
            act_attention(act, steps)
            act_layer_out(act, steps, 0)
            act_conformer(act, steps)
            act_layer_out(act, steps, 1)

        @block.vector
        def _(dve):
            steps = Chain(dve, dve_step)
            V = nc.vector
            dve.wait_ge(zeroed, 1)
            for t, (t0, nt) in enumerate(TILES):
                dve.wait_ge(tok_mm, t + 1)
                V.tensor_copy(TK[0:nt, t, :], ps[4 + t][0:nt, 0:296]).then_inc(tok_kept, 1)
            for k in range(3):
                dve.wait_ge(piece_mm, k + 1)
                V.tensor_copy(HQ[:, k, :], ps[k][:, 0:T]).then_inc(hq_kept, 1)
            dve.wait_ge(ld_const, 32)
            dve.wait_ge(tok_kept, 3)
            co = cst("cos").rearrange("p (t f) -> p t f", t=3)
            si = cst("sin").rearrange("p (t f) -> p t f", t=3)
            ka, kb = TK[:, :, 256:272], TK[:, :, 272:288]
            V.tensor_tensor(KPE[:, :, 0:16], ka, co, ALU.mult)
            V.tensor_tensor(KPE[:, :, 16:32], kb, co, ALU.mult)
            V.tensor_tensor(KT[:, :, 0:16], kb, si, ALU.mult)
            steps.step(V.tensor_tensor(KT[:, :, 16:32], ka, si, ALU.mult))
            V.tensor_tensor(KPE[:, :, 0:16], KPE[:, :, 0:16], KT[:, :, 0:16], ALU.subtract)
            steps.step(V.tensor_tensor(KPE[:, :, 16:32], KPE[:, :, 16:32], KT[:, :, 16:32], ALU.add))
            steps.step(V.tensor_tensor(TDT, TK[:, :, 288:296], prm("dt_bias").unsqueeze(1).to_broadcast([P, 3, 8]),
                                       ALU.add))
            V.scalar_tensor_tensor(T3, TDT, -1.0, TDT, ALU.mult, ALU.min).then_inc(dt_z, 1)
            dve.wait_ge(std_ready, 1)
            steps.step(V.reciprocal(RK, RK))
            for t, (t0, nt) in enumerate(TILES):
                op = V.scalar_tensor_tensor(CK[0:nt, t, :], TK[0:nt, t, 0:R], RK[0:nt, t:t + 1], prm("g_kv")[0:nt],
                                            ALU.mult, ALU.mult)
            op.then_inc(kv_ready, 1)
            dve.wait_ge(dt_ln, 1)
            steps.step(V.scalar_tensor_tensor(DT, TDT, 0.0, T3, ALU.max, ALU.add))
            steps.step(V.tensor_tensor(DTA, DT, NA.unsqueeze(1).to_broadcast([P, 3, 8]), ALU.mult))
            steps.step(V.tensor_scalar(DTA, DTA, -1.0, None, ALU.mult))
            V.tensor_tensor(DTAM[0:32], DTA[0:32, 2, :].unsqueeze(1).to_broadcast([32, NB, 8]),
                            cst("bmask", 32).unsqueeze(2).to_broadcast([32, NB, 8]), ALU.mult).then_inc(dtA_ready, 1)
            dve.wait_ge(ld_hist, 16)
            cw = prm("conv_w").rearrange("p (c k) -> p c k", k=4)
            cb = prm("conv_b")
            for n in range(8):
                dve.wait_ge(ch_kept, 5 + n)
                xsv = CS[:, n, :].rearrange("p (b s) -> p b s", s=NS)
                V.tensor_scalar(XB[:, n, 0:SEQ], XP[:, n, 0:SEQ], cw[:, n, 0:1], cb[:, n:n + 1], ALU.mult, ALU.add)
                steps.step(V.tensor_scalar(xsv, XS[:, n, :, 0:4], cw[:, n, 0:1], cb[:, n:n + 1], ALU.mult, ALU.add))
                for k in range(1, 4):
                    V.scalar_tensor_tensor(XB[:, n, 0:SEQ], XP[:, n, k:k + SEQ], cw[:, n, k:k + 1], XB[:, n, 0:SEQ],
                                           ALU.mult, ALU.add)
                    dst = xsv if k < 3 else XB[:, n, SEQ:T].rearrange("p (b s) -> p b s", s=NS)
                    op = V.scalar_tensor_tensor(dst, XS[:, n, :, k:k + 4], cw[:, n, k:k + 1], xsv, ALU.mult, ALU.add)
                    steps.step(op) if k < 3 else op.then_inc(conv_ready, 1)
                if n == 3:
                    dve.wait_ge(std_ready, 2)
                    steps.step(V.reciprocal(T1[:, 3, :], T1[:, 3, :]))
                    for k in range(3):
                        op = V.scalar_tensor_tensor(HQ[:, k, :], HQ[:, k, :], prm("g_q")[:, k:k + 1], T1[:, 3, :],
                                                    ALU.mult, ALU.mult)
                    op.then_inc(hq_ready, 1)
                if n == 5:
                    dve.wait_ge(kvT_mm, 1)
                    for r in range(2):
                        V.tensor_copy(CKT[:, r, :], ps[4 + r][:, 0:T])
                    V.tensor_copy(KPT[0:32], ps[6][0:32, 0:T]).then_inc(kvT_kept, 1)
            dve.wait_ge(kvT_mm, 2)
            V.tensor_copy(ACS[:, 0:96], ps[7][:, 0:96])
            steps.step(V.tensor_copy(ACS[0:32, 96:112], ps[7][0:32, 96:112]))
            V.tensor_tensor(TOE[:, 0:16], ACS[:, 16:32], ACS[:, 0:16], ALU.subtract)
            V.tensor_tensor(TOE[0:32, 16:24], ACS[0:32, 104:112], ACS[0:32, 96:104], ALU.subtract).then_inc(acs_kept, 1)
            for h in range(H):
                dve.wait_ge(row_mm, h + 1)
                for c in range(2):
                    V.scalar_tensor_tensor(L[:, h, c * P:(c + 1) * P], ps[h % 4][:, c * P:(c + 1) * P],
                                           ACS[:, 8 * c + h:8 * c + h + 1], cst("mask_ssd"), ALU.subtract, ALU.add)
                V.scalar_tensor_tensor(L[0:32, h, SEQ:T], ps[h % 4][0:32, SEQ:T], ACS[0:32, 96 + h:97 + h],
                                       cst("mask_ssd_s", 32), ALU.subtract, ALU.add).then_inc(seg_ready, 1)
            dve.wait_ge(decay_ready, 1)
            for t, (t0, nt) in enumerate(TILES):
                dve.wait_ge(xs_mm, t + 1)
                dxv = DX[0:nt, t, :].rearrange("p (h d) -> p h d", h=H)
                steps.step(V.tensor_tensor(dxv, ps[4 + t][0:nt, :].rearrange("p (h d) -> p h d", h=H),
                                           DT[0:nt, t, :].unsqueeze(2).to_broadcast([nt, H, 64]), ALU.mult))
                V.tensor_tensor(DXE[0:nt, t, :].rearrange("p (h d) -> p h d", h=H), dxv,
                                TOE[0:nt, 8 * t:8 * t + 8].unsqueeze(2).to_broadcast([nt, H, 64]),
                                ALU.mult).then_inc(dx_ready, 1)
            dve.wait_ge(decay_ready, H + 1)
            for g in range(2):
                dve.wait_ge(cb_mm, g + 1)
                for c, (t0, nt) in enumerate(TILES):
                    lv = L[0:nt, 4 * g:4 * g + 4, t0:t0 + nt]
                    op = V.tensor_tensor(lv, lv, ps[6 + g][0:nt, t0:t0 + nt].unsqueeze(1).to_broadcast([nt, 4, nt]), ALU.mult)
                op.then_inc(m_ready, 1)
            for q in range(4):
                op = V.tensor_scalar(Y[:, q, :], XB[:, q, :], prm("d_skip")[:, q:q + 1], None, ALU.mult)
            steps.step(op)
            for c, (t0, nt) in enumerate(TILES):
                dve.wait_ge(ydiag_mm, c + 1)
                yv = Y[:, :, t0:t0 + nt]
                op = V.tensor_tensor(yv, yv, ps[c][:, 0:4 * nt].rearrange("p (q t) -> p q t", q=4), ALU.add)
            steps.step(op)
            for c, off in ((2, ps[2][:, P:2 * P]), (1, ps[3][:, :])):
                t0, nt = TILES[c]
                dve.wait_ge(yoff_mm, 3 - c)
                dve.wait_ge(e_ready, H)
                steps.step(V.tensor_tensor(T1[:, :, t0:t0 + nt], E[:, :, t0:t0 + nt],
                                           off.rearrange("p (q t) -> p q t", q=4), ALU.mult))
                steps.step(V.tensor_tensor(Y[:, :, t0:t0 + nt], Y[:, :, t0:t0 + nt], T1[:, :, t0:t0 + nt], ALU.add))
            V.tensor_tensor(Y, Y, ZT, ALU.mult).then_inc(y_gated, 1)
            dve.wait_ge(h1_ready, 1)
            dve.wait_ge(state_mm, 2)
            h2v = H2.rearrange("p (h d) -> p h d", h=H)
            steps.step(V.tensor_tensor(h2v, H1.rearrange("p (h d) -> p h d", h=H),
                                       DEC[:, 8:16].unsqueeze(2).to_broadcast([P, H, 64]), ALU.mult))
            V.tensor_tensor(H2, H2, ps[5][:, :], ALU.add).then_inc(h2_ready, 1)
            dve.wait_ge(bm_ready, 2)
            for s in range(NB):
                dve.wait_ge(sstate_mm, s + 1)
                V.tensor_tensor(H0[:, s, :], H0[:, s, :], ps[(7, 4, 5)[s % 3]][:, :], ALU.add).then_inc(sstate_kept, 1)
            dve.wait_ge(std_ready, 3)
            steps.step(V.reciprocal(RG, RG))
            for q in range(4):
                op = V.scalar_tensor_tensor(CAT[:, 4 + q, :], Y[:, q, :], prm("g_y")[:, q:q + 1], RG[:, q // 2, :],
                                            ALU.mult, ALU.mult)
            op.then_inc(y_ready, 1)
            dve_attention(dve, steps)
            dve_layer_out(dve, steps, 0)
            dve_conformer(dve, steps)
            dve_layer_out(dve, steps, 1)

        @block.gpsimd
        def _(pool):
            G = nc.gpsimd
            G.memset(XS[:], 0.0)
            G.memset(XP[:, :, 0:3], 0.0)
            G.memset(SS, 1.0)
            G.memset(X[:, 2, :], 0.0)
            G.memset(TK[:, 2, :], 0.0).then_inc(zeroed, 1)

            pool.dma_start(pages[0:1, :], a["pages"]).then_inc(ld_pages, 16)

            def store(dst, src, done=None):
                if done is None:
                    n_stored[0] += 1
                pool.dma_start(dst, src).then_inc(stored if done is None else done, 16)

            pool.wait_ge(kv_ready, 1)
            for t in range(2):
                store(o["ckv_p"][t * P:(t + 1) * P], CK[:, t, :], ckv_stored)
                store(o["kpe_p"][t * P:(t + 1) * P], KPE[:, t, :])
            store(o["ckv_s"], CK[0:32, 2, :], ckv_stored)
            store(o["kpe_s"], KPE[0:32, 2, :])
            pool.wait_ge(ch_kept, 12)
            pool.wait_ge(ld_hist, 16)
            store(o["sconv_p"], XP[:, :, SEQ:SEQ + 3], conv_stored)
            store(o["sconv_s"], XS[:, :, :, 4:7], conv_stored)
            pool.wait_ge(bt_kept, 3)
            G.tensor_tensor(BM[0:32], BTOK[0:32, 2, :].unsqueeze(1).to_broadcast([32, NB, 256]),
                            cst("bmask", 32).unsqueeze(2).to_broadcast([32, NB, 256]), ALU.mult).then_inc(bm_ready, 1)
            pool.wait_ge(yoff_mm, 1)
            pool.wait_ge(decay_ready, 1)
            h0v = H0.rearrange("p b (h d) -> p (b h) d", d=64)
            G.tensor_tensor(h0v, h0v, DEC[:, 16:80].unsqueeze(2).to_broadcast([P, 64, 64]), ALU.mult).then_inc(bm_ready, 1)
            pool.wait_ge(h2_ready, 1)
            store(o["ssm_p"], H2, h2_stored)
            pool.wait_ge(sstate_kept, NB)
            store(o["ssm_s"], H0, h0_stored)
            pool_layer_out(pool, store, 0)
            pool_conformer(pool, store)
            pool_layer_out(pool, store, 1)
            pool.wait_ge(stored, 16 * n_stored[0])
            pool.wait_ge(ckv_stored, 48)
            pool.wait_ge(h2_stored, 16)
            pool.wait_ge(h0_stored, 16)
            pool.wait_ge(conv_stored, 64)


INPUTS = [("x", (T, D)), ("xT", (P, KC, T)), ("w_tok", (P, KC, 296)), ("w_ch", (15, P, KC, P)), ("consts", (P, NCONST)),
          ("params", (P, NPARAM)), ("conv_hist", (P, KC, NB, 3)), ("w_q", (P, 4352)), ("state", (P, NB, 512)),
          ("cache", (160, P, R + E_PE)), ("pages", (1, NB * NP)),
          ("w_out", (P, KC, D)), ("rows", (5, P, D)), ("rows_b", (4, P, D)), ("w_moe", (2, NE, P, 6144)),
          ("w_conf", (16, P, KC, P)), ("conf_hist", (P, KC, HIST, NB)), ("w_conf_out", (P, KC, D)),
          ("nobody", (SLOT_ROWS, 1)), ("token_ids", (P, 3))]
OUTPUTS = [("y", (T, D)), ("ckv_p", (SEQ, R)), ("kpe_p", (SEQ, E_PE)), ("ssm_p", (P, 512)), ("sconv_p", (P, KC, 3)),
           ("cconv_p", (P, KC, HIST)), ("ckv_s", (32, R)), ("kpe_s", (32, E_PE)), ("ssm_s", (P, NB, 512)),
           ("sconv_s", (P, KC, NB, 3)), ("cconv_s", (P, KC, HIST, NB))]
INT_INPUTS = ("pages", "nobody", "token_ids")


def lay_out(v):
    f = np.ascontiguousarray
    chunks = lambda w: f(w.reshape(-1, P, w.shape[-1]).transpose(1, 0, 2))
    cols = lambda x: f(x.reshape(-1, P).T)
    bcast = lambda x: np.broadcast_to(x, (P,) + x.shape)
    w = v["w_in_ab"][0]
    x = np.concatenate([v["x_prompt"][0], v["x_sample"].reshape(32, D)])
    d = {"x": x, "xT": chunks(f(x.T)), "consts": constants()}
    d["w_tok"] = chunks(np.concatenate([w[:, 384:672], w[:, 2208:2216]], axis=1))
    w_ch = np.concatenate([w[:, 0:384], w[:, 672:2208]], axis=1)
    pieces = lambda m: f(m.reshape(KC, P, -1, P).transpose(2, 1, 0, 3))
    d["w_ch"] = pieces(w_ch)
    uq = v["w_uq"][0]
    uqn = chunks(f(uq[:, :, :64].reshape(QL, 512))).reshape(P, -1)
    uqp = chunks(f(uq[:, :, 64:].reshape(QL, 256))).reshape(P, -1)
    uk = f(v["w_uk"][0].transpose(1, 2, 0).reshape(4, P, R).transpose(1, 0, 2)).reshape(P, -1)
    uv = chunks(v["w_uv"][0].reshape(R, 512)).reshape(P, -1)
    d["w_q"] = np.concatenate([uqn, uqp, uk, uv], axis=1)
    d["conv_hist"] = f(v["state_ssm_conv"][0].reshape(NB, 3, KC, P).transpose(3, 2, 0, 1))
    d["state"] = f(v["state_ssm"][0].transpose(3, 0, 1, 2).reshape(P, NB, 512))
    d["cache"] = np.concatenate([v["cache_ckv"][0], v["cache_kpe"][0]], axis=2)
    d["pages"] = f(v["page_table"].reshape(2, 4, NP // 2, 2).transpose(0, 2, 1, 3))
    d["w_out"] = chunks(v["w_out_ab"][0])
    d["rows"] = np.stack([bcast(r) for r in (v["ln_mix_g"][0], v["ln_ffn_g"][0], v["ln_mix_g"][1], v["ln_ffn_g"][1],
                                             v["conf_b_out"][0])])
    d["rows_b"] = np.stack([bcast(r) for r in (v["ln_mix_b"][0], v["ln_ffn_b"][0], v["ln_mix_b"][1], v["ln_ffn_b"][1])])
    halves = lambda m: m.reshape(2, NE, KC, P, 2, 1, P)
    gu = np.concatenate([halves(v["moe_w_gate"]), halves(v["moe_w_up"])], axis=5)
    gu = gu.transpose(0, 1, 3, 2, 4, 5, 6).reshape(2, NE, P, 4096)
    down = v["moe_w_down"].reshape(2, NE, 2, P, D).transpose(0, 1, 3, 2, 4).reshape(2, NE, P, 2048)
    d["w_moe"] = np.concatenate([gu, down], axis=3)
    d["w_conf"] = pieces(v["conf_w_in"][0])
    d["conf_hist"] = f(v["state_conf_conv"][0].reshape(NB, HIST, KC, P).transpose(3, 2, 1, 0))
    d["w_conf_out"] = chunks(v["conf_w_out"][0])
    d["nobody"] = np.full((SLOT_ROWS, 1), NOBODY, np.int32)
    ids = np.arange(3 * P, dtype=np.int32).reshape(3, P).T
    d["token_ids"] = f(ids)
    taps = lambda x: f(x.T.reshape(KC, P, -1).transpose(1, 0, 2)).reshape(P, -1)
    parts = {"g_q": cols(v["g_q_norm"][0]), "conv_w": taps(v["ssm_conv_w"][0]), "conv_b": cols(v["ssm_conv_b"][0]),
             "g_y": cols(v["ssm_norm_g"][0]), "d_skip": cols(np.repeat(v["ssm_d"][0], 64)),
             "dt_bias": bcast(v["ssm_dt_bias"][0]), "a_log": bcast(v["ssm_a_log"][0]), "b_in": cols(v["conf_b_in"][0]),
             "dw_w": taps(v["conf_dw_w"][0]), "dw_b": cols(v["conf_dw_b"][0]), "gn": cols(v["conf_norm_g"][0]),
             "bn": cols(v["conf_norm_b"][0]), "r_bias": bcast(v["router_bias"]),
             "w_router": chunks(v["w_router"]).reshape(P, -1), "g_kv": bcast(v["g_kv_norm"][0])}
    d["params"] = np.concatenate([parts[name] for name in PARAM], axis=1)
    return d


def kernel(**inputs):
    from concourse import bacc
    from concourse.bass_utils import run_bass_kernel_spmd

    nc = bacc.Bacc("TRN2", target_bir_lowering=False, num_devices=1)
    laid = lay_out({k: np.asarray(x) for k, x in inputs.items()})
    arrays, a, o = {}, {}, {}
    for name, shape in INPUTS:
        arrays[f"in_{name}"] = np.ascontiguousarray(laid[name].reshape(shape))
        dt = I32 if name in INT_INPUTS else F32
        a[name] = nc.dram_tensor(f"in_{name}", shape, dt, kind="ExternalInput").ap()
    for name, shape in OUTPUTS:
        o[name] = nc.dram_tensor(f"out_{name}", shape, F32, kind="ExternalOutput").ap()
    hybrid_trunk(nc, a, o)
    res = run_bass_kernel_spmd(nc, [arrays], core_ids=[0]).results[0]
    r = {name: np.asarray(res[f"out_{name}"]) for name, _ in OUTPUTS}
    rows = lambda x: x.transpose(2, 1, 0).reshape(1, 1, x.shape[2], -1)
    srows = lambda x: x.transpose(2, 3, 1, 0).reshape(1, NB, x.shape[3], -1)
    return (r["y"][:SEQ].reshape(1, SEQ, D), r["y"][SEQ:].reshape(NB, NS, D),
            r["ckv_p"].reshape(1, 1, SEQ, R), r["kpe_p"].reshape(1, 1, SEQ, E_PE),
            r["ssm_p"].reshape(P, 8, 64).transpose(1, 2, 0).reshape(1, 1, 8, 64, P), rows(r["sconv_p"]),
            rows(r["cconv_p"]), r["ckv_s"].reshape(1, NB, NS, R), r["kpe_s"].reshape(1, NB, NS, E_PE),
            r["ssm_s"].reshape(P, NB, 8, 64).transpose(1, 2, 3, 0).reshape(1, NB, 8, 64, P),
            srows(r["sconv_s"]), srows(r["cconv_s"].transpose(0, 1, 3, 2)))
```

```python
from contextlib import ExitStack

import numpy as np

import concourse.bass as bass
from concourse import mybir

F32 = mybir.dt.float32
I32 = mybir.dt.int32
ALU = mybir.AluOpType
ACT = mybir.ActivationFunctionType
AX = mybir.AxisListType.X

P = 128
D = 1024
KC = D // P
SEQ = 256
NB, NS = 8, 4
T = SEQ + NB * NS
TILES = ((0, 128), (128, 128), (256, 32))
H = 8
QL, R, E_PE, VD = 384, 256, 32, 64
NP = 16
NEG = -1.0e30
EPS = 1e-6
ALPHA = 4.0 ** 0.25
SCALE = 96.0 ** -0.5
NE = 16
CAP = 64
MAX_EXTRA = 8
SLOT_ROWS = (NE + MAX_EXTRA) * CAP
NOBODY = 1 << 20
KW = 31
HIST = KW - 1


def const_layout():
    widths = [("ident", P), ("ones", P), ("tri", P), ("tri_strict", P), ("mask_ssd", P), ("mask_q", P),
              ("tri_s", 32), ("blk_s", 32), ("mask_ssd_s", 32), ("bmask", NB), ("own_rows", 64), ("mask_new", 64),
              ("cos", 48), ("sin", 48), ("row_of", NE), ("base_of", NE), ("earlier", 16), ("later", 16), ("valid", 3),
              ("eps", 1), ("item_thr", 64), ("item_k", MAX_EXTRA)]
    at, cols = 0, {}
    for name, w in widths:
        cols[name] = (at, at + w)
        at += w
    return cols, at


CONST, NCONST = const_layout()


def constants():
    c = np.zeros((P, NCONST), np.float32)
    i = np.arange(P)

    def put(name, value):
        a, b = CONST[name]
        value = np.asarray(value, np.float32)
        c[:value.shape[0], a:b] = value.reshape(value.shape[0], b - a)

    put("ident", np.eye(P))
    put("ones", np.ones((P, P)))
    put("tri", i[:, None] <= i[None, :])
    put("tri_strict", i[:, None] < i[None, :])
    put("mask_ssd", np.where(i[:, None] <= i[None, :], 0.0, NEG))
    put("mask_q", np.where(i[None, :] <= i[:, None], 0.0, NEG))
    k = np.arange(32)
    same = (k[:, None] // NS) == (k[None, :] // NS)
    put("tri_s", same & (k[:, None] <= k[None, :]))
    put("blk_s", same)
    put("mask_ssd_s", np.where(same & (k[:, None] <= k[None, :]), 0.0, NEG))
    put("bmask", (k[:, None] // NS) == np.arange(NB)[None, :])
    own = np.zeros((P, 2, 32))
    for g in range(2):
        own[:, g] = (i[:, None] % 32 == k[None, :]) & (k[None, :] // NS == 4 * g + i[:, None] // 32)
    put("own_rows", own)
    row_b, row_s = i // 32, i % NS
    new = np.zeros((P, 2, 32), np.float32)
    for g in range(2):
        ok = ((k[None, :] // NS) == (4 * g + row_b[:, None])) & ((k[None, :] % NS) <= row_s[:, None])
        new[:, g] = np.where(ok, 0.0, NEG)
    put("mask_new", new)
    pos = np.zeros((P, 3))
    pos[:, 0], pos[:, 1] = i, i + P
    pos[:32, 2] = NP * P + k % NS
    inv = np.float32(10000.0) ** (-np.arange(16, dtype=np.float32) / np.float32(16))
    ang = pos.astype(np.float32)[:, :, None] * inv[None, None, :]
    put("cos", np.cos(ang))
    put("sin", np.sin(ang))
    put("row_of", np.broadcast_to(np.arange(NE) * CAP, (P, NE)))
    put("base_of", np.broadcast_to((NE - 1) * CAP - np.arange(NE) * CAP, (P, NE)))
    four = np.arange(4)
    put("earlier", np.broadcast_to((four[None, :] < four[:, None]).reshape(-1), (P, 16)))
    put("later", np.broadcast_to((four[None, :] >= four[:, None]).reshape(-1), (P, 16)))
    valid = np.ones((P, 3))
    valid[32:, 2] = 0
    put("valid", valid)
    put("eps", np.full((P, 1), EPS))
    put("item_thr", np.broadcast_to(np.tile(np.arange(1, 5) * CAP, NE), (P, 64)))
    put("item_k", np.broadcast_to(np.arange(MAX_EXTRA), (P, MAX_EXTRA)))
    return c


def param_layout():
    widths = [("g_q", 3), ("conv_w", 32), ("conv_b", 8), ("g_y", 4), ("d_skip", 4), ("dt_bias", 8),
              ("a_log", 8), ("b_in", 16), ("dw_w", 8 * KW), ("dw_b", 8), ("gn", 8), ("bn", 8),
              ("r_bias", NE), ("w_router", KC * NE), ("g_kv", R)]
    at, cols = 0, {}
    for name, w in widths:
        cols[name] = (at, at + w)
        at += w
    return cols, at


PARAM, NPARAM = param_layout()


class Chain:

    def __init__(self, engine, sem):
        self.engine, self.sem, self.count = engine, sem, 0

    def step(self, instruction):
        self.count += 1
        instruction.then_inc(self.sem, 1)
        self.engine.wait_ge(self.sem, self.count)


def hybrid_trunk(nc, a, o):
    ctx = ExitStack()
    with ctx:
        def sb(name, cols, dt=F32):
            return ctx.enter_context(nc.sbuf_tensor(name, [P, cols], dt))

        def sem(name):
            return ctx.enter_context(nc.semaphore(name))

        ps = [ctx.enter_context(nc.psum_tensor(f"bank{i}", [P, 512], F32)) for i in range(8)]
        X = sb("x_tok", 3 * D)[:].rearrange("p (t d) -> p t d", t=3)
        xT_t = sb("x_ch", KC * T)
        XT = xT_t[:].rearrange("p (c t) -> p c t", c=KC)
        ROWS = sb("rows", 2 * D)[:].rearrange("p (r d) -> p r d", r=2)
        C = sb("consts", NCONST)
        PM = sb("params", NPARAM)
        slot_t = sb("slots", 3 * 6144)
        M = sb("mixer", 24472)
        small = sb("small", 640)
        ints = sb("ints", 64, I32)

        def cst(name, rows=P):
            lo, hi = CONST[name]
            return C[0:rows, lo:hi]

        def prm(name):
            lo, hi = PARAM[name]
            return PM[:, lo:hi]

        def at(t, off, *dims):
            n = int(np.prod(dims))
            v = t[:, off:off + n]
            if len(dims) == 1:
                return v
            names = "abcd"[:len(dims)]
            return v.rearrange(f"p ({' '.join(names)}) -> p {' '.join(names)}", **dict(zip(names[1:], dims[1:])))

        ident, ones = cst("ident"), cst("ones")

        WUQN = at(slot_t, 0, 3, 4, P)
        WUQP = at(slot_t, 1536, 3, 256)
        WUK = at(slot_t, 2304, 4, R)
        WUV = at(slot_t, 3328, 2, H * VD)
        CK = at(slot_t, 4352, 3, R)
        CKT = at(slot_t, 5120, 2, T)
        KPT = at(slot_t, 5696, T)
        S1 = 6144
        DX = at(slot_t, S1, 3, 512)
        DXE = at(slot_t, S1 + 1536, 3, 512)
        BTOK = at(slot_t, S1 + 3072, 3, 256)
        BM = at(slot_t, S1 + 3840, NB, 256)
        L = at(slot_t, S1 + 5888, H, T)
        E = at(slot_t, S1 + 8192, 4, T)
        H1 = at(slot_t, S1 + 9344, 512)
        H2 = at(slot_t, S1 + 9856, 512)
        Y = at(slot_t, S1 + 10368, 4, T)
        RG = at(slot_t, S1 + 11520, 2, T)
        WIN = at(M, 0, 4, KC, P)
        WTOK = at(M, 4096, KC, 296)
        H0 = at(M, 0, NB, 512)
        T1 = at(M, 4096, 4, T)
        SQ = at(M, 5248, 4, T)
        TK = at(M, 6464, 3, 296)
        HQ = at(M, 7352, 3, T)
        CAT = at(M, 8216, KC, T)
        QN = at(M, 10520, 4, T)
        QA = at(M, 11672, 2, H, T)
        YO = at(M, 11672, 2, 512)
        XP = at(M, 16280, KC, 3 + SEQ)
        XS = at(M, 18352, KC, NB, 7)
        XB = at(M, 18800, KC, T)
        ZT = at(M, 21104, 4, T)
        CS = at(M, 22256, KC, NB * NS)
        QPT = at(M, 22512, 3, 256)
        TMP = at(M, 23280, 4, 128)
        WOUT = at(M, 16280, KC, D)
        QP = at(xT_t, 0, H, T)
        S = at(M, 0, 2080)
        PT = at(M, 2080, NP, P)
        PNT = at(M, 4128, P)
        OS = at(M, 4256, R)
        PP = at(M, 4512, 2, 384)
        PPT = at(M, 5280, 2, 384)

        SS, RK, TDT = small[:, 0:3], small[:, 3:6], at(small, 8, 3, 8)
        DT, DTA, T3 = at(small, 32, 3, 8), at(small, 56, 3, 8), at(small, 80, 3, 8)
        NA = small[:, 104:112]
        ACS, TOE, DEC = small[:, 112:224], small[:, 224:248], small[:, 248:328]
        DTAM = at(small, 328, NB, 8)
        KPE = at(small, 392, 3, 32)
        KT = at(small, 488, 3, 32)
        MXP, RSP = at(small, 600, 2, 4), at(small, 608, 2, 4)
        MXS, RSS = small[:, 616:620], small[:, 620:624]
        MX5, RS5 = small[:, 624:629], small[:, 629:634]

        ld_const, ld_x, ld_in0, ld_in1, ld_wq, ld_hist = map(sem, (
            "ld_const", "ld_x", "ld_in0", "ld_in1", "ld_wq", "ld_hist"))
        ld_h0, ld_wout, ld_rows = map(sem, ("ld_h0", "ld_wout", "ld_rows"))
        ring_ld = [sem(f"ring_ld{i}") for i in range(4)]
        zeroed, tok_mm, tok_kept, piece_mm, hq_kept, ch_kept = map(sem, (
            "zeroed", "tok_mm", "tok_kept", "piece_mm", "hq_kept", "ch_kept"))
        sq_ready, sum_mm, std_ready, hq_ready, kv_ready, kvT_mm, kvT_kept = map(sem, (
            "sq_ready", "sum_mm", "std_ready", "hq_ready", "kv_ready", "kvT_mm", "kvT_kept"))
        conv_ready, xb_ready, dt_z, dt_ln, dtA_ready = map(sem, (
            "conv_ready", "xb_ready", "dt_z", "dt_ln", "dtA_ready"))
        acs_kept, row_mm, seg_ready, decay_ready, e_ready = map(sem, (
            "acs_kept", "row_mm", "seg_ready", "decay_ready", "e_ready"))
        xs_mm, dx_ready, bt_mm, bt_kept, bm_ready, cb_mm, m_ready = map(sem, (
            "xs_mm", "dx_ready", "bt_mm", "bt_kept", "bm_ready", "cb_mm", "m_ready"))
        ydiag_mm, state_mm, h1_ready, yoff_mm, h2_ready, sstate_mm, sstate_kept = map(sem, (
            "ydiag_mm", "state_mm", "h1_ready", "yoff_mm", "h2_ready", "sstate_mm", "sstate_kept"))
        y_gated, y_ready = map(sem, ("y_gated", "y_ready"))
        stored = sem("stored")
        dve_step, act_step, pool_step = map(sem, ("dve_step", "act_step", "pool_step"))
        n_stored = [0]

        eps = cst("eps")

        qn_mm, q_kept, kvT_act, qa_mm, qa_act, qa_dve, qpT_mm, qpT_kept = map(sem, (
            "qn_mm", "q_kept", "kvT_act", "qa_mm", "qa_act", "qa_dve", "qpT_mm", "qpT_kept"))
        pscore_mm, pmax_ready, pexp_ready, prob_ready, probT_mm, probT_kept, po_mm, po_kept = map(sem, (
            "pscore_mm", "pmax_ready", "pexp_ready", "prob_ready", "probT_mm", "probT_kept", "po_mm",
            "po_kept"))
        s_mm, s_kept, s_new, s_max, s_exp, sT_mm, sT_kept, so_mm, so_kept, soT_mm, soT_kept = map(sem, (
            "s_mm", "s_kept", "s_new", "s_max", "s_exp", "sT_mm", "sT_kept", "so_mm", "so_kept", "soT_mm", "soT_kept"))
        slot_ld = [sem(f"slot_ld{n}") for n in range(6)]
        kv_ld = ring_ld + slot_ld[0:4]
        v_used, omla_mm, cat_kept, h2_stored, h0_stored, ckv_stored, conv_stored, ld_pages = map(sem, (
            "v_used", "omla_mm", "cat_kept", "h2_stored", "h0_stored", "ckv_stored", "conv_stored", "ld_pages"))
        QAS = at(M, 6464, 2, NB, 32)
        QPS = at(M, 6976, NB, 32)
        pages = sb("pages", NB * NP, I32)

        NCH, ROW = 8, R + E_PE
        PAGES = [at(slot_t, 6144 + n * 8 * ROW, 4, 2, ROW) for n in (3, 0, 1, 2, 4)] + [
            at(M, 16280 + n * 8 * ROW, 4, 2, ROW) for n in range(3)]
        V_ORDER = ((0, 1, 2, 3, 4, 5, 6, 7), (5, 6, 7, 0, 1, 2, 3, 4))
        KTR = [at(slot_t, 0, 4, 2, 256), ROWS.rearrange("p a (b t) -> p (a b) t", t=256).rearrange("p (j r) t -> p j r t", r=2)]
        KTE = [at(M, 23192, 2, 512), at(M, 10520, 2, 512)]

        def chunk_loaded(g, c):
            before_ = 16 * len(range(c, 15, 4)) if c < 4 else 0
            return before_ + 128 * (g + 1)

        def loads_attention(sp):
            sp.wait_ge(ld_pages, 16)
            for g in range(2):
                for c in range(NCH):
                    if g == 0 and c == 0:
                        sp.wait_ge(y_gated, 1)
                    if g == 0 and c == 1:
                        sp.wait_ge(sstate_mm, NB)
                    if g == 0 and c == 4:
                        sp.wait_ge(y_ready, 1)
                        sp.wait_ge(h2_stored, 16)
                    if g == 0 and c == 5:
                        sp.wait_ge(conv_stored, 32)
                        sp.wait_ge(qpT_mm, 5)
                    if g == 1:
                        sp.wait_ge(v_used, c + 1)
                    for half_ in range(2):
                        lo = (g * NCH + c) * 8 + 4 * half_
                        _, page = nc.values_load_multi_w_load_instructions(
                            pages[0:1, lo:lo + 4], engines=[mybir.EngineType.SP], min_val=0, max_val=159)
                        for n in range(4):
                            sp.dma_start(PAGES[c][:, 2 * half_ + n // 2, n % 2, :],
                                         a["cache"][bass.ds(page[n], 1)].rearrange("a p r -> (a p) r")
                                         ).then_inc(kv_ld[c], 16)
            sp.wait_ge(v_used, NCH + 3)
            sp.dma_start(ROWS[:, 0, :], a["rows"][0]).then_inc(ld_rows, 16)
            sp.dma_start(ROWS[:, 1, :], a["rows_b"][0]).then_inc(ld_rows, 16)
            sp.dma_start(WOUT, a["w_out"]).then_inc(ld_wout, 16)

        QN_BANKS = (7, 2, 3, 6)

        def query_products(pe):
            pe.wait_ge(hq_ready, 1)
            pe.wait_ge(ld_wq, 16)
            for n in range(4):
                if n == 1:
                    pe.wait_ge(y_gated, 1)
                for k in range(3):
                    mm = nc.tensor.matmul(ps[QN_BANKS[n]][:, 0:T], WUQN[:, k, n, :], HQ[:, k, :], start=(k == 0),
                                          stop=(k == 2))
                mm.then_inc(qn_mm, 1)

        def products_attention(pe):
            pe.wait_ge(std_ready, 3)
            pe.wait_ge(sstate_kept, NB)
            pe.wait_ge(q_kept, 4)
            for t, (t0, nt) in enumerate(TILES):
                for k in range(3):
                    mm = nc.tensor.matmul(ps[4 + t][0:nt, 0:256], HQ[:, k, t0:t0 + nt], WUQP[:, k, :],
                                          start=(k == 0), stop=(k == 2))
                mm.then_inc(qn_mm, 1)
            for p in range(H // 2):
                for r, h in ((0, 2 * p), (0, 2 * p + 1), (1, 2 * p), (1, 2 * p + 1)):
                    lo = 64 * (h % 2)
                    n = 2 * h + r
                    if n < 4:
                        pe.wait_ge(q_kept, 4)
                    elif n < 7:
                        pe.wait_ge(q_kept, n + 1)
                    elif n >= 8:
                        pe.wait_ge(qa_dve if r else qa_act, h - 3)
                    nc.tensor.matmul(ps[n % 8][:, 0:T], WUK[lo:lo + 64, h // 2, r * P:(r + 1) * P],
                                     QN[lo:lo + 64, h // 2, :], start=True, stop=True).then_inc(qa_mm, 1)
            pe.wait_ge(qa_act, 8)
            pe.wait_ge(qa_dve, 8)
            for n, (t, h0, nh) in enumerate(((0, 0, 4), (0, 4, 4), (1, 0, 4), (1, 4, 4), (2, 0, 8))):
                t0, nt = TILES[t]
                for h in range(nh):
                    mm = nc.tensor.transpose(ps[n][0:32, h * nt:(h + 1) * nt],
                                             QPT[0:nt, t, (h0 + h) * 32:(h0 + h + 1) * 32], ident[0:nt, 0:nt])
                mm.then_inc(qpT_mm, 1)
            pe.wait_ge(qpT_kept, 5)

            def prompt_scores(h):
                b = ps[h % 2]
                if h >= 2:
                    pe.wait_ge(pexp_ready, h - 1)
                for lo, q0, n in ((0, 0, P), (P, P, SEQ)):
                    for r in range(2):
                        nc.tensor.matmul(b[:, lo:lo + n], QA[:, r, h, q0:q0 + P], CKT[:, r, 0:n],
                                         start=(r == 0), stop=False, skip_group_check=True)
                    nc.tensor.matmul(b[:, lo + n - P:lo + n], ident, cst("mask_q"), start=False, stop=False,
                                     skip_group_check=True)
                    mm = nc.tensor.matmul(b[:, lo:lo + n], QP[0:32, h, q0:q0 + P], KPT[0:32, 0:n],
                                          start=False, stop=True, skip_group_check=True)
                mm.then_inc(pscore_mm, 1)

            def prompt_values(h):
                i = h % 2
                pe.wait_ge(prob_ready, h + 1)
                if h >= 2:
                    pe.wait_ge(probT_kept, h - 1)
                for n in range(3):
                    mm = nc.tensor.transpose(ps[2 + i][:, n * P:(n + 1) * P], PP[:, i, n * P:(n + 1) * P], ident)
                mm.then_inc(probT_mm, 1)
                pe.wait_ge(probT_kept, h + 1)
                if h >= 2:
                    pe.wait_ge(po_kept, h - 1)
                for r in range(2):
                    cr = slice(r * P, (r + 1) * P)
                    nc.tensor.matmul(ps[4 + i][:, r * SEQ:(r + 1) * SEQ], CK[:, 0, cr], PPT[:, i, 0:SEQ],
                                     start=True, stop=False, skip_group_check=True)
                    mm = nc.tensor.matmul(ps[4 + i][:, r * SEQ + P:(r + 1) * SEQ], CK[:, 1, cr], PPT[:, i, SEQ:384],
                                          start=False, stop=True, skip_group_check=True)
                mm.then_inc(po_mm, 1)

            def prompt_attention():
                pe.wait_ge(so_kept, 1)
                pe.wait_ge(soT_kept, 1)
                for h in range(H):
                    if h + 2 < H:
                        prompt_scores(h + 2)
                    prompt_values(h)
                pe.wait_ge(po_kept, H)
                pe.wait_ge(probT_kept, H)

            def key_transposes(g, c):
                n = NCH * g + c
                pe.wait_ge(kv_ld[c], chunk_loaded(g, c))
                if n:
                    pe.wait_ge(kvT_act, n)
                    pe.wait_ge(kvT_kept, n + 1)
                for j in range(4):
                    for pg in range(2):
                        for r in range(2):
                            nc.tensor.transpose(ps[j][:, r * 256 + pg * P:r * 256 + (pg + 1) * P],
                                                PAGES[c][:, j, pg, r * P:(r + 1) * P], ident)
                        mm = nc.tensor.transpose(ps[4 + j // 2][0:32, (j % 2 * 2 + pg) * P:(j % 2 * 2 + pg + 1) * P],
                                                 PAGES[c][:, j, pg, R:ROW], ident)
                mm.then_inc(kvT_mm, 1)

            for g in range(2):
                key_transposes(g, 0)
                for c in range(NCH):
                    if c + 1 < NCH:
                        key_transposes(g, c + 1)
                    kr, ke = KTR[c % 2], KTE[c % 2]
                    b, t0 = ps[6 + c // 2 % 2], c % 2 * 256
                    pe.wait_ge(kvT_act, NCH * g + c + 1)
                    pe.wait_ge(kvT_kept, NCH * g + c + 2)
                    if c % 2 == 0 and 4 * g + c // 2 >= 2:
                        pe.wait_ge(s_kept, 4 * g + c // 2 - 1)
                    if c == 0 and g == 1:
                        pe.wait_ge(s_new, 1)
                    for r in range(2):
                        for j in range(4):
                            nc.tensor.matmul(b[32 * j:32 * j + 32, t0:t0 + 256], QAS[:, r, 4 * g + j, :], kr[:, j, r, :],
                                             start=(r == 0), stop=False, skip_group_check=True)
                    for j in range(4):
                        mm = nc.tensor.matmul(b[32 * j:32 * j + 32, t0:t0 + 256], QPS[0:32, 4 * g + j, :],
                                              ke[0:32, j // 2, j % 2 * 256:j % 2 * 256 + 256],
                                              start=False, stop=True, skip_group_check=True)
                    mm.then_inc(s_mm, 1)
                pe.wait_ge(s_kept, 4 * g + 3)
                b = ps[6]
                for j in range(4):
                    for r in range(2):
                        nc.tensor.matmul(b[32 * j:32 * j + 32, 0:32], QAS[:, r, 4 * g + j, :], CKT[:, r, SEQ:T],
                                         start=(r == 0), stop=False, skip_group_check=True)
                    mm = nc.tensor.matmul(b[32 * j:32 * j + 32, 0:32], QPS[0:32, 4 * g + j, :],
                                          KPT[0:32, SEQ:T], start=False, stop=True, skip_group_check=True)
                mm.then_inc(s_mm, 1)
                if g == 0:
                    prompt_scores(0)
                    prompt_scores(1)
                for n in range(4):
                    pe.wait_ge(s_exp, 5 * g + n + 1)
                    if n >= 2 or g:
                        pe.wait_ge(sT_kept, 5 * g + n - 1)
                    for m in range(4):
                        mm = nc.tensor.transpose(ps[2 + n % 2][:, m * P:(m + 1) * P],
                                                 S[:, (4 * n + m) * P:(4 * n + m + 1) * P], ident)
                    mm.then_inc(sT_mm, 1)
                pe.wait_ge(s_exp, 5 * g + 5)
                nc.tensor.transpose(ps[5][0:32, 0:P], S[:, 2048:2080], ident).then_inc(sT_mm, 1)
                pe.wait_ge(sT_kept, 5 * g + 5)
                for m, c in enumerate(V_ORDER[g]):
                    for pg in range(2):
                        for j in range(4):
                            mm = nc.tensor.matmul(ps[4][32 * j:32 * j + 32, 0:R], PT[:, 2 * c + pg, 32 * j:32 * j + 32],
                                                  PAGES[c][:, j, pg, 0:R], start=(m == 0 and pg == 0), stop=False,
                                                  skip_group_check=True)
                    mm.then_inc(v_used, 1)
                for j in range(4):
                    mm = nc.tensor.matmul(ps[4][32 * j:32 * j + 32, 0:R], PNT[0:32, 32 * j:32 * j + 32], CK[0:32, 2, :],
                                          start=False, stop=True, skip_group_check=True)
                mm.then_inc(so_mm, 1)
                pe.wait_ge(so_kept, g + 1)
                for r in range(2):
                    mm = nc.tensor.transpose(ps[5][:, r * P:(r + 1) * P], OS[:, r * P:(r + 1) * P], ident)
                mm.then_inc(soT_mm, 1)
                if g == 0:
                    prompt_attention()
            pe.wait_ge(soT_kept, 2)
            for n in range(4):
                if n >= 2:
                    pe.wait_ge(cat_kept, n - 1)
                for hh in range(2):
                    h = 2 * n + hh
                    for r in range(2):
                        mm = nc.tensor.matmul(ps[n % 2][64 * hh:64 * hh + 64, 0:T], WUV[:, r, h * VD:(h + 1) * VD],
                                              QA[:, r, h, :], start=(r == 0), stop=(r == 1))
                mm.then_inc(omla_mm, 1)

        def act_attention(act):
            for n in range(8):
                act.wait_ge(qa_mm, n // 2 * 4 + n % 2 + 1)
                nc.scalar.copy(QA[:, 0, n, 0:SEQ], ps[(2 * n) % 8][:, 0:SEQ])
                nc.scalar.copy(QAS[:, 0, :, NS * n:NS * n + NS],
                               ps[(2 * n) % 8][:, SEQ:T].rearrange("p (b s) -> p b s", s=NS)).then_inc(qa_act, 1)
            for n, (t, h0, nh) in enumerate(((0, 0, 4), (0, 4, 4), (1, 0, 4), (1, 4, 4), (2, 0, 8))):
                t0, nt = TILES[t]
                act.wait_ge(qpT_mm, n + 1)
                src = ps[n][0:32, 0:nh * nt]
                if t < 2:
                    op = nc.scalar.copy(QP[0:32, h0:h0 + nh, t0:t0 + nt], src.rearrange("p (h t) -> p h t", h=nh))
                else:
                    op = nc.scalar.copy(QPS[0:32].rearrange("p b (h s) -> p b h s", s=NS),
                                        src.rearrange("p (h b s) -> p b h s", h=nh, s=NS))
                op.then_inc(qpT_kept, 1)

            def exp_head(h):
                i = h % 2
                act.wait_ge(pmax_ready, h + 1)
                if h >= 2:
                    act.wait_ge(probT_mm, h - 1)
                nc.scalar.activation(PP[:, i, 0:P], ps[i][:, 0:P], ACT.Exp, bias=MXP[:, i, 0:1], scale=SCALE,
                                     accum_out=RSP[:, i, 0:1])
                nc.scalar.activation(PP[:, i, P:384], ps[i][:, P:384], ACT.Exp, bias=MXP[:, i, 1:2], scale=SCALE,
                                     accum_out=RSP[:, i, 1:2]).then_inc(pexp_ready, 1)

            def prompt_attention():
                exp_head(0)
                for h in range(H):
                    i = h % 2
                    if h + 1 < H:
                        exp_head(h + 1)
                    act.wait_ge(probT_mm, h + 1)
                    if h >= 2:
                        act.wait_ge(po_mm, h - 1)
                    nc.scalar.copy(PPT[:, i, :], ps[2 + i][:, 0:384]).then_inc(probT_kept, 1)
                    act.wait_ge(po_mm, h + 1)
                    nc.scalar.copy(QA[:, :, h, 0:SEQ], ps[4 + i][:, :].rearrange("p (r t) -> p r t", r=2)
                                   ).then_inc(po_kept, 1)

            act.wait_ge(h0_stored, 16)

            def keep_scores(g, m):
                act.wait_ge(s_mm, 9 * g + 2 * m + 2)
                if m == 0 and g:
                    act.wait_ge(sT_mm, 5)
                nc.scalar.mul(S[:, m * 512:(m + 1) * 512], ps[6 + m % 2][:, :], SCALE).then_inc(s_kept, 1)

            for g in range(2):
                for c in range(NCH):
                    act.wait_ge(kvT_mm, NCH * g + c + 3)
                    if c >= 2 or g:
                        act.wait_ge(s_mm, 9 * g + max(c - 1, 0))
                    for j in (2, 3):
                        nc.scalar.copy(KTR[c % 2][:, j], ps[j][:, :].rearrange("p (r t) -> p r t", r=2))
                    nc.scalar.copy(KTE[c % 2][0:32, 1], ps[5][0:32, :]).then_inc(kvT_act, 1)
                    if c % 2 == 0 and c:
                        keep_scores(g, c // 2 - 1)
                keep_scores(g, 3)
                act.wait_ge(s_max, g + 1)
                if g:
                    act.wait_ge(so_mm, 1)
                for n in range(6):
                    if n < 5:
                        lo, hi = 512 * n, min(512 * n + 512, 2080)
                        nc.scalar.activation(S[:, lo:hi], S[:, lo:hi], ACT.Exp, bias=MXS[:, g:g + 1],
                                             accum_out=RS5[:, n:n + 1]).then_inc(s_exp, 1)
                    if n >= 2:
                        m = n - 2
                        act.wait_ge(sT_mm, 5 * g + m + 1)
                        nc.scalar.copy(PT[:, 4 * m:4 * m + 4, :],
                                       ps[2 + m % 2][:, :].rearrange("p (m q) -> p m q", m=4)).then_inc(sT_kept, 1)
                act.wait_ge(sT_mm, 5 * g + 5)
                nc.scalar.copy(PNT[0:32], ps[5][0:32, 0:P]).then_inc(sT_kept, 1)
                act.wait_ge(soT_mm, g + 1)
                for r in range(2):
                    op = nc.scalar.copy(QA[:, r, :, SEQ + 16 * g:SEQ + 16 * g + 16].rearrange("p h (j s) -> p j h s", j=4),
                                        ps[5][:, r * P:(r + 1) * P].rearrange("p (j h s) -> p j h s", j=4, h=H))
                op.then_inc(soT_kept, 1)
                if g == 0:
                    prompt_attention()
            for n in range(4):
                act.wait_ge(omla_mm, n + 1)
                nc.scalar.copy(CAT[:, n, :], ps[n % 2][:, 0:T]).then_inc(cat_kept, 1)

        def dve_attention(dve, steps):
            V = nc.vector
            co = cst("cos").rearrange("p (t f) -> p t f", t=3)
            si = cst("sin").rearrange("p (t f) -> p t f", t=3)
            for t, (t0, nt) in enumerate(TILES):
                dve.wait_ge(qn_mm, t + 5)
                if t == 2:
                    dve.wait_ge(q_kept, 5)
                q = ps[4 + t][0:nt, 0:256].rearrange("p (h f) -> p h f", h=H)
                out = QPT[0:nt, t, :].rearrange("p (h f) -> p h f", h=H)
                cb = co[0:nt, t, :].unsqueeze(1).to_broadcast([nt, H, 16])
                sb_ = si[0:nt, t, :].unsqueeze(1).to_broadcast([nt, H, 16])
                ta = TMP[0:nt, 2 * (t % 2), :].rearrange("p (h f) -> p h f", h=H)
                tb = TMP[0:nt, 2 * (t % 2) + 1, :].rearrange("p (h f) -> p h f", h=H)
                V.tensor_tensor(out[:, :, 0:16], q[:, :, 0:16], cb, ALU.mult)
                V.tensor_tensor(out[:, :, 16:32], q[:, :, 16:32], cb, ALU.mult)
                V.tensor_tensor(ta, q[:, :, 16:32], sb_, ALU.mult)
                steps.step(V.tensor_tensor(tb, q[:, :, 0:16], sb_, ALU.mult))
                V.tensor_tensor(out[:, :, 0:16], out[:, :, 0:16], ta, ALU.subtract)
                op = V.tensor_tensor(out[:, :, 16:32], out[:, :, 16:32], tb, ALU.add)
                op.then_inc(q_kept, 1)
            for n in range(8):
                dve.wait_ge(qa_mm, n // 2 * 4 + n % 2 + 3)
                V.tensor_copy(QA[:, 1, n, 0:SEQ], ps[(2 * n + 1) % 8][:, 0:SEQ])
                V.tensor_copy(QAS[:, 1, :, NS * n:NS * n + NS],
                              ps[(2 * n + 1) % 8][:, SEQ:T].rearrange("p (b s) -> p b s", s=NS)).then_inc(qa_dve, 1)

            def front(h):
                i = h % 2
                dve.wait_ge(pscore_mm, h + 1)
                V.tensor_reduce(MXP[:, i, 0:1], ps[i][:, 0:P], AX, ALU.max)
                steps.step(V.tensor_reduce(MXP[:, i, 1:2], ps[i][:, P:384], AX, ALU.max))
                V.tensor_scalar(MXP[:, i, 0:2], MXP[:, i, 0:2], -SCALE, None, ALU.mult).then_inc(pmax_ready, 1)

            def prompt_attention():
                for h in range(H):
                    i = h % 2
                    if h + 1 < H:
                        front(h + 1)
                    dve.wait_ge(pexp_ready, h + 1)
                    steps.step(V.reciprocal(RSP[:, i, 0:2], RSP[:, i, 0:2]))
                    V.tensor_scalar(PP[:, i, 0:P], PP[:, i, 0:P], RSP[:, i, 0:1], None, ALU.mult)
                    V.tensor_scalar(PP[:, i, P:384], PP[:, i, P:384], RSP[:, i, 1:2], None, ALU.mult
                                    ).then_inc(prob_ready, 1)

            def part_max(g, m):
                dve.wait_ge(s_kept, 4 * g + m + 1)
                V.tensor_reduce(MX5[:, m:m + 1], S[:, 512 * m:512 * m + 512], AX, ALU.max)

            dve.wait_ge(h0_stored, 16)
            for g in range(2):
                for c in range(NCH):
                    dve.wait_ge(kvT_mm, NCH * g + c + 3)
                    if c >= 2 or g:
                        dve.wait_ge(s_mm, 9 * g + max(c - 1, 0))
                    for j in (0, 1):
                        V.tensor_copy(KTR[c % 2][:, j], ps[j][:, :].rearrange("p (r t) -> p r t", r=2))
                    V.tensor_copy(KTE[c % 2][0:32, 0], ps[4][0:32, :]).then_inc(kvT_kept, 1)
                    if c % 2 and c > 1:
                        part_max(g, c // 2 - 1)
                part_max(g, 3)
                dve.wait_ge(s_mm, 9 * g + 9)
                if g:
                    dve.wait_ge(sT_mm, 5)
                V.scalar_tensor_tensor(S[:, 2048:2080], ps[6][:, 0:32], SCALE,
                                       cst("mask_new")[:, 32 * g:32 * g + 32], ALU.mult, ALU.add).then_inc(s_new, 1)
                dve.wait_ge(s_new, g + 1)
                steps.step(V.tensor_reduce(MX5[:, 4:5], S[:, 2048:2080], AX, ALU.max))
                steps.step(V.tensor_reduce(MXS[:, g:g + 1], MX5, AX, ALU.max))
                V.tensor_scalar(MXS[:, g:g + 1], MXS[:, g:g + 1], -1.0, None, ALU.mult).then_inc(s_max, 1)
                if g == 0:
                    front(0)
                dve.wait_ge(s_exp, 5 * g + 5)
                steps.step(V.tensor_reduce(RSS[:, g:g + 1], RS5, AX, ALU.add))
                steps.step(V.reciprocal(RSS[:, g:g + 1], RSS[:, g:g + 1]))
                dve.wait_ge(so_mm, g + 1)
                if g:
                    dve.wait_ge(soT_mm, 1)
                V.tensor_scalar(OS, ps[4][:, 0:R], RSS[:, g:g + 1], None, ALU.mult).then_inc(so_kept, 1)
                if g == 0:
                    prompt_attention()

        out_mm, res_kept, ln_var, ln_std, ln_done, xt_mm, xt_kept = map(sem, (
            "out_mm", "res_kept", "ln_var", "ln_std", "ln_done", "xt_mm", "xt_kept"))
        x1_stored = sem("x1_stored")
        ln_norm = sem("ln_norm")
        LNS = small[:, 512:572]

        def ln_finished(eng, s, t):
            eng.wait_ge(*((ln_norm, 3 * s + 3) if t == 2 else (ln_done, 2 * s + t + 1)))

        def out_projection(pe, l, lhs, w, t, ready=None):
            t0, nt = TILES[t]
            if t == 2:
                for k in range(KC):
                    for j in range(4):
                        mm = nc.tensor.matmul(ps[4][32 * j:32 * j + 32, 0:256], lhs[:, k, t0:t0 + nt],
                                              w[:, k, j * 256:(j + 1) * 256], start=(k == 0), stop=(k == KC - 1),
                                              skip_group_check=True)
                mm.then_inc(out_mm, 1)
                return
            for n in range(2):
                for k in range(KC):
                    if ready is not None and n == 0:
                        pe.wait_ge(ready, k + 1)
                    mm = nc.tensor.matmul(ps[2 * t + n][0:nt, :], lhs[:, k, t0:t0 + nt],
                                          w[:, k, n * 512:(n + 1) * 512], start=(k == 0), stop=(k == KC - 1))
            mm.then_inc(out_mm, 1)

        def ln_dve(dve, steps, s, t, nt):
            V = nc.vector
            st = LNS[0:nt, 20 * t:20 * t + 12].rearrange("p (a b) -> p a b", a=2)
            mv, rs = LNS[0:nt, 20 * t + 12:20 * t + 14], LNS[0:nt, 20 * t + 14:20 * t + 15]
            x = X[0:nt, t, :]
            for n in range(2):
                op = V.bn_stats(st[:, n, :], X[0:nt, t, n * 512:(n + 1) * 512])
            steps.step(op)
            V.bn_aggr(mv, st).then_inc(ln_var, 1)
            if t == 2:
                dve.wait_ge(ld_rows, 32 * (s + 1))
                dve.wait_ge(ln_var, 3 * s + 3)
                steps.step(V.scalar_tensor_tensor(x, x, mv[:, 0:1], ROWS[0:nt, 0, :], ALU.subtract, ALU.mult))
            dve.wait_ge(ln_std, 3 * s + t + 1)
            steps.step(V.reciprocal(rs, rs))
            if t == 2:
                op = V.scalar_tensor_tensor(x, x, rs, ROWS[0:nt, 1, :], ALU.mult, ALU.add)
            else:
                op = V.tensor_scalar(x, x, mv[:, 0:1], rs, ALU.subtract, ALU.mult)
            op.then_inc(ln_norm, 1)

        def ln_act(act, s, t):
            nt = TILES[t][1]
            act.wait_ge(ln_var, 3 * s + t + 1)
            nc.scalar.activation(LNS[0:nt, 20 * t + 14:20 * t + 15], LNS[0:nt, 20 * t + 13:20 * t + 14], ACT.Sqrt,
                                 bias=cst("eps", nt)).then_inc(ln_std, 1)

        def ln_pool(pool, s, dst=None, done=None):
            G = nc.gpsimd
            pool.wait_ge(ld_rows, 32 * (s + 1))
            for t, (t0, nt) in enumerate(TILES):
                if t < 2:
                    pool.wait_ge(ln_norm, 3 * s + t + 1)
                    G.tensor_tensor(X[0:nt, t, :], X[0:nt, t, :], ROWS[0:nt, 0, :], ALU.mult).then_inc(pool_step, 1)
                    pool.wait_ge(pool_step, 2 * s + t + 1)
                    G.tensor_tensor(X[0:nt, t, :], X[0:nt, t, :], ROWS[0:nt, 1, :], ALU.add).then_inc(ln_done, 1)
                if dst is not None:
                    ln_finished(pool, s, t)
                    pool.dma_start(dst[t0:t0 + nt], X[0:nt, t, :]).then_inc(done, 16)

        def transposes_x(pe, s, r, t):
            t0, nt = TILES[t]
            ln_finished(pe, s, t)
            if t == 1:
                pe.wait_ge(xt_kept, 3 * r + 1)
            for k in range(KC):
                bank, lo = (ps[0], k * nt) if t == 2 else (ps[6 + k // 4], k % 4 * P)
                mm = nc.tensor.transpose(bank[:, lo:lo + nt], X[0:nt, t, k * P:(k + 1) * P], ident[0:nt, 0:nt])
            mm.then_inc(xt_mm, 1)

        def keep_xt(act, r, t):
            t0, nt = TILES[t]
            act.wait_ge(xt_mm, 3 * r + t + 1)
            if t == 2:
                op = nc.scalar.copy(XT[:, :, t0:t0 + nt], ps[0][:, 0:KC * nt].rearrange("p (k t) -> p k t", k=KC))
            else:
                for n in range(2):
                    op = nc.scalar.copy(XT[:, 4 * n:4 * n + 4, t0:t0 + nt],
                                        ps[6 + n][:, :].rearrange("p (k t) -> p k t", k=4))
            op.then_inc(xt_kept, 1)

        NW = 6
        HS, HH, HT, YS = (at(M, 6144, 2, P), at(M, 6400, 2, P), at(M, 6656, 2, P), at(M, 6912, 2, 512))
        RT = M[:, 7936:9216]
        XG = at(M, 9216, 2, D)
        GY = at(M, 12184, 3, 2, D)
        XGT = at(xT_t, 0, 2, KC, 2 * CAP)
        yd = nc.dram_tensor("expert_rows", (SLOT_ROWS, D), F32).ap()
        xd = [nc.dram_tensor(f"x_rows{l}", (T, D), F32).ap() for l in range(2)]
        slots = [nc.dram_tensor(f"slot_tokens{l}", (SLOT_ROWS, 1), I32).ap() for l in range(2)]
        TID, DI = ints[:, 0:3], ints[:, 3:9]
        IDX, IDXX = ints[:, 9:17], ints[0:CAP, 17:17 + MAX_EXTRA]
        XE, XN = ints[:, 25:25 + MAX_EXTRA], ints[:, 33:35]
        tables_ready = sem("tables_ready")
        logit_mm, logit_exp, pick_ready, rank_mm, dest_ready, tok_scattered, xg_zero = map(sem, (
            "logit_mm", "logit_exp", "pick_ready", "rank_mm", "dest_ready", "tok_scattered", "xg_zero"))
        w_ld = slot_ld
        gat, ystore = [sem("gat0"), sem("gat1")], [sem("ystore0"), sem("ystore1")]
        gy_t = [sem(f"gy_t{t}") for t in range(3)]
        idx_ld, xT_mm, xgt_kept, gu_mm, hs_ready, hh_ready, ht_mm, ht_kept, y_mm, ys_kept = map(sem, (
            "idx_ld", "xT_mm", "xgt_kept", "gu_mm", "hs_ready", "hh_ready", "ht_mm", "ht_kept", "y_mm", "ys_kept"))
        EX = [{k: sem(f"extra{l}_{k}") for k in ("w_ld0", "w_ld1", "gat", "pe", "act", "dve", "ystore0", "ystore1")}
              for l in range(2)]
        EXTRA_STEPS = {"xT_mm": ("pe", 4, 1), "gu_mm": ("pe", 4, 2), "ht_mm": ("pe", 4, 3), "y_mm": ("pe", 4, 4),
                       "hs_ready": ("act", 3, 1), "ht_kept": ("act", 3, 2), "ys_kept": ("act", 3, 3),
                       "xgt_kept": ("dve", 2, 1), "hh_ready": ("dve", 2, 2)}

        def wait_extra(eng, l, step, i):
            who, n, k = EXTRA_STEPS[step]
            eng.wait_ge(EX[l][who], i * n + k)

        def w_slot(n):
            n = n % NW
            return slot_t[:, 6144 * n:6144 * (n + 1)] if n < 3 else M[:, (0, 18328, 12184)[n - 3]:][:, 0:6144]

        def w_loaded(l, n):
            pages_ = chunk_loaded(1, 4) if n % NW < 4 else 0
            return pages_ + 16 * (l * len(range(n % NW, NE, NW)) + n // NW + 1)

        def x_slot(u):
            return w_slot(15) if u else w_slot(5)

        def weights(w):
            return (w[:, 0:4096].rearrange("p (k h f) -> p k h f", k=KC, h=2),
                    w[:, 4096:6144].rearrange("p (h d) -> p h d", h=2))

        def each_extra(eng, l, body):
            eng.wait_ge(dest_ready, 2 * l + 2)
            n_extra = eng.value_load(XN[0:1, l:l + 1], min_val=0, max_val=MAX_EXTRA)
            with eng.If(n_extra > 0):
                body(0, 0)
                with eng.If(n_extra > 1):
                    body(1, 1)
                    with eng.Fori(1, MAX_EXTRA // 2) as q:
                        for u in range(2):
                            with eng.If(q * 2 + u < n_extra):
                                body(q * 2 + u, u)

        def before(N, n):
            return not (isinstance(N, int) and N < n)

        def loads_moe(sp, l):
            src = a["w_moe"]

            def load(layer, n):
                sp.dma_start(w_slot(n), src[layer, n]).then_inc(w_ld[n % NW], 16)

            if l == 0:
                sp.wait_ge(v_used, 2 * NCH)
                load(0, 1)
                load(0, 2)
                sp.wait_ge(omla_mm, 4)
                sp.wait_ge(ckv_stored, 48)
                load(0, 0)
            else:
                loads_conformer(sp)
                for n in range(3):
                    if n == 2:
                        sp.wait_ge(tap_mm, KC)
                    load(1, n)
            sp.wait_ge(out_mm, 3 * l + 3)
            load(l, 3)
            sp.wait_ge(ln_var, 6 * l + 3)
            sp.wait_ge(x1_stored, 48 * (l + 1))
            load(l, 4)
            sp.wait_ge(ln_done, 4 * l + 2)
            sp.wait_ge(ln_norm, 6 * l + 3)
            sp.dma_start(ROWS[:, 0, :], a["rows"][2 * l + 1]).then_inc(ld_rows, 16)
            sp.dma_start(ROWS[:, 1, :], a["rows_b"][2 * l + 1]).then_inc(ld_rows, 16)
            if l:
                sp.wait_ge(conv_stored, 64)
            sp.wait_ge(gat[1], 16 * (4 * l + 1))
            load(l, 5)
            for n in range(NW, NE):
                sp.wait_ge(y_mm, 16 * l + n - NW + 1)
                load(l, n)

            def body(i, u):
                e = sp.value_load(XE[0:1, bass.ds(i, 1)], min_val=0, max_val=NE - 1)
                sp.wait_ge(y_mm, 16 * l + (16 if u else 12))
                sp.wait_ge(EX[l]["gat"], i * 16 + 16)
                sp.dma_start(x_slot(u), src[l, bass.ds(e, 1)].rearrange("a p f -> (a p) f")
                             ).then_inc(EX[l][f"w_ld{u}"], 16)
            each_extra(sp, l, body)

        def gathered_transposes(pe, xb):
            for k in range(KC):
                mm = nc.tensor.transpose(ps[k // 4][:, k % 4 * P:(k % 4 + 1) * P], XG[:, xb, k * P:(k + 1) * P], ident)
            return mm

        def gate_up(pe, w, xb, b):
            wgu, _ = weights(w)
            for k in range(KC):
                for h in range(2):
                    mm = nc.tensor.matmul(ps[2 + b][64 * h:64 * h + 64, 0:256], XGT[:, xb, k, CAP * b:CAP * b + CAP],
                                          wgu[:, k, h, :], start=(k == 0), stop=(k == KC - 1), skip_group_check=True)
            return mm

        def down(pe, w, b):
            _, wd = weights(w)
            for h in range(2):
                for n in range(2):
                    mm = nc.tensor.matmul(ps[6 + b][64 * n:64 * n + 64, :], HT[:, b, h * 64:h * 64 + 64],
                                          wd[:, h, n * 512:(n + 1) * 512], start=(h == 0), stop=(h == 1),
                                          skip_group_check=True)
            return mm

        def router_products(pe, l, t):
            t0, nt = TILES[t]
            transposes_x(pe, 2 * l, 2 * l, t)
            pe.wait_ge(xt_kept, 6 * l + t + 1)
            wr = prm("w_router").rearrange("p (k e) -> p k e", k=KC)
            for k in range(KC):
                mm = nc.tensor.matmul(ps[1][0:nt, t * NE:(t + 1) * NE], XT[:, k, t0:t0 + nt], wr[:, k, :],
                                      start=(k == 0), stop=(k == KC - 1))
            if t == 2:
                mm.then_inc(logit_mm, 1)

        def products_moe(pe, l):
            pe.wait_ge(pick_ready, l + 1)
            picks = RT[:, 0:48].rearrange("p (t e) -> p t e", t=3)
            nc.tensor.matmul(ps[7][:, 0:NE], cst("tri_strict"), picks[:, 0, :], start=True, stop=True,
                             skip_group_check=True)
            for u in range(3):
                nc.tensor.matmul(ps[7][:, (u + 1) * NE:64].rearrange("p (t e) -> p t e", e=NE), ones,
                                 picks[:, u, :].unsqueeze(1).to_broadcast([P, 3 - u, NE]), start=(u == 0), stop=False,
                                 skip_group_check=True)
            mm = nc.tensor.matmul(ps[7][:, NE:48], cst("tri_strict"), RT[:, NE:48], start=False, stop=True,
                                  skip_group_check=True)
            mm.then_inc(rank_mm, 1)
            pe.wait_ge(dest_ready, 2 * l + 2)


            def transposes(n):
                N, xb = 16 * l + n, n // 2 % 2
                pe.wait_ge(gat[xb], 16 * (N // 4 + 1))
                if N:
                    pe.wait_ge(xgt_kept, N // 2)
                gathered_transposes(pe, xb).then_inc(xT_mm, 1)

            def second_half(n):
                N, b = 16 * l + n, n % 2
                pe.wait_ge(hh_ready, N + 1)
                if N >= 2:
                    pe.wait_ge(ht_kept, N - 1)
                nc.tensor.transpose(ps[4 + b][:, 0:P], HH[:, b, :], ident).then_inc(ht_mm, 1)
                pe.wait_ge(ht_kept, N + 1)
                if N >= 2:
                    pe.wait_ge(ys_kept, N - 1)
                down(pe, w_slot(n), b).then_inc(y_mm, 1)

            transposes(0)
            for n in range(NE):
                N = 16 * l + n
                pe.wait_ge(w_ld[n % NW], w_loaded(l, n))
                pe.wait_ge(xgt_kept, N // 2 + 1)
                if N >= 2:
                    pe.wait_ge(hh_ready, N - 1)
                gate_up(pe, w_slot(n), n // 2 % 2, n % 2).then_inc(gu_mm, 1)
                if n % 2 and n + 1 < NE:
                    transposes(n + 1)
                if n:
                    second_half(n - 1)
            second_half(NE - 1)
            pe.wait_ge(ys_kept, 16 * (l + 1))

            def extra(i, u):
                x = EX[l]
                pe.wait_ge(x["gat"], i * 16 + 16)
                gathered_transposes(pe, u).then_inc(x["pe"], 1)
                pe.wait_ge(x[f"w_ld{u}"], (i - u) * 8 + 16)
                wait_extra(pe, l, "xgt_kept", i)
                gate_up(pe, x_slot(u), 0, 0).then_inc(x["pe"], 1)
                wait_extra(pe, l, "hh_ready", i)
                nc.tensor.transpose(ps[4][:, 0:P], HH[:, 0, :], ident).then_inc(x["pe"], 1)
                wait_extra(pe, l, "ht_kept", i)
                down(pe, x_slot(u), 0).then_inc(x["pe"], 1)
            each_extra(pe, l, extra)

        def act_moe(act, l):
            act.wait_ge(logit_mm, l + 1)
            act.wait_ge(xg_zero, l + 1)
            lg = RT[:, 48:96].rearrange("p (t e) -> p t e", t=3)
            nc.scalar.activation(lg[:, 0:2, :], ps[1][:, 0:32].rearrange("p (t e) -> p t e", t=2), ACT.Exp, scale=-1.0)
            nc.scalar.activation(lg[0:32, 2, :], ps[1][0:32, 32:48], ACT.Exp, scale=-1.0).then_inc(logit_exp, 1)

            def silu(b):
                return nc.scalar.activation(HS[:, b, :], ps[2 + b][:, 0:P], ACT.Silu)

            def keep_ht(b):
                return nc.scalar.copy(HT[:, b, :], ps[4 + b][:, 0:P])

            def keep_y(b, to):
                return nc.scalar.copy(YS[:, to, :], ps[6 + b][:, :])

            def store_y(row, b, done):
                for n in range(2):
                    act.dma_start(yd[bass.ds(row, CAP), n * 512:(n + 1) * 512], YS[64 * n:64 * n + 64, b, :]
                                  ).then_inc(done, 16)

            def second_half(n):
                N, b = 16 * l + n, n % 2
                act.wait_ge(ht_mm, N + 1)
                if N >= 2:
                    act.wait_ge(y_mm, N - 1)
                keep_ht(b).then_inc(ht_kept, 1)
                act.wait_ge(y_mm, N + 1)
                if N >= 2:
                    act.wait_ge(ystore[b], N // 2 * 32)
                keep_y(b, b).then_inc(ys_kept, 1)
                act.wait_ge(ys_kept, N + 1)
                store_y(n * CAP, b, ystore[b])

            act.wait_ge(tok_scattered, 96 * (l + 1))
            act.dma_start(IDX, slots[l][0:NE * CAP].rearrange("(n p) o -> p (n o)", p=P),
                          allow_slow_non_contiguous=True).then_inc(idx_ld, 16)
            act.dma_start(IDXX, slots[l][NE * CAP:].rearrange("(n p) o -> p (n o)", p=CAP),
                          allow_slow_non_contiguous=True).then_inc(idx_ld, 16)
            for n in range(NE):
                N = 16 * l + n
                act.wait_ge(gu_mm, N + 1)
                if N >= 2:
                    act.wait_ge(hh_ready, N - 1)
                silu(n % 2).then_inc(hs_ready, 1)
                if n:
                    second_half(n - 1)
            second_half(NE - 1)

            def extra(i, u):
                x = EX[l]
                wait_extra(act, l, "gu_mm", i)
                silu(0).then_inc(x["act"], 1)
                wait_extra(act, l, "ht_mm", i)
                keep_ht(0).then_inc(x["act"], 1)
                wait_extra(act, l, "y_mm", i)
                if before(i, 2):
                    act.wait_ge(x[f"ystore{u}"], (i - u) * 16)
                keep_y(0, u).then_inc(x["act"], 1)
                wait_extra(act, l, "ys_kept", i)
                store_y(i * CAP + NE * CAP, u, x[f"ystore{u}"])
            act.wait_ge(ystore[0], 256 * (l + 1))
            act.wait_ge(ystore[1], 256 * (l + 1))
            each_extra(act, l, extra)

        def dve_moe(dve, steps, l):
            V = nc.vector
            t3 = lambda off, n=NE: RT[:, off:off + 3 * n].rearrange("p (t e) -> p t e", t=3)
            M12, EXPL, PR, SEL = t3(0), t3(48), t3(96), t3(144)
            O1, O2, W16, PLACE = t3(192), t3(240), t3(288), t3(336)
            G12, GPLACE, GSUM = RT[:, 384:396], RT[:, 396:408], RT[:, 408:420]
            three = RT[:, 480:480 + 8 * 3].rearrange("p (n t) -> p n t", n=8)
            RK_ = t3(520)
            D12 = RT[:, 568:574].rearrange("p (t k) -> p t k", t=3)
            W32 = RT[:, 424:472].rearrange("p (t e) -> p t e", t=3)
            four = lambda v: v.rearrange("p t (g m) -> p (t g) m", m=4)

            def places(v, out, n):
                gt, ge = (RT[:, 840 + 192 * i:840 + 192 * i + 16 * n].rearrange("p (g a b) -> p g a b", a=4, b=4)
                          for i in range(2))
                this, other = v.unsqueeze(3).to_broadcast([P, n, 4, 4]), v.unsqueeze(2).to_broadcast([P, n, 4, 4])
                V.tensor_tensor(gt, other, this, ALU.is_gt)
                steps.step(V.tensor_tensor(ge, other, this, ALU.is_ge))
                for x, mask in ((gt, "later"), (ge, "earlier")):
                    x = x.rearrange("p g a b -> p g (a b)")
                    op = V.tensor_tensor(x, x, cst(mask).unsqueeze(1).to_broadcast([P, n, 16]), ALU.mult)
                steps.step(op)
                steps.step(V.tensor_tensor(gt, gt, ge, ALU.add))
                steps.step(V.tensor_reduce(out, gt.rearrange("p g a b -> p (g a) b"), AX, ALU.add))

            if l:
                dve.wait_ge(conv_stored, 64)
            V.memset(EXPL, 0.0).then_inc(xg_zero, 1)
            dve.wait_ge(logit_exp, l + 1)
            steps.step(V.tensor_scalar(PR, EXPL, 1.0, None, ALU.add))
            steps.step(V.reciprocal(PR, PR))
            steps.step(V.tensor_tensor(SEL, PR, prm("r_bias").unsqueeze(1).to_broadcast([P, 3, NE]), ALU.add))
            places(four(SEL), PLACE.rearrange("p t e -> p (t e)"), 12)
            steps.step(V.scalar_tensor_tensor(W16, PLACE, 2.0, SEL, ALU.is_lt, ALU.mult))
            steps.step(V.tensor_reduce(GSUM, four(W16), AX, ALU.add))
            places(GSUM.rearrange("p (t g) -> p t g", t=3), GPLACE, 3)
            steps.step(V.scalar_tensor_tensor(G12.rearrange("p (t g) -> p t g", t=3),
                                              GPLACE.rearrange("p (t g) -> p t g", t=3), 0.0,
                                              cst("valid").unsqueeze(2).to_broadcast([P, 3, 4]), ALU.is_equal, ALU.mult))
            chosen = G12.unsqueeze(2).to_broadcast([P, 12, 4])
            V.scalar_tensor_tensor(four(M12), four(PLACE), 2.0, chosen, ALU.is_lt, ALU.mult).then_inc(pick_ready, 1)
            V.scalar_tensor_tensor(four(O1), four(PLACE), 0.0, chosen, ALU.is_equal, ALU.mult)
            steps.step(V.scalar_tensor_tensor(four(O2), four(PLACE), 1.0, chosen, ALU.is_equal, ALU.mult))
            V.tensor_tensor(W16, PR, O1, ALU.mult)
            steps.step(V.tensor_tensor(W32, PR, O2, ALU.mult))
            V.tensor_reduce(three[:, 1, :], W16, AX, ALU.add)
            steps.step(V.tensor_reduce(three[:, 2, :], W32, AX, ALU.add))
            steps.step(V.tensor_tensor(three[:, 3, :], three[:, 1, :], three[:, 2, :], ALU.add))
            steps.step(V.tensor_scalar(three[:, 3, :], three[:, 3, :], 1e-30, None, ALU.max))
            steps.step(V.reciprocal(three[:, 3, :], three[:, 3, :]))
            V.tensor_tensor(three[:, 4, :], three[:, 1, :], three[:, 3, :], ALU.mult)
            V.tensor_tensor(three[:, 5, :], three[:, 2, :], three[:, 3, :], ALU.mult)
            dve.wait_ge(rank_mm, l + 1)
            FL = RT[:, 600:664].rearrange("p (e j) -> p e j", e=NE)
            EXT, CUM, BASE = RT[:, 664:680], RT[:, 680:696], RT[:, 696:712]
            steps.step(V.tensor_tensor(FL, ps[7][:, 48:64].unsqueeze(2).to_broadcast([P, NE, 4]),
                                       cst("item_thr").rearrange("p (e j) -> p e j", e=NE), ALU.is_gt))
            steps.step(V.tensor_reduce(EXT, FL, AX, ALU.add))
            steps.step(V.tensor_tensor_scan(CUM, EXT, EXT, 0.0, ALU.add, ALU.bypass))
            V.tensor_copy(XN[0:1, l:l + 1], CUM[0:1, 15:16])
            rank = ps[7][:, 0:48].rearrange("p (t e) -> p t e", t=3)
            V.tensor_tensor(RK_, rank, cst("row_of").unsqueeze(1).to_broadcast([P, 3, NE]), ALU.add)
            steps.step(V.tensor_tensor(BASE, CUM, EXT, ALU.subtract))
            steps.step(V.scalar_tensor_tensor(BASE, BASE, float(CAP), cst("base_of"), ALU.mult, ALU.add))
            steps.step(V.scalar_tensor_tensor(W16, rank, float(CAP), BASE.unsqueeze(1).to_broadcast([P, 3, NE]),
                                              ALU.is_ge, ALU.mult))
            steps.step(V.tensor_tensor(RK_, RK_, W16, ALU.add))
            V.tensor_tensor(W16, RK_, O1, ALU.mult)
            steps.step(V.tensor_tensor(W32, RK_, O2, ALU.mult))
            V.tensor_reduce(D12[:, :, 0], W16, AX, ALU.add)
            steps.step(V.tensor_reduce(D12[:, :, 1], W32, AX, ALU.add))
            V.tensor_copy(DI.rearrange("p (t k) -> p t k", t=3), D12).then_inc(dest_ready, 1)
            ended = RT[0:1, 712:712 + MAX_EXTRA * NE].rearrange("p (i e) -> p i e", i=MAX_EXTRA)
            out8 = RT[0:1, 1264:1272]
            steps.step(V.tensor_tensor(ended, CUM[0:1].unsqueeze(1).to_broadcast([1, MAX_EXTRA, NE]),
                                       cst("item_k", 1).unsqueeze(2).to_broadcast([1, MAX_EXTRA, NE]), ALU.is_le))
            steps.step(V.tensor_reduce(out8, ended, AX, ALU.add))
            V.tensor_copy(XE[0:1], out8).then_inc(dest_ready, 1)
            dve.wait_ge(dest_ready, 2 * l + 2)
            for t, (t0, nt) in enumerate(TILES):
                dve.wait_ge(x1_stored, 48 * (l + 1))
                dve.wait_ge(xt_kept, 6 * l + 3)
                op = V.tensor_scalar(X[0:nt, t, :], X[0:nt, t, :], ALPHA, None, ALU.mult)
            steps.step(op)

            def keep_xgt(xb):
                for n in range(2):
                    op = V.tensor_copy(XGT[:, xb, 4 * n:4 * n + 4], ps[n][:, :].rearrange("p (k s) -> p k s", k=4))
                return op

            def gate(b):
                return V.tensor_tensor(HH[:, b, :], HS[:, b, :], ps[2 + b][:, P:256], ALU.mult)

            def keep(n):
                N = 16 * l + n
                dve.wait_ge(xT_mm, N // 2 + 1)
                if N >= 4:
                    dve.wait_ge(gu_mm, N - 2)
                keep_xgt(n // 2 % 2).then_inc(xgt_kept, 1)

            keep(0)
            for n in range(NE):
                N = 16 * l + n
                if n % 2 and n + 1 < NE:
                    keep(n + 1)
                dve.wait_ge(hs_ready, N + 1)
                if N >= 2:
                    dve.wait_ge(ht_mm, N - 1)
                gate(n % 2).then_inc(hh_ready, 1)

            def extra(i, u):
                x = EX[l]
                wait_extra(dve, l, "xT_mm", i)
                keep_xgt(0).then_inc(x["dve"], 1)
                wait_extra(dve, l, "hs_ready", i)
                gate(0).then_inc(x["dve"], 1)
            each_extra(dve, l, extra)
            for t, (t0, nt) in enumerate(TILES):
                dve.wait_ge(gy_t[t], 32 * (l + 1))
                for k in range(2):
                    op = V.scalar_tensor_tensor(X[0:nt, t, :], GY[0:nt, t, k, :], three[0:nt, 4 + k, t:t + 1], X[0:nt, t, :],
                                                ALU.mult, ALU.add)
                    steps.step(op)
                ln_dve(dve, steps, 2 * l + 1, t, nt)

        ZERO_ROWS = P - 32
        CLEARS = range(NE * CAP, SLOT_ROWS, ZERO_ROWS)
        N_TABLES = 3 + len(CLEARS)

        def fill_tables(pool):
            for n in range(2):
                pool.dma_start(slots[n], a["nobody"]).then_inc(tables_ready, 16)
            pool.dma_start(TID, a["token_ids"]).then_inc(tables_ready, 16)
            pool.wait_ge(zeroed, 1)
            for row in CLEARS:
                n = min(ZERO_ROWS, SLOT_ROWS - row)
                pool.dma_start(yd[row:row + n], X[32:32 + n, 2, :]).then_inc(tables_ready, 16)

        def pool_moe(pool, l):
            G = nc.gpsimd
            pool.wait_ge(out_mm, 3 * (l + 1))
            if l == 0:
                G.memset(XG, 0.0).then_inc(zeroed, 1)
            pool.wait_ge(zeroed, 2)
            pool.wait_ge(tables_ready, 16 * N_TABLES)
            pool.wait_ge(dest_ready, 2 * l + 1)
            for t, (t0, nt) in enumerate(TILES):
                for k in range(2):
                    pool.indirect_dma_start(out=slots[l], out_offset=bass.IndirectOffsetOnAxis(
                        ap=DI[0:nt, 2 * t + k:2 * t + k + 1], axis=0), in_=TID[0:nt, t:t + 1], in_offset=None
                        ).then_inc(tok_scattered, 16)
            pool.wait_ge(tok_scattered, 96 * (l + 1))

            pool.wait_ge(idx_ld, 32 * (l + 1))
            pool.wait_ge(x1_stored, 48 * (l + 1))

            def gather(b, rows, idx, done):
                pool.indirect_dma_start(out=XG[0:rows, b, :], out_offset=None, in_=xd[l],
                                        in_offset=bass.IndirectOffsetOnAxis(ap=idx, axis=0),
                                        bounds_check=T - 1, oob_is_err=False).then_inc(done, 16)

            for n in range(NE // 2):
                if n >= 2:
                    pool.wait_ge(xT_mm, 8 * l + n - 1)
                gather(n % 2, P, IDX[:, n:n + 1], gat[n % 2])
            pool.wait_ge(dest_ready, 2 * l + 2)
            n_extra = pool.value_load(XN[0:1, l:l + 1], min_val=0, max_val=MAX_EXTRA)
            x = EX[l]

            def extras_from(i):
                with pool.If(n_extra > i):
                    if i:
                        pool.wait_ge(x["gat"], 16 * i)
                    if i < 2:
                        pool.wait_ge(xT_mm, 8 * l + 7 + i)
                    else:
                        pool.wait_ge(x["pe"], 4 * (i - 1))
                    gather(i % 2, CAP, IDXX[:, i:i + 1], x["gat"])
                    if i + 1 < MAX_EXTRA:
                        extras_from(i + 1)
                    pool.wait_ge(x[f"ystore{i % 2}"], 32 * (i // 2 + 1))

            extras_from(0)
            pool.wait_ge(ystore[0], 256 * (l + 1))
            pool.wait_ge(ystore[1], 256 * (l + 1))
            for t, (t0, nt) in enumerate(TILES):
                for k in range(2):
                    pool.indirect_dma_start(out=GY[0:nt, t, k, :], out_offset=None, in_=yd,
                                            in_offset=bass.IndirectOffsetOnAxis(
                                                ap=DI[0:nt, 2 * t + k:2 * t + k + 1], axis=0)).then_inc(gy_t[t], 16)

        def products_layer_out(pe, l):
            if l == 0:
                pe.wait_ge(cat_kept, 4)
                pe.wait_ge(ld_wout, 16)
                pe.wait_ge(y_ready, 1)
                lhs, w = CAT, WOUT
            else:
                pe.wait_ge(ld_wout, 48)
                lhs, w = CV, CWO
            out_projection(pe, l, lhs, w, 0, cn_ready if l else None)
            out_projection(pe, l, lhs, w, 1)
            router_products(pe, l, 0)
            out_projection(pe, l, lhs, w, 2)
            router_products(pe, l, 1)
            router_products(pe, l, 2)
            products_moe(pe, l)

        def act_layer_out(act, l):
            for t in range(3):
                ln_act(act, 2 * l, t)
                keep_xt(act, 2 * l, t)
            act_moe(act, l)
            for t in range(3):
                ln_act(act, 2 * l + 1, t)

        def dve_layer_out(dve, steps, l):
            V = nc.vector
            dve.wait_ge(ld_x, 48)
            if l:
                dve.wait_ge(ld_wout, 48)
                dve.wait_ge(xt_kept, 6)
            for t, (t0, nt) in enumerate(TILES):
                dve.wait_ge(out_mm, 3 * l + t + 1)
                for n in range(4 if t == 2 else 2):
                    wide, y = (256, ps[4][32 * n:32 * n + 32, 0:256]) if t == 2 else (512, ps[2 * t + n][0:nt, :])
                    xv = X[0:nt, t, n * wide:(n + 1) * wide]
                    op = V.scalar_tensor_tensor(xv, xv, ALPHA, y, ALU.mult, ALU.add)
                op.then_inc(res_kept, 1)
                dve.wait_ge(res_kept, 3 * l + t + 1)
                if l:
                    steps.step(V.tensor_tensor(X[0:nt, t, :], X[0:nt, t, :], BOUT[0:nt], ALU.add))
                ln_dve(dve, steps, 2 * l, t, nt)
            dve_moe(dve, steps, l)

        def pool_layer_out(pool, store, l):
            ln_pool(pool, 2 * l, xd[l], x1_stored)
            pool_moe(pool, l)
            if l == 0:
                ln_pool(pool, 1)
            else:
                ln_pool(pool, 3, o["y"], stored)
                n_stored[0] += 3


        CWO = at(M, 0, KC, D)
        VP = at(M, 8192, KC, HIST + SEQ)
        VS = at(M, 10480, KC, HIST + NS, NB)
        CV = at(M, 12656, KC, T)
        CQ = at(M, 14960, KC, T)
        PE_TAPS = 10
        DIAG = [at(M, 14960, PE_TAPS, P), at(slot_t, 12288, PE_TAPS, P)]
        PROD = at(M, 18432, 4, NB, NS, KW)
        CW = at(M, 18432, 4, KC, P)
        MU, RC = M[:, 22528:22816], M[:, 22816:23104]
        BOUT = M[:, 23104:24128]
        SG = at(M, 17264, 2, T)
        diag_ready, tap_mm, prod_ready = sem("diag_ready"), sem("tap_mm"), sem("prod_ready")
        glu_mm, sig_ready, v_ready, dw_ready, mean_kept, cn_ready = map(sem, (
            "glu_mm", "sig_ready", "v_ready", "dw_ready", "mean_kept", "cn_ready"))

        def loads_conformer(sp):
            for t in range(3):
                sp.wait_ge(gy_t[t], 32)
            for n in range(16):
                if n == 4:
                    sp.wait_ge(ln_norm, 6)
                    sp.wait_ge(zeroed, 3)
                    sp.dma_start(VS[:, :, 0:HIST, :], a["conf_hist"]).then_inc(ld_hist, 16)
                if n >= 4:
                    sp.wait_ge(glu_mm, n - 3)
                sp.dma_start(CW[:, n % 4], a["w_conf"][n // 2 + 8 * (n % 2)]).then_inc(ring_ld[n % 4], 16)
            sp.dma_start(CWO, a["w_conf_out"]).then_inc(ld_wout, 16)
            sp.wait_ge(ln_done, 4)
            sp.wait_ge(ln_norm, 6)
            sp.dma_start(ROWS[:, 0, :], a["rows"][2]).then_inc(ld_rows, 16)
            sp.dma_start(ROWS[:, 1, :], a["rows_b"][2]).then_inc(ld_rows, 16)
            sp.dma_start(BOUT, a["rows"][4]).then_inc(ld_wout, 16)

        def products_conformer(pe):
            for t in range(3):
                transposes_x(pe, 1, 1, t)
            pe.wait_ge(xt_kept, 6)
            for n in range(16):
                pe.wait_ge(ring_ld[n % 4], chunk_loaded(1, n % 4) + 16 * (n // 4 + 1))
                if n >= 8:
                    pe.wait_ge(v_ready, (n - 8) // 2 + 1)
                for k in range(KC):
                    mm = nc.tensor.matmul(ps[n % 8][:, 0:T], CW[:, n % 4, k, :], XT[:, k, :], start=(k == 0),
                                          stop=(k == KC - 1))
                mm.then_inc(glu_mm, 1)
            pe.wait_ge(v_ready, 6)
            for k in range(KC):
                pe.wait_ge(v_ready, max(6, k + 1))
                pe.wait_ge(diag_ready, k + 1)
                for j in range(PE_TAPS):
                    tap = KW - PE_TAPS + j
                    mm = nc.tensor.matmul(ps[k // 2][:, k % 2 * SEQ:(k % 2 + 1) * SEQ], DIAG[k % 2][:, j, :],
                                          VP[:, k, tap:tap + SEQ], start=(j == 0), stop=(j == PE_TAPS - 1),
                                          skip_group_check=True)
                mm.then_inc(tap_mm, 1)
            for k in range(KC):
                pe.wait_ge(dw_ready, KC + 2 + k)
                mm = nc.tensor.matmul(ps[4][:, 0:T], ones, CV[:, k, :], start=(k == 0), stop=(k == KC - 1))
            mm.then_inc(sum_mm, 1)
            for k in range(KC):
                pe.wait_ge(sq_ready, 8 + k // 2)
                mm = nc.tensor.matmul(ps[5][:, 0:T], ones, CQ[:, k, :], start=(k == 0), stop=(k == KC - 1))
            mm.then_inc(sum_mm, 1)
            pe.wait_ge(std_ready, 4)

        def act_conformer(act):
            bi = prm("b_in")
            dw = prm("dw_w").rearrange("p (c k) -> p c k", k=KW)

            def diagonals(k):
                for j in range(PE_TAPS):
                    tap = KW - PE_TAPS + j
                    op = nc.scalar.activation(DIAG[k % 2][:, j, :], ident, ACT.Copy, scale=dw[:, k, tap:tap + 1])
                op.then_inc(diag_ready, 1)

            for t in range(3):
                keep_xt(act, 1, t)
            diagonals(0)
            diagonals(1)
            for k in range(8):
                act.wait_ge(glu_mm, 2 * k + 2)
                if k >= 2:
                    act.wait_ge(v_ready, k - 1)
                nc.scalar.activation(SG[:, k % 2, :], ps[(2 * k + 1) % 8][:, 0:T], ACT.Sigmoid,
                                     bias=bi[:, 8 + k:9 + k]).then_inc(sig_ready, 1)
            for k in range(2, KC):
                act.wait_ge(tap_mm, k - 1)
                diagonals(k)
            act.wait_ge(tap_mm, KC)
            for q in range(KC // 2):
                act.wait_ge(mean_kept, q + 1)
                nc.scalar.activation(CQ[:, 2 * q:2 * q + 2], CV[:, 2 * q:2 * q + 2], ACT.Square).then_inc(sq_ready, 1)
            act.wait_ge(sum_mm, 4)
            nc.scalar.activation(RC, ps[5][:, 0:T], ACT.Sqrt, bias=eps, scale=1.0 / D).then_inc(std_ready, 1)
            for k in range(8):
                act.wait_ge(mean_kept, KC // 2 + k // 2 + 1)
                nc.scalar.activation(CV[:, k, :], CV[:, k, :], ACT.Silu, bias=prm("bn")[:, k:k + 1],
                                     scale=prm("gn")[:, k:k + 1]).then_inc(cn_ready, 1)

        def dve_conformer(dve, steps):
            V = nc.vector
            bi = prm("b_in")
            dw = prm("dw_w").rearrange("p (c k) -> p c k", k=KW)
            dve.wait_ge(zeroed, 3)
            dve.wait_ge(ld_hist, 32)

            def glu(k):
                dve.wait_ge(sig_ready, k + 1)
                b = ps[(2 * k) % 8]
                V.scalar_tensor_tensor(VP[:, k, HIST:], b[:, 0:SEQ], bi[:, k:k + 1], SG[:, k % 2, 0:SEQ], ALU.add, ALU.mult)
                V.scalar_tensor_tensor(VS[:, k, HIST:, :], b[:, SEQ:T].rearrange("p (b s) -> p s b", s=NS), bi[:, k:k + 1],
                                       SG[:, k % 2, SEQ:T].rearrange("p (b s) -> p s b", s=NS), ALU.add, ALU.mult
                                       ).then_inc(v_ready, 1)

            def sample_sum(k):
                dve.wait_ge(prod_ready, k + 1)
                V.tensor_reduce(CV[:, k, SEQ:T], PROD[:, k % 4].rearrange("p b s j -> p (b s) j"), AX, ALU.add
                                ).then_inc(dw_ready, 1)

            def tap(k, j):
                cp = CV[:, k, 0:SEQ]
                if j == 0:
                    return V.tensor_scalar(cp, VP[:, k, 0:SEQ], dw[:, k, 0:1], prm("dw_b")[:, k:k + 1], ALU.mult, ALU.add)
                return V.scalar_tensor_tensor(cp, VP[:, k, j:j + SEQ], dw[:, k, j:j + 1], cp, ALU.mult, ALU.add)

            glu(0)
            glu(1)
            for k in range(0, KC, 2):
                dve.wait_ge(v_ready, k + 2)
                for j in range(KW - PE_TAPS):
                    for c in (k, k + 1):
                        if j:
                            dve.wait_ge(dve_step, steps.count - 1)
                        steps.count += 1
                        tap(c, j).then_inc(dve_step, 1)
                    if j in (5, 14) and k + 2 < KC:
                        glu(k + 2 + (j == 14))
                    if k + 2 == KC and j in (10, 13, 16, 19):
                        sample_sum((j - 10) // 3)
            for k in range(4, KC):
                sample_sum(k)
            dve.wait_ge(dw_ready, KC)
            V.tensor_tensor(CV[:, :, SEQ:T], CV[:, :, SEQ:T], prm("dw_b").unsqueeze(2).to_broadcast([P, KC, T - SEQ]),
                            ALU.add).then_inc(dw_ready, 1)
            dve.wait_ge(dve_step, steps.count)
            for k in range(KC):
                dve.wait_ge(tap_mm, 2 * (k // 2) + 2)
                cp = CV[:, k, 0:SEQ]
                V.tensor_tensor(cp, cp, ps[k // 2][:, k % 2 * SEQ:(k % 2 + 1) * SEQ], ALU.add).then_inc(dw_ready, 1)
            dve.wait_ge(sum_mm, 3)
            steps.step(V.tensor_scalar(MU, ps[4][:, 0:T], 1.0 / D, None, ALU.mult))
            dve.wait_ge(dw_ready, 2 * KC + 1)
            pair = lambda q: CV[:, 2 * q:2 * q + 2]
            for q in range(KC // 2):
                V.tensor_tensor(pair(q), pair(q), MU.unsqueeze(1).to_broadcast([P, 2, T]), ALU.subtract
                                ).then_inc(mean_kept, 1)
            dve.wait_ge(std_ready, 4)
            steps.step(V.reciprocal(RC, RC))
            dve.wait_ge(mean_kept, KC // 2)
            dve.wait_ge(sq_ready, 11)
            for q in range(KC // 2):
                V.tensor_tensor(pair(q), pair(q), RC.unsqueeze(1).to_broadcast([P, 2, T]), ALU.mult
                                ).then_inc(mean_kept, 1)

        def pool_conformer(pool, store):
            G = nc.gpsimd
            pool.wait_ge(ln_norm, 6)
            G.memset(VP[:, :, 0:HIST], 0.0).then_inc(zeroed, 1)
            pool.wait_ge(ld_hist, 32)
            pool.wait_ge(glu_mm, 16)
            pool.wait_ge(v_ready, 8)
            dw = prm("dw_w").rearrange("p (c k) -> p c k", k=KW)
            for k in range(KC):
                if k >= 4:
                    pool.wait_ge(dw_ready, k - 3)
                for s in range(NS):
                    op = G.tensor_tensor(PROD[:, k % 4, :, s, :], VS[:, k, s:s + KW, :].rearrange("p j b -> p b j"),
                                         dw[:, k, :].unsqueeze(1).to_broadcast([P, NB, KW]), ALU.mult)
                op.then_inc(prod_ready, 1)
            store(o["cconv_p"], VP[:, :, SEQ:SEQ + HIST], conv_stored)
            store(o["cconv_s"], VS[:, :, NS:, :], conv_stored)

        block = ctx.enter_context(nc.Block())

        @block.sync
        def _(sp):
            for k, done in ((0, ld_in0), (KC // 2, ld_in1)):
                sp.dma_start(XT[:, k:k + KC // 2], a["xT"][:, k:k + KC // 2]).then_inc(done, 16)
                sp.dma_start(WTOK[:, k:k + KC // 2], a["w_tok"][:, k:k + KC // 2]).then_inc(done, 16)
            for n in range(4):
                sp.dma_start(WIN[:, n], a["w_ch"][n]).then_inc(ring_ld[n], 16)
            sp.dma_start(C[:], a["consts"]).then_inc(ld_const, 16)
            sp.dma_start(PM[:], a["params"]).then_inc(ld_const, 16)
            sp.wait_ge(zeroed, 1)
            sp.dma_start(XS[:, :, :, 0:3], a["conv_hist"]).then_inc(ld_hist, 16)
            for n in range(4, 15):
                sp.wait_ge(piece_mm, n - 3)
                sp.dma_start(WIN[:, n % 4], a["w_ch"][n]).then_inc(ring_ld[n % 4], 16)
            sp.dma_start(slot_t[:, 0:4352], a["w_q"]).then_inc(ld_wq, 16)
            for t, (t0, nt) in enumerate(TILES):
                sp.dma_start(X[0:nt, t, :], a["x"][t0:t0 + nt]).then_inc(ld_x, 16)
            sp.wait_ge(piece_mm, 15)
            sp.dma_start(H0, a["state"]).then_inc(ld_h0, 16)
            loads_attention(sp)
            loads_moe(sp, 0)
            loads_moe(sp, 1)

        @block.tensor
        def _(pe):
            for k0, done in ((0, ld_in0), (KC // 2, ld_in1)):
                pe.wait_ge(done, 32)
                for t, (t0, nt) in enumerate(TILES):
                    for k in range(k0, k0 + KC // 2):
                        mm = nc.tensor.matmul(ps[4 + t][0:nt, 0:296], XT[:, k, t0:t0 + nt], WTOK[:, k, :],
                                              start=(k == 0), stop=(k == KC - 1))
                    if k0:
                        mm.then_inc(tok_mm, 1)
            def latents():
                pe.wait_ge(sq_ready, 6)
                for k in range(3):
                    mm = nc.tensor.matmul(ps[7][:, 0:T], ones, SQ[:, k, :], start=(k == 0), stop=(k == 2))
                mm.then_inc(sum_mm, 1)
                pe.wait_ge(kv_ready, 1)
                pe.wait_ge(tok_kept, 3)
                for t, (t0, nt) in enumerate(TILES):
                    for r in range(2):
                        nc.tensor.transpose(ps[4 + r][:, t0:t0 + nt], CK[0:nt, t, r * P:(r + 1) * P], ident[0:nt, 0:nt])
                    mm = nc.tensor.transpose(ps[6][0:32, t0:t0 + nt], KPE[0:nt, t, :], ident[0:nt, 0:nt])
                mm.then_inc(kvT_mm, 1)

            def log_decays():
                pe.wait_ge(dtA_ready, 1)
                pe.wait_ge(std_ready, 2)
                b = ps[7]
                for c in range(2):
                    nc.tensor.matmul(b[:, 8 * c:8 * c + 8], cst("tri"), DTA[:, c, :], start=True, stop=True)
                    nc.tensor.matmul(b[:, 16 + 8 * c:24 + 8 * c], ones, DTA[:, c, :], start=True, stop=True)
                nc.tensor.matmul(b[:, 32:96], ones[0:32, :], DTAM[0:32].rearrange("p b h -> p (b h)"), start=True, stop=True)
                nc.tensor.matmul(b[0:32, 96:104], cst("tri_s", 32), DTA[0:32, 2, :], start=True, stop=True)
                nc.tensor.matmul(b[0:32, 104:112], cst("blk_s", 32), DTA[0:32, 2, :], start=True,
                                 stop=True).then_inc(kvT_mm, 1)

            for n in range(15):
                pe.wait_ge(ring_ld[n % 4], 16 * (n // 4 + 1))
                if 4 <= n < 7:
                    pe.wait_ge(hq_kept, n - 3)
                elif n >= 7:
                    pe.wait_ge(ch_kept, n - 6)
                for k in range(KC):
                    mm = nc.tensor.matmul(ps[n % 4][:, 0:T], WIN[:, n % 4, k, :], XT[:, k, :],
                                          start=(k == 0), stop=(k == KC - 1))
                mm.then_inc(piece_mm, 1)
                if n == 7:
                    latents()
                if n == 9:
                    log_decays()
            pe.wait_ge(ch_kept, 12)
            for h in range(H):
                if h >= 4:
                    pe.wait_ge(seg_ready, h - 3)
                    pe.wait_ge(e_ready, h - 3)
                for c in range(2):
                    nc.tensor.matmul(ps[h % 4][:, c * P:(c + 1) * P], DTA[:, c, h:h + 1].to_broadcast([P, P]),
                                     cst("tri"), start=True, stop=True)
                nc.tensor.matmul(ps[h % 4][:, SEQ:T], DTA[0:32, 2, h:h + 1].to_broadcast([32, P]),
                                 cst("tri_s", 32), start=True, stop=True).then_inc(row_mm, 1)
            pe.wait_ge(xb_ready, 1)
            pe.wait_ge(kvT_kept, 1)
            for t, (t0, nt) in enumerate(TILES):
                for k in range(4):
                    mm = nc.tensor.transpose(ps[4 + t][0:nt, k * P:(k + 1) * P], XB[:, k, t0:t0 + nt], ident)
                mm.then_inc(xs_mm, 1)
            for t, (t0, nt) in enumerate(TILES):
                pe.wait_ge(acs_kept, 1) if t == 0 else pe.wait_ge(dx_ready, t)
                bank = ps[7] if t == 0 else ps[3 + t]
                for k in range(2):
                    mm = nc.tensor.transpose(bank[0:nt, k * P:(k + 1) * P], XB[:, 4 + k, t0:t0 + nt], ident)
                mm.then_inc(bt_mm, 1)
            pe.wait_ge(dx_ready, 3)
            pe.wait_ge(bt_kept, 1)
            for g in range(2):
                bank = ps[6 + g]
                for c in range(2):
                    nc.tensor.matmul(bank[:, c * P:(c + 1) * P], XB[:, 4 + g, c * P:(c + 1) * P],
                                     XB[:, 6 + g, c * P:(c + 1) * P], start=True, stop=True)
                nc.tensor.matmul(bank[0:32, SEQ:T], XB[:, 4 + g, SEQ:T], XB[:, 6 + g, SEQ:T],
                                 start=True, stop=True).then_inc(cb_mm, 1)
            pe.wait_ge(bt_kept, 3)
            pe.wait_ge(ld_h0, 16)
            for s in range(NB):
                j = s % 4
                for g in range(2):
                    mm = nc.tensor.matmul(ps[4 + s // 4][32 * j:32 * j + 32, g * 256:(g + 1) * 256],
                                          XB[:, 6 + g, SEQ:T], H0[:, s, g * 256:(g + 1) * 256], start=True, stop=True)
            mm.then_inc(bt_mm, 1)
            pe.wait_ge(m_ready, 2)
            pe.wait_ge(seg_ready, H)
            pe.wait_ge(e_ready, H)
            for c, (t0, nt) in enumerate(TILES):
                for h in range(H):
                    mm = nc.tensor.matmul(ps[c][64 * (h % 2):64 * (h % 2) + 64, (h // 2) * nt:(h // 2 + 1) * nt],
                                          DX[0:nt, c, h * 64:(h + 1) * 64], L[0:nt, h, t0:t0 + nt],
                                          start=True, stop=True)
                mm.then_inc(ydiag_mm, 1)
            pe.wait_ge(bt_kept, 5)
            own = cst("own_rows").rearrange("p (g t) -> p g t", g=2)
            for q in range(4):
                for g in range(2):
                    mm = nc.tensor.matmul(ps[6][:, q * 32:(q + 1) * 32], YO[:, g, q * P:(q + 1) * P], own[:, g, :],
                                          start=(g == 0), stop=(g == 1))
            mm.then_inc(yoff_mm, 1)
            pe.wait_ge(bt_kept, 3)
            for c in range(2):
                for g in range(2):
                    mm = nc.tensor.matmul(ps[4 + c][:, g * 256:(g + 1) * 256], BTOK[:, c, g * P:(g + 1) * P],
                                          DXE[:, c, g * 256:(g + 1) * 256], start=True, stop=True)
                mm.then_inc(state_mm, 1)
            pe.wait_ge(h1_ready, 1)
            for q in range(4):
                mm = nc.tensor.matmul(ps[3][:, q * P:(q + 1) * P], H1[:, q * P:(q + 1) * P],
                                      XB[:, 6 + q // 2, P:SEQ], start=True, stop=True)
            mm.then_inc(yoff_mm, 1)
            query_products(pe)
            pe.wait_ge(sq_ready, 7)
            for g in range(2):
                for k in range(2):
                    mm = nc.tensor.matmul(ps[g][:, 0:T], ones, SQ[:, 2 * g + k, :], start=(k == 0), stop=(k == 1))
            mm.then_inc(sum_mm, 1)
            pe.wait_ge(bm_ready, 1)
            pe.wait_ge(h2_ready, 1)
            pe.wait_ge(q_kept, 1)
            for s in range(NB):
                if s >= 3:
                    pe.wait_ge(sstate_kept, s - 2)
                for g in range(2):
                    mm = nc.tensor.matmul(ps[(7, 4, 5)[s % 3]][:, g * 256:(g + 1) * 256],
                                          BM[0:32, s, g * P:(g + 1) * P], DXE[0:32, 2, g * 256:(g + 1) * 256],
                                          start=True, stop=True)
                mm.then_inc(sstate_mm, 1)
            products_attention(pe)
            products_layer_out(pe, 0)
            products_conformer(pe)
            products_layer_out(pe, 1)

        @block.scalar
        def _(act):
            steps = Chain(act, act_step)
            act.wait_ge(ld_const, 32)
            act.wait_ge(zeroed, 1)
            for t, (t0, nt) in enumerate(TILES):
                act.wait_ge(tok_kept, 3)
                op = nc.scalar.activation(T1[0:nt, t, 0:R], TK[0:nt, t, 0:R], ACT.Square, accum_out=SS[0:nt, t:t + 1])
                op.then_inc(sq_ready, 1)
            for k in range(3):
                act.wait_ge(hq_kept, k + 1)
                nc.scalar.activation(SQ[:, k, :], HQ[:, k, :], ACT.Square).then_inc(sq_ready, 1)
            act.wait_ge(sq_ready, 3)
            nc.scalar.activation(RK, SS, ACT.Sqrt, bias=eps, scale=1.0 / R).then_inc(std_ready, 1)
            act.wait_ge(dt_z, 1)
            steps.step(nc.scalar.activation(T3, T3, ACT.Exp))
            nc.scalar.activation(NA, prm("a_log"), ACT.Exp)
            nc.scalar.activation(T3, T3, ACT.Ln, bias=1.0).then_inc(dt_ln, 1)
            for n in range(4):
                act.wait_ge(piece_mm, 4 + n)
                nc.scalar.activation(ZT[:, n, :], ps[(3 + n) % 4][:, 0:T], ACT.Silu).then_inc(ch_kept, 1)
            for n in range(8):
                act.wait_ge(piece_mm, 8 + n)
                bank = ps[(7 + n) % 4]
                if n == 1:
                    act.wait_ge(sum_mm, 1)
                    nc.scalar.activation(T1[:, 3, :], ps[7][:, 0:T], ACT.Sqrt, bias=eps, scale=1.0 / QL).then_inc(std_ready, 1)
                nc.scalar.copy(XP[:, n, 3:3 + SEQ], bank[:, 0:SEQ])
                nc.scalar.copy(XS[:, n, :, 3:7], bank[:, SEQ:T].rearrange("p (b s) -> p b s", s=NS)).then_inc(ch_kept, 1)
            for n in range(8):
                act.wait_ge(conv_ready, n + 1)
                op = nc.scalar.activation(XB[:, n, :], XB[:, n, :], ACT.Silu)
            op.then_inc(xb_ready, 1)
            act.wait_ge(acs_kept, 1)
            nc.scalar.activation(TOE[:, 0:16], TOE[:, 0:16], ACT.Exp)
            nc.scalar.activation(TOE[0:32, 16:24], TOE[0:32, 16:24], ACT.Exp)
            nc.scalar.activation(DEC, ACS[:, 16:96], ACT.Exp).then_inc(decay_ready, 1)
            for h in range(H):
                act.wait_ge(seg_ready, h + 1)
                lo = 64 * (h % 2)
                nc.scalar.activation(E[lo:lo + 64, h // 2, :], ps[h % 4][lo:lo + 64, 0:T], ACT.Exp).then_inc(e_ready, 1)
                nc.scalar.activation(L[:, h, 0:SEQ], L[:, h, 0:SEQ], ACT.Exp)
                nc.scalar.activation(L[0:32, h, SEQ:T], L[0:32, h, SEQ:T], ACT.Exp).then_inc(decay_ready, 1)
            for t, (t0, nt) in enumerate(TILES):
                act.wait_ge(bt_mm, t + 1)
                bank = ps[7] if t == 0 else ps[3 + t]
                nc.scalar.copy(BTOK[0:nt, t, :], bank[0:nt, 0:256]).then_inc(bt_kept, 1)
            act.wait_ge(bt_mm, 4)
            for g in range(2):
                nc.scalar.copy(YO[:, g, :], ps[4 + g][:, :]).then_inc(bt_kept, 1)
            act.wait_ge(state_mm, 1)
            nc.scalar.copy(H1, ps[4][:, :]).then_inc(h1_ready, 1)
            act.wait_ge(y_gated, 1)
            nc.scalar.activation(SQ, Y, ACT.Square).then_inc(sq_ready, 1)
            act.wait_ge(sum_mm, 2)
            for g in range(2):
                op = nc.scalar.activation(RG[:, g, :], ps[g][:, 0:T], ACT.Sqrt, bias=eps, scale=1.0 / 256)
            op.then_inc(std_ready, 1)
            act_attention(act)
            act_layer_out(act, 0)
            act_conformer(act)
            act_layer_out(act, 1)

        @block.vector
        def _(dve):
            steps = Chain(dve, dve_step)
            V = nc.vector
            dve.wait_ge(zeroed, 1)
            for t, (t0, nt) in enumerate(TILES):
                dve.wait_ge(tok_mm, t + 1)
                V.tensor_copy(TK[0:nt, t, :], ps[4 + t][0:nt, 0:296]).then_inc(tok_kept, 1)
            for k in range(3):
                dve.wait_ge(piece_mm, k + 1)
                V.tensor_copy(HQ[:, k, :], ps[k][:, 0:T]).then_inc(hq_kept, 1)
            dve.wait_ge(ld_const, 32)
            dve.wait_ge(tok_kept, 3)
            co = cst("cos").rearrange("p (t f) -> p t f", t=3)
            si = cst("sin").rearrange("p (t f) -> p t f", t=3)
            ka, kb = TK[:, :, 256:272], TK[:, :, 272:288]
            V.tensor_tensor(KPE[:, :, 0:16], ka, co, ALU.mult)
            V.tensor_tensor(KPE[:, :, 16:32], kb, co, ALU.mult)
            V.tensor_tensor(KT[:, :, 0:16], kb, si, ALU.mult)
            steps.step(V.tensor_tensor(KT[:, :, 16:32], ka, si, ALU.mult))
            V.tensor_tensor(KPE[:, :, 0:16], KPE[:, :, 0:16], KT[:, :, 0:16], ALU.subtract)
            steps.step(V.tensor_tensor(KPE[:, :, 16:32], KPE[:, :, 16:32], KT[:, :, 16:32], ALU.add))
            steps.step(V.tensor_tensor(TDT, TK[:, :, 288:296], prm("dt_bias").unsqueeze(1).to_broadcast([P, 3, 8]),
                                       ALU.add))
            V.scalar_tensor_tensor(T3, TDT, -1.0, TDT, ALU.mult, ALU.min).then_inc(dt_z, 1)
            dve.wait_ge(std_ready, 1)
            steps.step(V.reciprocal(RK, RK))
            for t, (t0, nt) in enumerate(TILES):
                op = V.scalar_tensor_tensor(CK[0:nt, t, :], TK[0:nt, t, 0:R], RK[0:nt, t:t + 1], prm("g_kv")[0:nt],
                                            ALU.mult, ALU.mult)
            op.then_inc(kv_ready, 1)
            dve.wait_ge(dt_ln, 1)
            steps.step(V.scalar_tensor_tensor(DT, TDT, 0.0, T3, ALU.max, ALU.add))
            steps.step(V.tensor_tensor(DTA, DT, NA.unsqueeze(1).to_broadcast([P, 3, 8]), ALU.mult))
            steps.step(V.tensor_scalar(DTA, DTA, -1.0, None, ALU.mult))
            V.tensor_tensor(DTAM[0:32], DTA[0:32, 2, :].unsqueeze(1).to_broadcast([32, NB, 8]),
                            cst("bmask", 32).unsqueeze(2).to_broadcast([32, NB, 8]), ALU.mult).then_inc(dtA_ready, 1)
            dve.wait_ge(ld_hist, 16)
            cw = prm("conv_w").rearrange("p (c k) -> p c k", k=4)
            cb = prm("conv_b")
            for n in range(8):
                dve.wait_ge(ch_kept, 5 + n)
                xsv = CS[:, n, :].rearrange("p (b s) -> p b s", s=NS)
                V.tensor_scalar(XB[:, n, 0:SEQ], XP[:, n, 0:SEQ], cw[:, n, 0:1], cb[:, n:n + 1], ALU.mult, ALU.add)
                steps.step(V.tensor_scalar(xsv, XS[:, n, :, 0:4], cw[:, n, 0:1], cb[:, n:n + 1], ALU.mult, ALU.add))
                for k in range(1, 4):
                    V.scalar_tensor_tensor(XB[:, n, 0:SEQ], XP[:, n, k:k + SEQ], cw[:, n, k:k + 1], XB[:, n, 0:SEQ],
                                           ALU.mult, ALU.add)
                    dst = xsv if k < 3 else XB[:, n, SEQ:T].rearrange("p (b s) -> p b s", s=NS)
                    op = V.scalar_tensor_tensor(dst, XS[:, n, :, k:k + 4], cw[:, n, k:k + 1], xsv, ALU.mult, ALU.add)
                    steps.step(op) if k < 3 else op.then_inc(conv_ready, 1)
                if n == 3:
                    dve.wait_ge(std_ready, 2)
                    steps.step(V.reciprocal(T1[:, 3, :], T1[:, 3, :]))
                    for k in range(3):
                        op = V.scalar_tensor_tensor(HQ[:, k, :], HQ[:, k, :], prm("g_q")[:, k:k + 1], T1[:, 3, :],
                                                    ALU.mult, ALU.mult)
                    op.then_inc(hq_ready, 1)
                if n == 5:
                    dve.wait_ge(kvT_mm, 1)
                    for r in range(2):
                        V.tensor_copy(CKT[:, r, :], ps[4 + r][:, 0:T])
                    V.tensor_copy(KPT[0:32], ps[6][0:32, 0:T]).then_inc(kvT_kept, 1)
            dve.wait_ge(kvT_mm, 2)
            V.tensor_copy(ACS[:, 0:96], ps[7][:, 0:96])
            steps.step(V.tensor_copy(ACS[0:32, 96:112], ps[7][0:32, 96:112]))
            V.tensor_tensor(TOE[:, 0:16], ACS[:, 16:32], ACS[:, 0:16], ALU.subtract)
            V.tensor_tensor(TOE[0:32, 16:24], ACS[0:32, 104:112], ACS[0:32, 96:104], ALU.subtract).then_inc(acs_kept, 1)
            for h in range(H):
                dve.wait_ge(row_mm, h + 1)
                for c in range(2):
                    V.scalar_tensor_tensor(L[:, h, c * P:(c + 1) * P], ps[h % 4][:, c * P:(c + 1) * P],
                                           ACS[:, 8 * c + h:8 * c + h + 1], cst("mask_ssd"), ALU.subtract, ALU.add)
                V.scalar_tensor_tensor(L[0:32, h, SEQ:T], ps[h % 4][0:32, SEQ:T], ACS[0:32, 96 + h:97 + h],
                                       cst("mask_ssd_s", 32), ALU.subtract, ALU.add).then_inc(seg_ready, 1)
            dve.wait_ge(decay_ready, 1)
            for t, (t0, nt) in enumerate(TILES):
                dve.wait_ge(xs_mm, t + 1)
                dxv = DX[0:nt, t, :].rearrange("p (h d) -> p h d", h=H)
                steps.step(V.tensor_tensor(dxv, ps[4 + t][0:nt, :].rearrange("p (h d) -> p h d", h=H),
                                           DT[0:nt, t, :].unsqueeze(2).to_broadcast([nt, H, 64]), ALU.mult))
                V.tensor_tensor(DXE[0:nt, t, :].rearrange("p (h d) -> p h d", h=H), dxv,
                                TOE[0:nt, 8 * t:8 * t + 8].unsqueeze(2).to_broadcast([nt, H, 64]),
                                ALU.mult).then_inc(dx_ready, 1)
            dve.wait_ge(decay_ready, H + 1)
            for g in range(2):
                dve.wait_ge(cb_mm, g + 1)
                for c, (t0, nt) in enumerate(TILES):
                    lv = L[0:nt, 4 * g:4 * g + 4, t0:t0 + nt]
                    op = V.tensor_tensor(lv, lv, ps[6 + g][0:nt, t0:t0 + nt].unsqueeze(1).to_broadcast([nt, 4, nt]), ALU.mult)
                op.then_inc(m_ready, 1)
            for q in range(4):
                op = V.tensor_scalar(Y[:, q, :], XB[:, q, :], prm("d_skip")[:, q:q + 1], None, ALU.mult)
            steps.step(op)
            for c, (t0, nt) in enumerate(TILES):
                dve.wait_ge(ydiag_mm, c + 1)
                yv = Y[:, :, t0:t0 + nt]
                op = V.tensor_tensor(yv, yv, ps[c][:, 0:4 * nt].rearrange("p (q t) -> p q t", q=4), ALU.add)
            steps.step(op)
            for c, off in ((2, ps[6][:, 0:P]), (1, ps[3][:, :])):
                t0, nt = TILES[c]
                dve.wait_ge(yoff_mm, 3 - c)
                dve.wait_ge(e_ready, H)
                steps.step(V.tensor_tensor(T1[:, :, t0:t0 + nt], E[:, :, t0:t0 + nt],
                                           off.rearrange("p (q t) -> p q t", q=4), ALU.mult))
                steps.step(V.tensor_tensor(Y[:, :, t0:t0 + nt], Y[:, :, t0:t0 + nt], T1[:, :, t0:t0 + nt], ALU.add))
            V.tensor_tensor(Y, Y, ZT, ALU.mult).then_inc(y_gated, 1)
            for n in range(4):
                dve.wait_ge(qn_mm, n + 1)
                V.tensor_copy(QN[:, n, :], ps[QN_BANKS[n]][:, 0:T]).then_inc(q_kept, 1)
            dve.wait_ge(h1_ready, 1)
            dve.wait_ge(state_mm, 2)
            h2v = H2.rearrange("p (h d) -> p h d", h=H)
            steps.step(V.tensor_tensor(h2v, H1.rearrange("p (h d) -> p h d", h=H),
                                       DEC[:, 8:16].unsqueeze(2).to_broadcast([P, H, 64]), ALU.mult))
            V.tensor_tensor(H2, H2, ps[5][:, :], ALU.add).then_inc(h2_ready, 1)
            dve.wait_ge(bm_ready, 2)
            for s in range(NB):
                dve.wait_ge(sstate_mm, s + 1)
                V.tensor_tensor(H0[:, s, :], H0[:, s, :], ps[(7, 4, 5)[s % 3]][:, :], ALU.add).then_inc(sstate_kept, 1)
            dve.wait_ge(std_ready, 3)
            steps.step(V.reciprocal(RG, RG))
            for q in range(4):
                op = V.scalar_tensor_tensor(CAT[:, 4 + q, :], Y[:, q, :], prm("g_y")[:, q:q + 1], RG[:, q // 2, :],
                                            ALU.mult, ALU.mult)
            op.then_inc(y_ready, 1)
            dve_attention(dve, steps)
            dve_layer_out(dve, steps, 0)
            dve_conformer(dve, steps)
            dve_layer_out(dve, steps, 1)

        @block.gpsimd
        def _(pool):
            G = nc.gpsimd
            G.memset(XS[:], 0.0)
            G.memset(XP[:, :, 0:3], 0.0)
            G.memset(SS, 1.0)
            G.memset(X[:, 2, :], 0.0)
            G.memset(TK[:, 2, :], 0.0).then_inc(zeroed, 1)

            pool.dma_start(pages[0:1, :], a["pages"]).then_inc(ld_pages, 16)

            def store(dst, src, done=None):
                if done is None:
                    n_stored[0] += 1
                pool.dma_start(dst, src).then_inc(stored if done is None else done, 16)

            pool.wait_ge(kv_ready, 1)
            for t in range(2):
                store(o["ckv_p"][t * P:(t + 1) * P], CK[:, t, :], ckv_stored)
                store(o["kpe_p"][t * P:(t + 1) * P], KPE[:, t, :])
            store(o["ckv_s"], CK[0:32, 2, :], ckv_stored)
            store(o["kpe_s"], KPE[0:32, 2, :])
            pool.wait_ge(ch_kept, 12)
            pool.wait_ge(ld_hist, 16)
            store(o["sconv_p"], XP[:, :, SEQ:SEQ + 3], conv_stored)
            store(o["sconv_s"], XS[:, :, :, 4:7], conv_stored)
            fill_tables(pool)
            pool.wait_ge(bt_kept, 3)
            G.tensor_tensor(BM[0:32], BTOK[0:32, 2, :].unsqueeze(1).to_broadcast([32, NB, 256]),
                            cst("bmask", 32).unsqueeze(2).to_broadcast([32, NB, 256]), ALU.mult).then_inc(bm_ready, 1)
            pool.wait_ge(bt_mm, 4)
            pool.wait_ge(decay_ready, 1)
            h0v = H0.rearrange("p b (h d) -> p (b h) d", d=64)
            G.tensor_tensor(h0v, h0v, DEC[:, 16:80].unsqueeze(2).to_broadcast([P, 64, 64]), ALU.mult).then_inc(bm_ready, 1)
            pool.wait_ge(h2_ready, 1)
            store(o["ssm_p"], H2, h2_stored)
            pool.wait_ge(sstate_kept, NB)
            store(o["ssm_s"], H0, h0_stored)
            pool_layer_out(pool, store, 0)
            pool_conformer(pool, store)
            pool_layer_out(pool, store, 1)
            pool.wait_ge(stored, 16 * n_stored[0])
            pool.wait_ge(ckv_stored, 48)
            pool.wait_ge(h2_stored, 16)
            pool.wait_ge(h0_stored, 16)
            pool.wait_ge(conv_stored, 64)


INPUTS = [("x", (T, D)), ("xT", (P, KC, T)), ("w_tok", (P, KC, 296)), ("w_ch", (15, P, KC, P)), ("consts", (P, NCONST)),
          ("params", (P, NPARAM)), ("conv_hist", (P, KC, NB, 3)), ("w_q", (P, 4352)), ("state", (P, NB, 512)),
          ("cache", (160, P, R + E_PE)), ("pages", (1, NB * NP)),
          ("w_out", (P, KC, D)), ("rows", (5, P, D)), ("rows_b", (4, P, D)), ("w_moe", (2, NE, P, 6144)),
          ("w_conf", (16, P, KC, P)), ("conf_hist", (P, KC, HIST, NB)), ("w_conf_out", (P, KC, D)),
          ("nobody", (SLOT_ROWS, 1)), ("token_ids", (P, 3))]
OUTPUTS = [("y", (T, D)), ("ckv_p", (SEQ, R)), ("kpe_p", (SEQ, E_PE)), ("ssm_p", (P, 512)), ("sconv_p", (P, KC, 3)),
           ("cconv_p", (P, KC, HIST)), ("ckv_s", (32, R)), ("kpe_s", (32, E_PE)), ("ssm_s", (P, NB, 512)),
           ("sconv_s", (P, KC, NB, 3)), ("cconv_s", (P, KC, HIST, NB))]
INT_INPUTS = ("pages", "nobody", "token_ids")


def lay_out(v):
    f = np.ascontiguousarray
    chunks = lambda w: f(w.reshape(-1, P, w.shape[-1]).transpose(1, 0, 2))
    cols = lambda x: f(x.reshape(-1, P).T)
    bcast = lambda x: np.broadcast_to(x, (P,) + x.shape)
    w = v["w_in_ab"][0]
    x = np.concatenate([v["x_prompt"][0], v["x_sample"].reshape(32, D)])
    d = {"x": x, "xT": chunks(f(x.T)), "consts": constants()}
    d["w_tok"] = chunks(np.concatenate([w[:, 384:672], w[:, 2208:2216]], axis=1))
    w_ch = np.concatenate([w[:, 0:384], w[:, 672:2208]], axis=1)
    pieces = lambda m: f(m.reshape(KC, P, -1, P).transpose(2, 1, 0, 3))
    d["w_ch"] = pieces(w_ch)
    uq = v["w_uq"][0]
    uqn = chunks(f(uq[:, :, :64].reshape(QL, 512))).reshape(P, -1)
    uqp = chunks(f(uq[:, :, 64:].reshape(QL, 256))).reshape(P, -1)
    uk = f(v["w_uk"][0].transpose(1, 2, 0).reshape(4, P, R).transpose(1, 0, 2)).reshape(P, -1)
    uv = chunks(v["w_uv"][0].reshape(R, 512)).reshape(P, -1)
    d["w_q"] = np.concatenate([uqn, uqp, uk, uv], axis=1)
    d["conv_hist"] = f(v["state_ssm_conv"][0].reshape(NB, 3, KC, P).transpose(3, 2, 0, 1))
    d["state"] = f(v["state_ssm"][0].transpose(3, 0, 1, 2).reshape(P, NB, 512))
    d["cache"] = np.concatenate([v["cache_ckv"][0], v["cache_kpe"][0]], axis=2)
    d["pages"] = f(v["page_table"].reshape(2, 4, NP // 2, 2).transpose(0, 2, 1, 3))
    d["w_out"] = chunks(v["w_out_ab"][0])
    d["rows"] = np.stack([bcast(r) for r in (v["ln_mix_g"][0], v["ln_ffn_g"][0], v["ln_mix_g"][1], v["ln_ffn_g"][1],
                                             v["conf_b_out"][0])])
    d["rows_b"] = np.stack([bcast(r) for r in (v["ln_mix_b"][0], v["ln_ffn_b"][0], v["ln_mix_b"][1], v["ln_ffn_b"][1])])
    halves = lambda m: m.reshape(2, NE, KC, P, 2, 1, P)
    gu = np.concatenate([halves(v["moe_w_gate"]), halves(v["moe_w_up"])], axis=5)
    gu = gu.transpose(0, 1, 3, 2, 4, 5, 6).reshape(2, NE, P, 4096)
    down = v["moe_w_down"].reshape(2, NE, 2, P, D).transpose(0, 1, 3, 2, 4).reshape(2, NE, P, 2048)
    d["w_moe"] = np.concatenate([gu, down], axis=3)
    d["w_conf"] = pieces(v["conf_w_in"][0])
    d["conf_hist"] = f(v["state_conf_conv"][0].reshape(NB, HIST, KC, P).transpose(3, 2, 1, 0))
    d["w_conf_out"] = chunks(v["conf_w_out"][0])
    d["nobody"] = np.full((SLOT_ROWS, 1), NOBODY, np.int32)
    ids = np.arange(3 * P, dtype=np.int32).reshape(3, P).T
    d["token_ids"] = f(ids)
    taps = lambda x: f(x.T.reshape(KC, P, -1).transpose(1, 0, 2)).reshape(P, -1)
    parts = {"g_q": cols(v["g_q_norm"][0]), "conv_w": taps(v["ssm_conv_w"][0]), "conv_b": cols(v["ssm_conv_b"][0]),
             "g_y": cols(v["ssm_norm_g"][0]), "d_skip": cols(np.repeat(v["ssm_d"][0], 64)),
             "dt_bias": bcast(v["ssm_dt_bias"][0]), "a_log": bcast(v["ssm_a_log"][0]), "b_in": cols(v["conf_b_in"][0]),
             "dw_w": taps(v["conf_dw_w"][0]), "dw_b": cols(v["conf_dw_b"][0]), "gn": cols(v["conf_norm_g"][0]),
             "bn": cols(v["conf_norm_b"][0]), "r_bias": bcast(v["router_bias"]),
             "w_router": chunks(v["w_router"]).reshape(P, -1), "g_kv": bcast(v["g_kv_norm"][0])}
    d["params"] = np.concatenate([parts[name] for name in PARAM], axis=1)
    return d


def kernel(**inputs):
    from concourse import bacc
    from concourse.bass_utils import run_bass_kernel_spmd

    nc = bacc.Bacc("TRN2", target_bir_lowering=False, num_devices=1)
    laid = lay_out({k: np.asarray(x) for k, x in inputs.items()})
    arrays, a, o = {}, {}, {}
    for name, shape in INPUTS:
        arrays[f"in_{name}"] = np.ascontiguousarray(laid[name].reshape(shape))
        dt = I32 if name in INT_INPUTS else F32
        a[name] = nc.dram_tensor(f"in_{name}", shape, dt, kind="ExternalInput").ap()
    for name, shape in OUTPUTS:
        o[name] = nc.dram_tensor(f"out_{name}", shape, F32, kind="ExternalOutput").ap()
    hybrid_trunk(nc, a, o)
    res = run_bass_kernel_spmd(nc, [arrays], core_ids=[0]).results[0]
    r = {name: np.asarray(res[f"out_{name}"]) for name, _ in OUTPUTS}
    rows = lambda x: x.transpose(2, 1, 0).reshape(1, 1, x.shape[2], -1)
    srows = lambda x: x.transpose(2, 3, 1, 0).reshape(1, NB, x.shape[3], -1)
    return (r["y"][:SEQ].reshape(1, SEQ, D), r["y"][SEQ:].reshape(NB, NS, D),
            r["ckv_p"].reshape(1, 1, SEQ, R), r["kpe_p"].reshape(1, 1, SEQ, E_PE),
            r["ssm_p"].reshape(P, 8, 64).transpose(1, 2, 0).reshape(1, 1, 8, 64, P), rows(r["sconv_p"]),
            rows(r["cconv_p"]), r["ckv_s"].reshape(1, NB, NS, R), r["kpe_s"].reshape(1, NB, NS, E_PE),
            r["ssm_s"].reshape(P, NB, 8, 64).transpose(1, 2, 3, 0).reshape(1, NB, 8, 64, P),
            srows(r["sconv_s"]), srows(r["cconv_s"].transpose(0, 1, 3, 2)))
```
